# Optimizing a Trainium2 kernel written in Bass

```python
import jax
import jax.numpy as jnp
from jax import lax
import numpy as np
import math
import jax, jax.numpy as jnp

D_MODEL = 1024
BATCH = 1
SEQ = 512
DEPTH = 1

GRID_W = 64
CTX_LEN = 256

NA_HEADS = 8
NA_HEAD_DIM = 64
NA_WIDTH = NA_HEADS * NA_HEAD_DIM
NA_KH = 8
NA_KW = 16
NA_QB_W = 16
NA_KB_W = NA_QB_W + NA_KW
NA_NCB = GRID_W // NA_QB_W

HG_HEADS = 4
HG_DK = 128
HG_WIDTH = HG_HEADS * HG_DK
HG_CHUNK = 64

MIX_WIDTH = NA_WIDTH + HG_WIDTH
IN_COLS = 3 * NA_WIDTH + 5 * HG_WIDTH

PEER_HEADS = 8
PEER_NKEYS = 128
PEER_EXPERTS = PEER_NKEYS * PEER_NKEYS
PEER_TOPK = 16
PEER_DQ = 256
PEER_BLOCK = 128

N_MOD = 6
EPS = 1e-6


def rms_norm(x, g):
    xf = x.astype(jnp.float32)
    y = xf * lax.rsqrt(jnp.mean(xf * xf, axis=-1, keepdims=True) + EPS)
    return (y * g.astype(jnp.float32)).astype(x.dtype)

def modulate(h, shift, scale):
    return h * (1 + scale) + shift

def neighbourhood_attention(q, k, v, k_ctx, v_ctx, rpb):
    B, S, H, Dh = q.shape
    rows = S // GRID_W
    kh = min(NA_KH, rows)
    scale = Dh ** -0.5
    qg = q.reshape(B, rows, GRID_W, H, Dh)
    kg = k.reshape(B, rows, GRID_W, H, Dh)
    vg = v.reshape(B, rows, GRID_W, H, Dh)
    qcol = np.arange(GRID_W).reshape(NA_NCB, NA_QB_W)
    kc0 = np.clip(qcol[:, 0] - NA_KW // 2, 0, GRID_W - NA_KB_W)
    kcol = kc0[:, None] + np.arange(NA_KB_W)[None, :]
    cstart = np.clip(qcol - NA_KW // 2, 0, GRID_W - NA_KW)
    col_ok = (kcol[:, None, :] >= cstart[..., None]) & (kcol[:, None, :] < cstart[..., None] + NA_KW)
    dc_idx = np.clip(kcol[:, None, :] - qcol[..., None] + NA_KW - 1, 0, 2 * NA_KW - 2)
    n_win = kh * NA_KB_W

    def row_block(r):
        rs = jnp.clip(r - kh // 2, 0, rows - kh)
        q_r = lax.dynamic_index_in_dim(qg, r, axis=1, keepdims=False).reshape(B, NA_NCB, NA_QB_W, H, Dh)
        k_rows = lax.dynamic_slice_in_dim(kg, rs, kh, axis=1)
        v_rows = lax.dynamic_slice_in_dim(vg, rs, kh, axis=1)
        kb = k_rows[:, :, kcol]
        vb = v_rows[:, :, kcol]
        dr_idx = rs + jnp.arange(kh) - r + NA_KH - 1
        bias = rpb[:, dr_idx[None, None, :, None], dc_idx[:, :, None, :]]
        s_win = jnp.einsum('bcqhd,bkcjhd->bhcqkj', q_r, kb).astype(jnp.float32) * scale
        s_win = jnp.where(col_ok[None, None, :, :, None, :], s_win + bias.astype(jnp.float32)[None], -jnp.inf)
        s_ctx = jnp.einsum('bcqhd,blhd->bhcql', q_r, k_ctx).astype(jnp.float32) * scale
        p = jax.nn.softmax(jnp.concatenate([s_win.reshape(B, H, NA_NCB, NA_QB_W, n_win), s_ctx], axis=-1), axis=-1)
        p = p.astype(v.dtype)
        p_win = p[..., :n_win].reshape(B, H, NA_NCB, NA_QB_W, kh, NA_KB_W)
        o = (jnp.einsum('bhcqkj,bkcjhd->bcqhd', p_win, vb)
             + jnp.einsum('bhcql,blhd->bcqhd', p[..., n_win:], v_ctx))
        return o.reshape(B, GRID_W, H, Dh)

    out = lax.map(row_block, jnp.arange(rows))
    return jnp.moveaxis(out, 0, 1).reshape(B, S, H * Dh)

def context_attention(q, k, v):
    B, L, H, Dh = q.shape
    s = jnp.einsum('blhd,bmhd->bhlm', q, k).astype(jnp.float32) * Dh ** -0.5
    p = jax.nn.softmax(s, axis=-1).astype(v.dtype)
    return jnp.einsum('bhlm,bmhd->blhd', p, v).reshape(B, L, H * Dh)

def _na_heads(t):
    B, T, _ = t.shape
    return t.reshape(B, T, NA_HEADS, NA_HEAD_DIM)

def _hg_heads(t):
    B, T, _ = t.shape
    return t.reshape(B, T, HG_HEADS, HG_DK).transpose(0, 2, 1, 3)

def _forget(z, lb):
    lb = lb.reshape(HG_HEADS, 1, HG_DK)
    f = lb + (1 - lb) * jax.nn.sigmoid(z.astype(jnp.float32))
    return jnp.log(f), 1 - f

def _time_flip(t, rev):
    return jnp.flip(t, axis=2) if rev else t

def gla_chunked(q, k, v, log_f, s0, with_output):
    B, H, T, _ = q.shape
    n_chunks = T // HG_CHUNK

    def chunks(t):
        return t.astype(jnp.float32).reshape(B, H, n_chunks, HG_CHUNK, t.shape[-1]).transpose(2, 0, 1, 3, 4)

    kc, vc, lfc = chunks(k), chunks(v), chunks(log_f)

    def update(S, k_n, v_n, b):
        b_last = b[:, :, -1:, :]
        k_dec = k_n * jnp.exp(b_last - b)
        return jnp.exp(b_last[:, :, 0, :])[..., None] * S + jnp.einsum('bhsd,bhsv->bhdv', k_dec, v_n)

    if not with_output:
        def state_step(S, xs):
            k_n, v_n, lf_n = xs
            return update(S, k_n, v_n, jnp.cumsum(lf_n, axis=2)), None
        s_fin, _ = lax.scan(state_step, s0, (kc, vc, lfc))
        return None, s_fin

    qc = chunks(q)
    causal = jnp.tril(jnp.ones((HG_CHUNK, HG_CHUNK), dtype=bool))

    def step(S, xs):
        q_n, k_n, v_n, lf_n = xs
        b = jnp.cumsum(lf_n, axis=2)
        pair = b[:, :, :, None, :] - b[:, :, None, :, :]
        decay = jnp.exp(jnp.where(causal[:, :, None], pair, -jnp.inf))
        A = jnp.einsum('bhtd,bhsd,bhtsd->bhts', q_n, k_n, decay)
        o = jnp.einsum('bhts,bhsv->bhtv', A, v_n) + jnp.einsum('bhtd,bhdv->bhtv', q_n * jnp.exp(b), S)
        return update(S, k_n, v_n, b), o

    s_fin, o = lax.scan(step, s0, (qc, kc, vc, lfc))
    o = o.transpose(1, 2, 0, 3, 4).reshape(B, H, T, -1)
    return o, s_fin

def _gated_out(o, g, norm_g):
    B, H, T, Dv = o.shape
    o = o * lax.rsqrt(jnp.mean(o * o, axis=-1, keepdims=True) + EPS) * norm_g.astype(jnp.float32).reshape(H, 1, Dv)
    o = o * jax.nn.silu(_hg_heads(g).astype(jnp.float32))
    return o.transpose(0, 2, 1, 3).reshape(B, T, H * Dv).astype(g.dtype)

def hgrn2_mixer(px, pc, lb, norm_g, need_ctx):
    qx, vx = jax.nn.silu(_hg_heads(px[0])), _hg_heads(px[3])
    qc, vc = jax.nn.silu(_hg_heads(pc[0])), _hg_heads(pc[3])
    s0 = jnp.zeros((qx.shape[0], HG_HEADS, HG_DK, HG_DK), jnp.float32)
    outs_x, outs_c = [], []
    for d in range(2):
        rev = d == 1
        lf_c, k_c = _forget(_hg_heads(pc[1 + d]), lb[d])
        lf_x, k_x = _forget(_hg_heads(px[1 + d]), lb[d])
        o_c, s_c = gla_chunked(_time_flip(qc, rev), _time_flip(k_c, rev), _time_flip(vc, rev),
                               _time_flip(lf_c, rev), s0, need_ctx)
        o_x, _ = gla_chunked(_time_flip(qx, rev), _time_flip(k_x, rev), _time_flip(vx, rev),
                             _time_flip(lf_x, rev), s_c, True)
        outs_x.append(_time_flip(o_x, rev))
        if need_ctx:
            outs_c.append(_time_flip(o_c, rev))
    y_x = _gated_out(outs_x[0] + outs_x[1], px[4], norm_g)
    y_c = _gated_out(outs_c[0] + outs_c[1], pc[4], norm_g) if need_ctx else None
    return y_x, y_c

def peer_ffn(h, wq, sub_keys, u, v):
    B, T, D = h.shape
    tok = h.reshape(-1, PEER_BLOCK, D)

    def block(t):
        q = (t @ wq).reshape(PEER_BLOCK, PEER_HEADS, 2, PEER_DQ // 2)
        s = jnp.einsum('tpcd,pckd->tpck', q, sub_keys).astype(jnp.float32)
        s1, i1 = lax.top_k(s[:, :, 0], PEER_TOPK)
        s2, i2 = lax.top_k(s[:, :, 1], PEER_TOPK)
        cand = (s1[..., :, None] + s2[..., None, :]).reshape(PEER_BLOCK, PEER_HEADS, PEER_TOPK * PEER_TOPK)
        cidx = (i1[..., :, None] * PEER_NKEYS + i2[..., None, :]).reshape(PEER_BLOCK, PEER_HEADS, PEER_TOPK * PEER_TOPK)
        top, pos = lax.top_k(cand, PEER_TOPK)
        idx = jnp.take_along_axis(cidx, pos, axis=-1)
        g = jax.nn.softmax(top, axis=-1)
        a = jax.nn.gelu(jnp.einsum('tpkd,td->tpk', u[idx], t).astype(jnp.float32), approximate=False)
        return jnp.einsum('tpk,tpkd->td', (g * a).astype(t.dtype), v[idx])

    return lax.map(block, tok).reshape(B, T, D)

def first_inputs(seed: int = 0) -> dict:
    key = jax.random.key(seed)
    ks = jax.random.split(key, 18)

    def nrm(k, shape, scale):
        return jax.random.normal(k, shape, jnp.float32) * scale

    return {
        'x': nrm(ks[0], (BATCH, SEQ, D_MODEL), 1.0),
        'c': nrm(ks[1], (BATCH, D_MODEL), 1.0),
        'ctx': nrm(ks[2], (BATCH, CTX_LEN, D_MODEL), 1.0),
        'c_ctx': nrm(ks[3], (D_MODEL,), 1.0),
        'w_mod': nrm(ks[4], (DEPTH, D_MODEL, N_MOD * D_MODEL), 0.5 * D_MODEL ** -0.5),
        'b_mod': nrm(ks[5], (DEPTH, N_MOD * D_MODEL), 0.01),
        'norm1': 1.0 + nrm(ks[6], (DEPTH, D_MODEL), 0.05),
        'norm2': 1.0 + nrm(ks[7], (DEPTH, D_MODEL), 0.05),
        'w_in': nrm(ks[8], (DEPTH, D_MODEL, IN_COLS), D_MODEL ** -0.5),
        'w_out': nrm(ks[9], (DEPTH, MIX_WIDTH, D_MODEL), MIX_WIDTH ** -0.5),
        'na_rpb': nrm(ks[10], (DEPTH, NA_HEADS, 2 * NA_KH - 1, 2 * NA_KW - 1), 0.2),
        'hg_lb': nrm(ks[11], (DEPTH + 1, 2, HG_WIDTH), 1.0),
        'hg_norm': 1.0 + nrm(ks[12], (DEPTH, HG_WIDTH), 0.05),
        'peer_wq': nrm(ks[13], (DEPTH, D_MODEL, PEER_HEADS * PEER_DQ), D_MODEL ** -0.5),
        'peer_keys': nrm(ks[14], (DEPTH, PEER_HEADS, 2, PEER_NKEYS, PEER_DQ // 2), (PEER_DQ // 2) ** -0.5),
        'peer_u': nrm(ks[15], (DEPTH, PEER_EXPERTS, D_MODEL), D_MODEL ** -0.5),
        'peer_v': nrm(ks[16], (DEPTH, PEER_EXPERTS, D_MODEL), PEER_HEADS ** -0.5),
        'norm_f': 1.0 + nrm(ks[17], (D_MODEL,), 0.05),
    }

def first_block(x, c, ctx, c_ctx, w_mod, b_mod, norm1, norm2, w_in, w_out, na_rpb, hg_lb, hg_norm,
              peer_wq, peer_keys, peer_u, peer_v, norm_f):
    lb_all = jnp.cumsum(jax.nn.softmax(hg_lb.astype(jnp.float32), axis=0), axis=0)
    splits = [NA_WIDTH, 2 * NA_WIDTH, 3 * NA_WIDTH] + [3 * NA_WIDTH + j * HG_WIDTH for j in range(1, 5)]
    for l in range(DEPTH):
        need_ctx = l < DEPTH - 1
        mod_x = (jax.nn.silu(c) @ w_mod[l] + b_mod[l])[:, None, :]
        mod_c = jax.nn.silu(c_ctx) @ w_mod[l] + b_mod[l]
        sh1, sc1, gt1, sh2, sc2, gt2 = jnp.split(mod_x, N_MOD, axis=-1)
        csh1, csc1, cgt1, csh2, csc2, cgt2 = jnp.split(mod_c, N_MOD, axis=-1)

        px = jnp.split(modulate(rms_norm(x, norm1[l]), sh1, sc1) @ w_in[l], splits, axis=-1)
        pc = jnp.split(modulate(rms_norm(ctx, norm1[l]), csh1, csc1) @ w_in[l], splits, axis=-1)
        k_ctx, v_ctx = _na_heads(pc[1]), _na_heads(pc[2])
        na_x = neighbourhood_attention(_na_heads(px[0]), _na_heads(px[1]), _na_heads(px[2]),
                                       k_ctx, v_ctx, na_rpb[l])
        hg_x, hg_c = hgrn2_mixer(px[3:], pc[3:], lb_all[l], hg_norm[l], need_ctx)
        x = x + gt1 * (jnp.concatenate([na_x, hg_x], axis=-1) @ w_out[l])
        if need_ctx:
            na_c = context_attention(_na_heads(pc[0]), k_ctx, v_ctx)
            ctx = ctx + cgt1 * (jnp.concatenate([na_c, hg_c], axis=-1) @ w_out[l])
            ctx = ctx + cgt2 * peer_ffn(modulate(rms_norm(ctx, norm2[l]), csh2, csc2),
                                        peer_wq[l], peer_keys[l], peer_u[l], peer_v[l])

        x = x + gt2 * peer_ffn(modulate(rms_norm(x, norm2[l]), sh2, sc2),
                               peer_wq[l], peer_keys[l], peer_u[l], peer_v[l])
    return rms_norm(x, norm_f)


SB_HEADS = 8
SB_HEAD_DIM = 64
SB_WIDTH = SB_HEADS * SB_HEAD_DIM
MLA_HEADS = 8
MLA_NOPE_DIM = 64
MLA_ROPE_DIM = 32
MLA_V_DIM = 64
MLA_Q_RANK = 384
MLA_KV_RANK = 256
MLA_WIDTH = MLA_HEADS * MLA_V_DIM
MLA_QK_DIM = MLA_NOPE_DIM + MLA_ROPE_DIM

Q_BLOCK = 128
ROPE_BASE = 10000.0

SPLITS = (SB_WIDTH, SB_WIDTH, SB_WIDTH, SB_WIDTH,
          MLA_Q_RANK, MLA_KV_RANK, MLA_ROPE_DIM, MLA_WIDTH,
          D_MODEL, D_MODEL)
IN_WIDTH = int(sum(SPLITS))
SPLIT_POINTS = tuple(int(v) for v in np.cumsum(SPLITS)[:-1])


def rmsnorm(x, g):
    xf = x.astype(jnp.float32)
    y = xf * lax.rsqrt(jnp.mean(xf * xf, axis=-1, keepdims=True) + EPS)
    return (y * g.astype(jnp.float32)).astype(x.dtype)

def rope(x, positions):
    r = x.shape[-1]
    inv_freq = ROPE_BASE ** (-jnp.arange(0, r, 2, dtype=jnp.float32) / r)
    ang = positions.astype(jnp.float32)[:, :, None, None] * inv_freq
    cos, sin = jnp.cos(ang), jnp.sin(ang)
    xf = x.astype(jnp.float32)
    x1, x2 = xf[..., : r // 2], xf[..., r // 2:]
    return jnp.concatenate([x1 * cos - x2 * sin, x1 * sin + x2 * cos], axis=-1)

def to_blocks(t):
    b, h, s, d = t.shape
    return t.reshape(b, h, s // Q_BLOCK, Q_BLOCK, d).transpose(2, 0, 1, 3, 4)

def from_blocks(t):
    n, b, h, q, d = t.shape
    return t.transpose(1, 2, 0, 3, 4).reshape(b, h, n * q, d)

def stick_breaking_attention(q, k, v):
    s_len = k.shape[2]
    scale = 1.0 / math.sqrt(q.shape[-1])
    key_idx = jnp.arange(s_len)

    def block(args):
        qb, i = args
        z = jnp.einsum('bhqd,bhkd->bhqk', qb, k) * scale
        q_idx = i * Q_BLOCK + jnp.arange(Q_BLOCK)
        strict = key_idx[None, :] < q_idx[:, None]
        log_one_minus = jnp.where(strict, jax.nn.log_sigmoid(-z), 0.0)
        suffix = lax.cumsum(log_one_minus, axis=3, reverse=True) - log_one_minus
        w = jnp.where(strict, jnp.exp(jax.nn.log_sigmoid(z) + suffix), 0.0)
        return jnp.einsum('bhqk,bhkd->bhqd', w, v)

    n_blk = s_len // Q_BLOCK
    out = lax.map(block, (to_blocks(q), jnp.arange(n_blk)))
    return from_blocks(out)

def latent_attention(q_nope, q_pe, k_nope, k_pe, v):
    s_len = k_nope.shape[2]
    scale = 1.0 / math.sqrt(MLA_QK_DIM)
    key_idx = jnp.arange(s_len)

    def block(args):
        qn, qp, i = args
        sc = (jnp.einsum('bhqd,bhkd->bhqk', qn, k_nope)
              + jnp.einsum('bhqr,bkr->bhqk', qp, k_pe)) * scale
        q_idx = i * Q_BLOCK + jnp.arange(Q_BLOCK)
        causal = key_idx[None, :] <= q_idx[:, None]
        p = jax.nn.softmax(jnp.where(causal, sc, -jnp.inf), axis=-1)
        return jnp.einsum('bhqk,bhkd->bhqd', p, v)

    n_blk = s_len // Q_BLOCK
    out = lax.map(block, (to_blocks(q_nope), to_blocks(q_pe), jnp.arange(n_blk)))
    return from_blocks(out)

def split_heads(t, h):
    b, s, w = t.shape
    return t.reshape(b, s, h, w // h).transpose(0, 2, 1, 3)

def merge_heads(t):
    b, h, s, d = t.shape
    return t.transpose(0, 2, 1, 3).reshape(b, s, h * d)

def second_inputs(seed: int = 0) -> dict:
    key = jax.random.key(seed)
    ks = jax.random.split(key, 16)
    f32 = jnp.float32

    def nrm(k, shape, fan_in, mult=1.0):
        return jax.random.normal(k, shape, f32) * (mult * fan_in ** -0.5)

    x = jax.random.normal(ks[0], (BATCH, SEQ, D_MODEL), f32)
    c = jax.random.normal(ks[1], (BATCH, D_MODEL), f32)
    positions = jnp.broadcast_to(jnp.arange(SEQ, dtype=jnp.int32), (BATCH, SEQ))
    w_ada = nrm(ks[2], (DEPTH, D_MODEL, 3 * D_MODEL), D_MODEL, 0.2)
    b_ada = jax.random.normal(ks[3], (DEPTH, 3 * D_MODEL), f32) * 0.02
    norm_gain = 1.0 + 0.02 * jax.random.normal(ks[4], (DEPTH, D_MODEL), f32)
    w_in = nrm(ks[5], (DEPTH, D_MODEL, IN_WIDTH), D_MODEL)
    q_norm_gain = 1.0 + 0.02 * jax.random.normal(ks[6], (DEPTH, MLA_Q_RANK), f32)
    w_uq = nrm(ks[7], (DEPTH, MLA_Q_RANK, MLA_HEADS * MLA_QK_DIM), MLA_Q_RANK)
    kv_norm_gain = 1.0 + 0.02 * jax.random.normal(ks[8], (DEPTH, MLA_KV_RANK), f32)
    w_ukv = nrm(ks[9], (DEPTH, MLA_KV_RANK, MLA_HEADS * (MLA_NOPE_DIM + MLA_V_DIM)), MLA_KV_RANK)
    w_branch_a = nrm(ks[10], (DEPTH, SB_WIDTH, D_MODEL), SB_WIDTH)
    w_branch_b = nrm(ks[11], (DEPTH, MLA_WIDTH, D_MODEL), MLA_WIDTH)
    w_out = nrm(ks[12], (DEPTH, D_MODEL, D_MODEL), D_MODEL)
    final_norm_gain = 1.0 + 0.02 * jax.random.normal(ks[13], (D_MODEL,), f32)
    return {"x": x, "c": c, "positions": positions, "w_ada": w_ada, "b_ada": b_ada,
            "norm_gain": norm_gain, "w_in": w_in, "q_norm_gain": q_norm_gain, "w_uq": w_uq,
            "kv_norm_gain": kv_norm_gain, "w_ukv": w_ukv, "w_branch_a": w_branch_a,
            "w_branch_b": w_branch_b, "w_out": w_out, "final_norm_gain": final_norm_gain}

def second_block(x, c, positions, w_ada, b_ada, norm_gain, w_in, q_norm_gain, w_uq,
              kv_norm_gain, w_ukv, w_branch_a, w_branch_b, w_out, final_norm_gain):
    b, s, _ = x.shape
    f32 = jnp.float32
    for l in range(DEPTH):
        mod = c @ w_ada[l] + b_ada[l]
        shift, scale, gate = jnp.split(mod, 3, axis=-1)
        h = rmsnorm(x, norm_gain[l]) * (1.0 + scale[:, None, :]) + shift[:, None, :]

        proj = h @ w_in[l]
        (sb_q, sb_k, sb_v, sb_z, c_q, c_kv, k_rot, mla_z, g_a, g_b) = jnp.split(proj, SPLIT_POINTS, axis=-1)

        o_a = stick_breaking_attention(split_heads(sb_q, SB_HEADS).astype(f32),
                                       split_heads(sb_k, SB_HEADS).astype(f32),
                                       split_heads(sb_v, SB_HEADS).astype(f32))
        o_a = merge_heads(o_a).astype(x.dtype)
        y_a = (o_a * jax.nn.silu(sb_z)) @ w_branch_a[l]

        q = (rmsnorm(c_q, q_norm_gain[l]) @ w_uq[l]).reshape(b, s, MLA_HEADS, MLA_QK_DIM)
        q_nope = q[..., :MLA_NOPE_DIM].astype(f32)
        q_pe = rope(q[..., MLA_NOPE_DIM:], positions)
        kv = (rmsnorm(c_kv, kv_norm_gain[l]) @ w_ukv[l]).reshape(b, s, MLA_HEADS, MLA_NOPE_DIM + MLA_V_DIM)
        k_nope = kv[..., :MLA_NOPE_DIM].astype(f32)
        v_b = kv[..., MLA_NOPE_DIM:].astype(f32)
        k_pe = rope(k_rot[:, :, None, :], positions)[:, :, 0, :]
        o_b = latent_attention(q_nope.transpose(0, 2, 1, 3), q_pe.transpose(0, 2, 1, 3),
                               k_nope.transpose(0, 2, 1, 3), k_pe, v_b.transpose(0, 2, 1, 3))
        o_b = merge_heads(o_b).astype(x.dtype)
        y_b = (o_b * jax.nn.silu(mla_z)) @ w_branch_b[l]

        merged = jax.nn.sigmoid(g_a) * y_a + jax.nn.sigmoid(g_b) * y_b
        x = x + gate[:, None, :] * (merged @ w_out[l])
    return rmsnorm(x, final_norm_gain)


def setup_inputs(seed=0):
    out = dict(first_inputs(seed))
    for name, value in second_inputs(seed + 1).items():
        if name != "x":
            out[name + "_2"] = value
    return out


def reference(
    x, c, ctx, c_ctx, w_mod, b_mod, norm1, norm2, w_in, w_out, na_rpb, hg_lb, hg_norm, peer_wq,
    peer_keys, peer_u, peer_v, norm_f, c_2, positions_2, w_ada_2, b_ada_2, norm_gain_2, w_in_2,
    q_norm_gain_2, w_uq_2, kv_norm_gain_2, w_ukv_2, w_branch_a_2, w_branch_b_2, w_out_2,
    final_norm_gain_2,
):
    x = first_block(
        x, c, ctx, c_ctx, w_mod, b_mod, norm1, norm2, w_in, w_out, na_rpb, hg_lb, hg_norm,
        peer_wq, peer_keys, peer_u, peer_v, norm_f,
    )
    return second_block(
        x, c_2, positions_2, w_ada_2, b_ada_2, norm_gain_2, w_in_2, q_norm_gain_2, w_uq_2,
        kv_norm_gain_2, w_ukv_2, w_branch_a_2, w_branch_b_2, w_out_2, final_norm_gain_2,
    )


_drawn_inputs = setup_inputs


def setup_inputs(seed=0):
    import zlib

    import numpy as np

    out = dict(_drawn_inputs(seed))
    spreads = {}
    factors = {'ctx': 2.833,
     'b_mod': 5.407,
     'norm1': 5.118,
     'norm2': 3.796,
     'na_rpb': 8.0,
     'hg_lb': 5.201,
     'hg_norm': 6.613,
     'b_ada_2': 8.0,
     'norm_gain_2': 8.0,
     'q_norm_gain_2': 8.0,
     'w_uq_2': 6.682,
     'kv_norm_gain_2': 8.0,
     'w_ukv_2': 3.224,
     'w_branch_b_2': 3.332,
     'final_norm_gain_2': 2.773}
    for name, (base, spread) in spreads.items():
        noise = np.random.default_rng([zlib.crc32(name.encode()), seed]).standard_normal(out[name].shape)
        drawn = base * np.exp(spread * noise) if base else spread * noise
        out[name] = jnp.asarray(drawn.astype(out[name].dtype))
    for name, factor in factors.items():
        out[name] = (out[name] * factor).astype(out[name].dtype)
    return out
```

```python
from contextlib import ExitStack

import numpy as np
import concourse.bass as bass
from concourse import mybir

F32 = mybir.dt.float32
U32 = mybir.dt.uint32
I32 = mybir.dt.int32
ALU = mybir.AluOpType
ACT = mybir.ActivationFunctionType
AX = mybir.AxisListType

P = 128
D = 1024
T = 512
C = 256
KT = D // P
NH, DH = 8, 64
ROWS, GW = 8, 64
NCB, QB, KB = 4, 16, 32
HG = 4
EPS = 1e-6
NEG = -1e30
LOWEST = -3e38
NKEYS, TOPK, PH = 128, 16, 8
CHUNK = 512
SLOTS = 2

TWO_PI = (6.28125, 0.0019350051879882812, 3.0199159819602908e-07)
PI_DOWN = float(np.nextafter(np.float32(np.pi), np.float32(0)))

_COLS = [("c", 8), ("c_ctx", 8), ("c_2", 8), ("b_mod", 48), ("norm1", 8), ("norm2", 8), ("norm_f", 8),
         ("b_ada_2", 24), ("norm_gain_2", 8), ("q_norm_gain_2", 3), ("kv_norm_gain_2", 2),
         ("final_norm_gain_2", 8), ("hg_norm", 4), ("hg_lb", 16)]
COL = {}
_n = 0
for _name, _count in _COLS:
    COL[_name] = (_n, _count)
    _n += _count
NCOL = _n


def col(k, name, a=0, b=None):
    start, count = COL[name]
    return k.cols[:, start + a:start + (count if b is None else b)]


class Kernel:
    def __init__(self, nc, dram, out):
        self.nc, self.dram, self.out = nc, dram, out


class Product:
    def __init__(self, chunk, mm, kind=None, dest=None, N=None, out=None, act=None, dve=None, after_act=False,
                 after_dve=0, before=None):
        self.chunk, self.mm, self.kind, self.dest, self.N, self.out = chunk, mm, kind, dest, N, out
        self.act, self.dve, self.after_act, self.after_dve, self.before = act, dve, after_act, after_dve, before


def chain(eng, sem, start=0):
    state = [start]

    def link(ins):
        state[0] += 1
        ins.then_inc(sem, 1)
        eng.wait_ge(sem, state[0])
        return state[0]

    link.state = state
    return link



def plan_stream(k):
    d = k.dram

    def cols_of(w, a, n):
        return w.rearrange("(k p) n -> p k n", p=P)[:, :, a:a + n]

    s = []
    for i in range(4):
        s.append((f"mod{i}", cols_of(d["w_mod"], i * CHUNK, CHUNK)))
    for i in range(8):
        s.append((f"in{i}", cols_of(d["w_in"], i * CHUNK, CHUNK)))
    for i in range(4, 12):
        s.append((f"mod{i}", cols_of(d["w_mod"], i * CHUNK, CHUNK)))
    for i in range(6):
        s.append((f"ada{i}", cols_of(d["w_ada_2"], i * CHUNK, CHUNK)))
    for i in range(2):
        s.append((f"out{i}", cols_of(d["w_out"], i * CHUNK, CHUNK)))
    for i in range(4):
        s.append((f"wq{i}", cols_of(d["peer_wq"], i * CHUNK, CHUNK)))
    for name, a, n in (("cq", 2048, 384), ("kvr", None, 320), ("sq", 0, 512), ("sk", 512, 512), ("sv", 1024, 512),
                       ("sz", 1536, 512), ("mz", 2720, 512)):
        s.append((name, cols_of(d["w_in_2"], a, n) if a is not None else cols_of(d["w_kvr_2"], 0, n)))
    s.append(("uq", cols_of(d["w_uq_2"], 0, 1024)))
    s.append(("ukv", cols_of(d["w_ukv_2"], 0, 1024)))
    for x, a in (("a", 3232), ("b", 4256)):
        for i in range(2):
            s.append((f"g{x}{i}", cols_of(d["w_in_2"], a + i * CHUNK, CHUNK)))
        s.append((f"br{x}", cols_of(d[f"w_branch_{x}_2"], 0, D)))
    for i in range(2):
        s.append((f"wo{i}", cols_of(d["w_out_2"], i * CHUNK, CHUNK)))
    k.stream = s
    k.at = {name: i for i, (name, _) in enumerate(s)}
    k.used = {}
    k.issued = 0


def chunk_view(k, name):
    i = k.at[name]
    _, kt, n = k.stream[i][1].shape
    return k.ring[:, i % SLOTS, 0:kt * n].rearrange("p (k n) -> p k n", k=kt)


def chunk_landed(k, eng, name):
    i = k.at[name]
    eng.wait_ge(k.ring_full[i % SLOTS], 16 * (i // SLOTS + 1))


def load_chunks(k, eng, last):
    while k.issued <= min(last, len(k.stream) - 1):
        i = k.issued
        if i >= SLOTS:
            sem, value = k.used[i - SLOTS]
            eng.wait_ge(sem, value)
        eng.dma_start(chunk_view(k, k.stream[i][0]), k.stream[i][1]).then_inc(k.ring_full[i % SLOTS], 16)
        k.issued += 1



def phase_project(k):
    nc, ps = k.nc, k.ps
    with ExitStack() as ctx:
        def sb(name, shape, dt=F32):
            return ctx.enter_context(nc.sbuf_tensor(name, shape, dt))

        ctxT = sb("ctxT", [P, KT, C])
        hcT = sb("hcT", [P, KT, C])
        vnat = sb("vnat", [P, 4, 512])
        rx = sb("rx", [P, T])
        rc = sb("rc", [P, C])
        sig = sb("sig", [P, 2, 512])
        sc = sb("sc", [P, KT, 2])
        sgc = sb("sgc", [P, 24])
        m1 = sb("m1", [P, 16, 2])
        a1 = sb("a1", [P, 8, 2])
        lbt = sb("lbt", [P, 4, 8])
        hT = k.mixT
        load_x, load_c, load_cols = k.sem("load_x", 2), k.sem("load_ctx"), k.sem("load_cols")
        consts, ones_ready = k.sem("consts_ready"), k.sem("ones_ready")
        squared = k.sem("squared")
        summed = k.sem("a_summed")
        silu_c = k.sem("silu_c")
        sg_c = k.sem("sigmoid_c")
        mod_done = k.sem("mod_done")
        root_in, root_out = k.sem("a_root_in"), k.sem("a_root_out")
        scaled, modulated, affine = k.sem("h_scaled"), k.sem("h_modulated"), k.sem("mod_affine")
        proj, evac, gated = k.sem("proj_done"), k.sem("proj_evac"), k.sem("proj_gated")
        lbs, lb_exp = k.sem("lb_in"), k.sem("lb_exp")
        moved = k.sem("v_moved")
        dve_chain = k.sem("a_dve_chain")

        jobs = []

        def feature_job(chunk, n, tokens, kind, dest):
            w = chunk_view(k, chunk)
            src, N = (hT, T) if tokens == "x" else (hcT, C)
            jobs.append(Product(chunk=chunk, kind=kind, dest=dest, N=N, mm=[
                (w[:, t, n * P:(n + 1) * P], src[:, t, :]) for t in range(KT)]))

        def token_job(chunk, tile, tokens, dest):
            w = chunk_view(k, chunk)
            src = hT if tokens == "x" else hcT
            jobs.append(Product(chunk=chunk, kind="copy", dest=dest, N=512, mm=[
                (src[:, t, tile * P:(tile + 1) * P], w[:, t, :]) for t in range(KT)]))

        for n in range(4):
            feature_job("in0", n, "x", "query", k.qT[:, n, :])
        for n in range(4):
            feature_job("in1", n, "x", "copy", k.kT[:, n, 0:T])
            feature_job("in1", n, "ctx", "copy", k.kT[:, n, T:T + C])
        for t in range(4):
            token_job("in2", t, "x", vnat[:, t, :])
        v_last = len(jobs)
        for t in range(2):
            token_job("in2", t, "ctx", k.vc[:, t, :])
        for n in range(4):
            feature_job("in3", n, "x", "silu", k.hq[:, n, :])
        for d in range(2):
            for n in range(4):
                feature_job(f"in{4 + d}", n, "x", "sigmoid", k.fx[d][:, n, :])
                feature_job(f"in{4 + d}", n, "ctx", "sigmoid", k.fc[d][:, n, :])
        f_last = len(jobs)
        for t in range(4):
            token_job("in6", t, "x", k.ix[:, t, :])
        for t in range(2):
            token_job("in6", t, "ctx", k.ic[:, t, :])
        for n in range(4):
            feature_job("in7", n, "x", "silu", k.hgate[:, n, :])
        NB = 5
        silu_before = [sum(x.kind == "silu" for x in jobs[:j + 1]) for j in range(len(jobs))]
        for j, job in enumerate(jobs):
            k.used[k.at[job.chunk]] = (proj, j + 1)
        n_mod = 0
        mods = [f"mod{i}" for i in range(4)] + [f"mod{i}" for i in range(4, 12)] + [f"ada{i}" for i in range(6)]
        for name in mods:
            n_mod += 1
            k.used[k.at[name]] = (mod_done, n_mod)

        block = ctx.enter_context(nc.Block())

        @block.sync
        def _(sp):
            sp.dma_start(k.cols[:], k.dram["cols"]).then_inc(load_cols, 16)
            xv = k.dram["xT"].rearrange("(k p) t -> p k t", p=P)
            for h in range(2):
                sp.dma_start(k.xT[:, 4 * h:4 * h + 4, :], xv[:, 4 * h:4 * h + 4, :]).then_inc(load_x[h], 16)
            sp.dma_start(ctxT[:], k.dram["ctxT"].rearrange("(k p) t -> p k t", p=P)).then_inc(load_c, 16)
            load_chunks(k, sp, k.at["in2"] + 1)
            sp.wait_ge(evac, v_last)
            for c in range(NCB):
                k0 = min(max(QB * c - KB // 4, 0), GW - KB)
                for r in range(ROWS):
                    sp.dma_start(k.vw[KB * (r % 4):KB * (r % 4) + KB, 2 * c + r // 4, :],
                                 vnat[GW * (r % 2) + k0:GW * (r % 2) + k0 + KB, r // 2, :]).then_inc(moved, 16)
            load_chunks(k, sp, k.at["ada5"] + SLOTS)
            sp.wait_ge(moved, 16 * NCB * ROWS)

        @block.gpsimd
        def _(pool):
            pool.memset(k.ones[:], 1.0).then_inc(ones_ready, 1)
            pool.memset(k.zeros[:], 0.0).then_inc(consts, 1)
            pool.wait_ge(consts, 1)
            pool.affine_select(out=k.ident[:], in_=k.zeros[:, 0:P], compare_op=ALU.not_equal, fill=1.0, base=0,
                               pattern=[[-1, P]], channel_multiplier=1).then_inc(consts, 1)

        @block.vector
        def _(dve):
            link = chain(dve, dve_chain)
            dve.wait_ge(load_cols, 16)
            lb0, lb1 = col(k, "hg_lb", 0, 8), col(k, "hg_lb", 8, 16)
            link(dve.tensor_tensor(lbt[:, 2, :], lb0, lb1, ALU.max))
            dve.tensor_tensor(lbt[:, 0, :], lb0, lbt[:, 2, :], ALU.subtract).then_inc(lbs, 1)
            dve.tensor_tensor(lbt[:, 1, :], lb1, lbt[:, 2, :], ALU.subtract).then_inc(lbs, 1)
            dve.wait_ge(sg_c, 1)
            dve.tensor_tensor(sc[:, :, 0], col(k, "c"), sgc[:, 0:8], ALU.mult).then_inc(silu_c, 1)
            dve.tensor_tensor(sc[:, :, 1], col(k, "c_ctx"), sgc[:, 8:16], ALU.mult).then_inc(silu_c, 1)
            for h in range(2):
                dve.wait_ge(load_x[h], 16)
                dve.tensor_tensor(hT[:, 4 * h:4 * h + 4, :], k.xT[:, 4 * h:4 * h + 4, :],
                                  k.xT[:, 4 * h:4 * h + 4, :], ALU.mult).then_inc(squared, 1)
            dve.wait_ge(load_c, 16)
            dve.tensor_tensor(hcT[:], ctxT[:], ctxT[:], ALU.mult).then_inc(squared, 1)
            dve.wait_ge(summed, 1)
            dve.tensor_scalar(rx[:], ps[:, 5, :], 1.0 / D, EPS, ALU.mult, ALU.add).then_inc(root_in, 1)
            dve.wait_ge(summed, 2)
            dve.tensor_scalar(rc[:], ps[:, 6, 0:C], 1.0 / D, EPS, ALU.mult, ALU.add).then_inc(root_in, 1)
            dve.wait_ge(lb_exp, 1)
            link(dve.tensor_tensor(lbt[:, 2, :], lbt[:, 0, :], lbt[:, 1, :], ALU.add))
            link(dve.reciprocal(lbt[:, 3, :], lbt[:, 2, :]))
            link(dve.tensor_tensor(lbt[:, 0, :], lbt[:, 0, :], lbt[:, 3, :], ALU.mult))
            link(dve.tensor_scalar(lbt[:, 1, :], lbt[:, 0, :], -1.0, 1.0, ALU.mult, ALU.add))
            dve.wait_ge(root_out, 1)
            link(dve.reciprocal(rx[:], rx[:]))
            dve.wait_ge(root_out, 2)
            link(dve.reciprocal(rc[:], rc[:]))
            dve.wait_ge(mod_done, 4)
            b16 = col(k, "b_mod", 0, 16).unsqueeze(2).to_broadcast([P, 16, 2])
            link(dve.tensor_tensor(m1[:], ps[:, 7, 0:32].rearrange("p (j s) -> p j s", s=2), b16, ALU.add))
            g8 = col(k, "norm1").unsqueeze(2).to_broadcast([P, 8, 2])
            dve.scalar_tensor_tensor(a1[:], m1[:, 8:16, :], 1.0, g8, ALU.add, ALU.mult).then_inc(affine, 1)
            for t in range(KT):
                dve.tensor_tensor(hT[:, t, :], k.xT[:, t, :], rx[:], ALU.mult).then_inc(scaled, 1)
                dve.tensor_tensor(hcT[:, t, :], ctxT[:, t, :], rc[:], ALU.mult).then_inc(scaled, 1)
            n = 0
            for j, job in enumerate(jobs):
                if job.kind == "silu":
                    n += 1
                    dve.wait_ge(evac, j + 1)
                    dve.tensor_tensor(job.dest, ps[:, j % NB, 0:job.N], sig[:, n % 2, :], ALU.mult).then_inc(gated, 1)
                if j == f_last - 1:
                    dve.wait_ge(evac, f_last)
                    for d in range(2):
                        for h in range(HG):
                            i = 4 * d + h
                            for f in (k.fx[d], k.fc[d]):
                                dve.tensor_scalar(f[:, h, :], f[:, h, :], lbt[:, 1, i:i + 1], lbt[:, 0, i:i + 1],
                                                  ALU.mult, ALU.add)
            dve.wait_ge(mod_done, n_mod)
            link(dve.tensor_tensor(k.mod[:], ps[:, 7, 0:96].rearrange("p (j s) -> p j s", s=2)[:, :, 0],
                                   col(k, "b_mod"), ALU.add))
            link(dve.tensor_tensor(k.ada[:], ps[:, 7, 96:120], col(k, "b_ada_2"), ALU.add))

        @block.scalar
        def _(act):
            act.wait_ge(load_cols, 16)
            act.activation(sgc[:, 0:16], k.cols[:, 0:16], ACT.Sigmoid).then_inc(sg_c, 1)
            act.wait_ge(lbs, 2)
            act.activation(lbt[:, 0:2, :], lbt[:, 0:2, :], ACT.Exp).then_inc(lb_exp, 1)
            act.wait_ge(root_in, 1)
            act.activation(rx[:], rx[:], ACT.Sqrt).then_inc(root_out, 1)
            act.wait_ge(root_in, 2)
            act.activation(rc[:], rc[:], ACT.Sqrt).then_inc(root_out, 1)
            act.wait_ge(affine, 1)
            for t in range(KT):
                for s, h in ((0, hT), (1, hcT)):
                    act.wait_ge(scaled, 2 * t + s + 1)
                    act.activation(h[:, t, :], h[:, t, :], ACT.Identity, scale=a1[:, t, s:s + 1],
                                   bias=m1[:, t, s:s + 1]).then_inc(modulated, 1)
            n = 0
            for j, job in enumerate(jobs):
                act.wait_ge(proj, j + 1)
                src = ps[:, j % NB, 0:job.N]
                if job.kind == "query":
                    act.activation(job.dest.rearrange("p (c r l) -> p r c l", c=NCB, r=ROWS),
                                   src.rearrange("p (r c l) -> p r c l", r=ROWS, c=NCB), ACT.Copy,
                                   scale=DH ** -0.5).then_inc(evac, 1)
                elif job.kind == "silu":
                    n += 1
                    if n > 2:
                        act.wait_ge(gated, n - 2)
                    act.activation(sig[:, n % 2, :], src, ACT.Sigmoid).then_inc(evac, 1)
                else:
                    act.activation(job.dest, src, ACT.Sigmoid if job.kind == "sigmoid" else ACT.Copy).then_inc(evac, 1)

        @block.tensor
        def _(pe):
            pe.wait_ge(ones_ready, 1)
            for t in range(KT):
                if t % 4 == 0:
                    pe.wait_ge(squared, t // 4 + 1)
                last = pe.matmul(ps[:, 5, :], k.ones[:], hT[:, t, :], start=t == 0, stop=t == KT - 1)
            last.then_inc(summed, 1)
            pe.wait_ge(squared, 3)
            for t in range(KT):
                last = pe.matmul(ps[:, 6, 0:C], k.ones[:], hcT[:, t, :], start=t == 0, stop=t == KT - 1)
            last.then_inc(summed, 1)
            pe.wait_ge(silu_c, 2)

            def modulation(names, rhs, first, width):
                for i, name in enumerate(names):
                    chunk_landed(k, pe, name)
                    w = chunk_view(k, name)
                    for n in range(4):
                        at = first + width * (4 * i + n)
                        for t in range(KT):
                            last = pe.matmul(ps[:, 7, at:at + width], w[:, t, n * P:(n + 1) * P], rhs[:, t, :],
                                             start=t == 0, stop=t == KT - 1)
                    last.then_inc(mod_done, 1)

            modulation([f"mod{i}" for i in range(4)], sc, 0, 2)
            pe.wait_ge(modulated, 2 * KT)
            now = None
            for j, job in enumerate(jobs):
                if job.chunk != now:
                    now = job.chunk
                    chunk_landed(k, pe, now)
                if j >= NB:
                    pe.wait_ge(evac, j - NB + 1)
                    if jobs[j - NB].kind == "silu":
                        pe.wait_ge(gated, silu_before[j - NB])
                for i, (a, b) in enumerate(job.mm):
                    last = pe.matmul(ps[:, j % NB, 0:job.N], a, b, start=i == 0, stop=i == KT - 1)
                last.then_inc(proj, 1)
            modulation([f"mod{i}" for i in range(4, 12)], sc, 32, 2)
            modulation([f"ada{i}" for i in range(6)], col(k, "c_2").unsqueeze(2), 96, 1)



def phase_neighbourhood(k):
    nc, ps = k.nc, k.ps
    WIN = ROWS * KB
    items = [(2 * hp + s, c) for hp in range(4) for c in range(NCB) for s in range(2)]
    N = len(items)
    variant = [0, 1, 1, 2]
    with ExitStack() as ctx:
        def sb(name, shape, dt=F32):
            return ctx.enter_context(nc.sbuf_tensor(name, shape, dt))

        toep = sb("toep", [P, ROWS, NH, KB + QB])
        bias = sb("bias", [P, 3, ROWS, NH, KB])
        mask = sb("win_mask", [P, 3, KB])
        s_sb = sb("s_sb", [P, 3, 512])
        pT = sb("pT", [P, 2, 512])
        mx = sb("na_max", [P, N, 4])
        sums = sb("na_sums", [P, N, 2])
        loaded, table = k.sem("rpb_loaded"), k.sem("bias_table")
        scored, maxed, nmax = k.sem("na_scored"), k.sem("na_maxed"), k.sem("na_nmax")
        exped, recip, normed = k.sem("na_exp"), k.sem("na_recip"), k.sem("na_normed")
        turned, turned_sb, summed, stored = (k.sem("na_turned"), k.sem("na_turned_sb"), k.sem("na_pv"),
                                             k.sem("na_stored"))
        block = ctx.enter_context(nc.Block())

        @block.sync
        def _(sp):
            for r in range(ROWS):
                sp.dma_start(toep[QB * r:QB * r + QB], k.dram["rpb_shifted"][:, ROWS - 1 - r:2 * ROWS - 1 - r])\
                  .then_inc(loaded, 16)
            sp.dma_start(mask[:], k.dram["win_mask"]).then_inc(loaded, 16)

        @block.gpsimd
        def _(pool):
            pool.wait_ge(loaded, 16 * (ROWS + 1))
            for v, off in enumerate((16, 8, 0)):
                pool.tensor_tensor(bias[:, v].rearrange("p a h m -> p (a h) m"),
                                   toep[:, :, :, off:off + KB].rearrange("p a h m -> p (a h) m"),
                                   mask[:, v, :].unsqueeze(1).to_broadcast([P, ROWS * NH, KB]),
                                   ALU.add).then_inc(table, 1)

        @block.tensor
        def _(pe):
            def scores(i):
                h, c = items[i]
                a, hp = DH * (h % 2), h // 2
                if i >= 2:
                    pe.wait_ge(maxed, 2 * (i - 1))
                q = k.qT[a:a + DH, hp, c * P:(c + 1) * P]
                k0 = min(max(QB * c - KB // 4, 0), GW - KB)
                win = k.kT[a:a + DH, hp, 0:T].rearrange("p (r x) -> p r x", r=ROWS)[:, :, k0:k0 + KB]
                pe.matmul(ps[:, i % 2, 0:WIN], q, win, start=True, stop=True)
                pe.matmul(ps[:, i % 2, WIN:512], q, k.kT[a:a + DH, hp, T:T + C], start=True, stop=True)\
                  .then_inc(scored, 1)

            def turn(i):
                pe.wait_ge(normed, i + 1)
                if i >= 2:
                    pe.wait_ge(turned_sb, i - 1)
                for j in range(4):
                    last = pe.transpose(ps[:, 2 + i % 2, j * P:(j + 1) * P], s_sb[:, i % 3, j * P:(j + 1) * P],
                                        k.ident[:])
                last.then_inc(turned, 1)

            def values(i):
                h, c = items[i]
                pair = i // 2
                pe.wait_ge(turned_sb, i + 1)
                if i % 2 == 0 and pair >= 2:
                    pe.wait_ge(stored, pair - 1)
                a = DH * (h % 2)
                for j in range(4):
                    v = (k.vw[:, 2 * c + j, :] if j < 2 else k.vc[:, j - 2, :])[:, h * DH:(h + 1) * DH]
                    last = pe.matmul(ps[a:a + DH, 4 + pair % 2, 0:P], v, pT[:, i % 2, j * P:(j + 1) * P],
                                     start=j == 0, stop=j == 3)
                last.then_inc(summed, 1)

            for n in range(N + 3):
                if n < N:
                    scores(n)
                if 0 <= n - 2 < N:
                    turn(n - 2)
                if 0 <= n - 3 < N:
                    values(n - 3)

        @block.vector
        def _(dve):
            dve.wait_ge(table, 3)
            for n in range(N + 1):
                if n < N:
                    h, c = items[n]
                    dve.wait_ge(scored, n + 1)
                    if n >= 3:
                        dve.wait_ge(turned, n - 2)
                    dve.tensor_tensor_reduce(
                        s_sb[:, n % 3, 0:WIN].rearrange("p (r x) -> p r x", r=ROWS),
                        ps[:, n % 2, 0:WIN].rearrange("p (r x) -> p r x", r=ROWS), bias[:, variant[c], :, h, :],
                        1.0, LOWEST, ALU.add, ALU.max, mx[:, n, 0:1]).then_inc(maxed, 1)
                    dve.tensor_tensor_reduce(s_sb[:, n % 3, WIN:512], ps[:, n % 2, WIN:512], k.zeros[:, 0:C], 1.0, LOWEST,
                                             ALU.add, ALU.max, mx[:, n, 1:2]).then_inc(maxed, 1)
                    dve.wait_ge(maxed, 2 * n + 2)
                    dve.tensor_reduce(mx[:, n, 2:3], mx[:, n, 0:2], AX.X, ALU.max, negate=True).then_inc(nmax, 1)
                if n >= 1:
                    i = n - 1
                    dve.wait_ge(exped, i + 1)
                    dve.reciprocal(sums[:, i, 1:2], sums[:, i, 0:1]).then_inc(recip, 1)
                    dve.wait_ge(recip, i + 1)
                    dve.tensor_scalar(s_sb[:, i % 3, :], s_sb[:, i % 3, :], sums[:, i, 1:2], None, ALU.mult)\
                       .then_inc(normed, 1)

        @block.scalar
        def _(act):
            for n in range(N + 4):
                if n < N:
                    act.wait_ge(nmax, n + 1)
                    act.activation(s_sb[:, n % 3, :], s_sb[:, n % 3, :], ACT.Exp, bias=mx[:, n, 2:3],
                                   accum_out=sums[:, n, 0:1]).then_inc(exped, 1)
                if 0 <= n - 2 < N:
                    i = n - 2
                    act.wait_ge(turned, i + 1)
                    if i >= 2:
                        act.wait_ge(summed, i - 1)
                    act.activation(pT[:, i % 2, :], ps[:, 2 + i % 2, :], ACT.Copy).then_inc(turned_sb, 1)
                if 0 <= n - 4 < N and (n - 4) % 2:
                    pair = (n - 4) // 2
                    hp, c = divmod(pair, NCB)
                    act.wait_ge(summed, 2 * pair + 2)
                    act.activation(k.mixT[:, hp, :].rearrange("p (r c l) -> p c r l", r=ROWS, c=NCB)[:, c],
                                   ps[:, 4 + pair % 2, 0:P].rearrange("p (r l) -> p r l", r=ROWS),
                                   ACT.Copy).then_inc(stored, 1)



def phase_hgrn(k):
    nc, ps = k.nc, k.ps
    TILES = T // P
    LEV = 7
    with ExitStack() as ctx:
        def sb(name, shape, dt=F32):
            return ctx.enter_context(nc.sbuf_tensor(name, shape, dt))

        kk = sb("kk", [P, HG, T])
        suf = sb("suf", [P, HG, T])
        qd = sb("qd", [P, 2, HG, T])
        kd = sb("kd", [P, 2, HG, T])
        A = sb("A_diag", [P, HG * TILES, P])
        aoff = sb("A_off", [P, HG, 6, P])
        state = sb("ctx_state", [P, 2, HG, P])
        pred = sb("pred", [P, 2, LEV, P], mybir.dt.uint8)
        kc, sufc = kd[:, 0, 0:2, :].rearrange("p a t -> p (a t)").rearrange("p (h t) -> p h t", h=HG), \
            kd[:, 0, 2:4, :].rearrange("p a t -> p (a t)").rearrange("p (h t) -> p h t", h=HG)
        kcT = kd[:, 1, 0:2, :].rearrange("p a t -> p (a t)").rearrange("p (n d) -> p n d", d=P)
        square, root = qd[:, 0], qd[:, 1]
        pred_f = qd[:, 1].rearrange("p h t -> p (h t)")[:, 0:2 * LEV * P]
        cdve = k.sem("hg_dve_chain")
        keys_c, turned_c, turned_c_sb = k.sem("ctx_keys"), k.sem("ctx_turned"), k.sem("ctx_turned_sb")
        state_mm, state_sb, preds = k.sem("ctx_state_mm"), k.sem("ctx_state_sb"), k.sem("pred_loaded")
        kk_ready, ready, updated = k.sem("kk_ready"), k.sem("level_ready"), k.sem("level_updated")
        level_mm, level_cp, av = k.sem("level_mm"), k.sem("level_copied"), k.sem("av_done")
        suf_one = k.sem("suf_one")
        squares, norm_mm, rooted, rin, o_norm = (k.sem("hg_squares"), k.sem("hg_norm_mm"), k.sem("hg_rooted"),
                                                 k.sem("hg_root_in"), k.sem("hg_o_norm"))

        def n_ready(d, s):
            return 19 * d + min(2 * s, 19)

        def n_mm(d, s, half=1):
            return 18 * d + (2 * s + half + 1 if s <= LEV else s + 9)

        def n_upd(d, s):
            return 17 * d + min(2 * s, 17)

        def halves(x, s, d):
            v = x.rearrange("p h t -> p (h t)").rearrange("p (n two m) -> p n two m", two=2, m=1 << (s - 1))
            return v[:, :, d, :], v[:, :, 1 - d, :]

        def totals(pre, s, d):
            m = 1 << (s - 1)
            a, b = halves(pre, s, d)
            at = 0 if d else m - 1
            return [x[:, :, at:at + 1].to_broadcast([P, HG * T // (2 * m), m]) for x in (a, b)]

        block = ctx.enter_context(nc.Block())

        @block.sync
        def _(sp):
            sp.dma_start(pred_f, k.dram["pred"].rearrange("p d s t -> p (d s t)")).then_inc(preds, 16)

        @block.gpsimd
        def _(pool):
            for d in range(2):
                if d:
                    pool.wait_ge(ready, n_ready(0, 9))
                    pool.wait_ge(updated, n_upd(0, 9))
                else:
                    pool.wait_ge(state_mm, 2)
                pool.memset(suf[:], 1.0).then_inc(suf_one, 1)
                for s in range(1, 11):
                    m = 10 * d + s - 1
                    if s == 1:
                        pool.wait_ge(kk_ready, d + 1)
                        pool.wait_ge(suf_one, d + 1)
                    else:
                        pool.wait_ge(updated, n_upd(d, s - 1))
                    if m >= 2:
                        if s == 1:
                            pool.wait_ge(level_mm, n_mm(0, 9))
                        elif s == 2:
                            pool.wait_ge(level_mm, n_mm(d - 1, 9))
                            if d:
                                pool.wait_ge(av, HG * d)
                        else:
                            pool.wait_ge(level_mm, n_mm(d, s - 2))
                    q, key = qd[:, m % 2], kd[:, m % 2]
                    pre = k.fx[d]
                    if s == 10:
                        pool.tensor_tensor(q[:], k.hq[:], pre[:], ALU.mult).then_inc(ready, 1)
                        continue
                    if m < 2:
                        pool.tensor_tensor(key[:], kk[:], suf[:], ALU.mult).then_inc(ready, 1)
                        pool.tensor_tensor(q[:], k.hq[:], pre[:], ALU.mult).then_inc(ready, 1)
                        continue
                    pool.tensor_tensor(halves(key, s, d)[0], halves(kk, s, d)[0], halves(suf, s, d)[0],
                                       ALU.mult).then_inc(ready, 1)
                    pool.tensor_tensor(halves(q, s, d)[1], halves(k.hq, s, d)[1], halves(pre, s, d)[1],
                                       ALU.mult).then_inc(ready, 1)

        @block.vector
        def _(dve):
            link = chain(dve, cdve)
            for d in range(2):
                if d:
                    dve.wait_ge(turned_c, 1)
                f = k.fc[d]
                link(dve.memset(sufc[:], 1.0))
                link(dve.tensor_scalar(kc[:], f[:], -1.0, 1.0, ALU.mult, ALU.add))
                for h in range(HG):
                    if d == 0:
                        o, g = sufc[:, h, C - 2::-1], f[:, h, C - 1:0:-1]
                    else:
                        o, g = sufc[:, h, 1:C], f[:, h, 0:C - 1]
                    last = dve.tensor_tensor_scan(out=o, data0=g, data1=k.zeros[:, 0:C - 1], initial=1.0,
                                                  op0=ALU.mult, op1=ALU.add)
                link(last)
                dve.tensor_tensor(kc[:], kc[:], sufc[:], ALU.mult).then_inc(keys_c, 1)
            dve.wait_ge(preds, 16)
            link(dve.tensor_copy(pred[:].rearrange("p d s t -> p (d s t)"), pred_f))
            for d in range(2):
                if d:
                    dve.wait_ge(ready, n_ready(0, 9))
                dve.tensor_scalar(kk[:], k.fx[d][:], -1.0, 1.0, ALU.mult, ALU.add).then_inc(kk_ready, 1)
                for s in range(10):
                    if s <= LEV:
                        for half in range(2):
                            dve.wait_ge(level_mm, n_mm(d, s, half))
                            src = ps[:, 2 * half:2 * half + 2, :].rearrange("p b (i t) -> p (b i) t", t=P)
                            dst = A[:, 8 * half:8 * half + 8, :]
                            if s == 0:
                                if d and half == 0:
                                    dve.wait_ge(av, HG)
                                ins = dve.tensor_tensor(dst, src, k.ident[:].unsqueeze(1).to_broadcast([P, 8, P]),
                                                        ALU.mult)
                            else:
                                dve.wait_ge(level_cp, n_mm(d, s - 1, half))
                                ins = dve.copy_predicated(
                                    dst, pred[:, d, s - 1, :].unsqueeze(1).to_broadcast([P, 8, P]), src)
                            ins.then_inc(level_cp, 1)
                    else:
                        dve.wait_ge(level_mm, n_mm(d, s))
                        if s == 8:
                            dve.tensor_copy(aoff[:, :, 0:2, :], ps[:, 0:2, :].rearrange("p b (h i t) -> p (b h) i t", i=2, t=P))\
                               .then_inc(level_cp, 1)
                        else:
                            dve.tensor_copy(aoff[:, :, 2:6, :], ps[:, 0:4, :].rearrange("p h (i t) -> p h i t", t=P))\
                               .then_inc(level_cp, 1)
                    if s >= 1:
                        dve.wait_ge(ready, n_ready(d, s))
                        pre = k.fx[d]
                        tot_s, tot_q = totals(pre, s, d)
                        if s < 9:
                            side = halves(suf, s, d)[0]
                            dve.tensor_tensor(side, side, tot_q, ALU.mult).then_inc(updated, 1)
                        dve.wait_ge(updated, n_upd(d, s) - 1)
                        side = halves(pre, s, d)[1]
                        dve.tensor_tensor(side, side, tot_s, ALU.mult).then_inc(updated, 1)
                        dve.wait_ge(updated, n_upd(d, s))
            for h in range(HG):
                dve.wait_ge(norm_mm, h + 1)
                dve.tensor_scalar(root[:, h, :], ps[:, h, :], 1.0 / P, EPS, ALU.mult, ALU.add).then_inc(rin, 1)
            for h in range(HG):
                dve.wait_ge(rooted, h + 1)
                link(dve.reciprocal(root[:, h, :], root[:, h, :]))
                link(dve.scalar_tensor_tensor(root[:, h, :], ps[:, 4 + h, :], col(k, "hg_norm", h, h + 1),
                                              root[:, h, :], ALU.mult, ALU.mult))
                dve.tensor_tensor(k.mixT[:, 4 + h, :], root[:, h, :], k.hgate[:, h, :], ALU.mult)

        @block.scalar
        def _(act):
            for d in range(2):
                act.wait_ge(turned_c, d + 1)
                if d:
                    act.wait_ge(state_mm, 1)
                act.activation(kcT[:], ps[:, 0:2, :].rearrange("p b (i t) -> p (b i) t", t=P), ACT.Copy)\
                   .then_inc(turned_c_sb, 1)
                act.wait_ge(state_mm, d + 1)
                act.activation(state[:, d], ps[:, 2, :].rearrange("p (h t) -> p h t", t=P), ACT.Copy)\
                   .then_inc(state_sb, 1)
            act.wait_ge(av, 2 * HG)
            for h in range(HG):
                act.activation(square[:, h, :], ps[:, 4 + h, :], ACT.Square).then_inc(squares, 1)
            for h in range(HG):
                act.wait_ge(rin, h + 1)
                act.activation(root[:, h, :], root[:, h, :], ACT.Sqrt).then_inc(rooted, 1)

        @block.tensor
        def _(pe):
            for d in range(2):
                pe.wait_ge(keys_c, d + 1)
                if d:
                    pe.wait_ge(turned_c_sb, 1)
                for i in range(2 * HG):
                    h, j = divmod(i, 2)
                    last = pe.transpose(ps[:, i // 4, (i % 4) * P:(i % 4 + 1) * P], kc[:, h, j * P:(j + 1) * P],
                                        k.ident[:])
                last.then_inc(turned_c, 1)
                pe.wait_ge(turned_c_sb, d + 1)
                if d:
                    pe.wait_ge(state_sb, 1)
                for h in range(HG):
                    for j in range(2):
                        last = pe.matmul(ps[:, 2, h * P:(h + 1) * P], kcT[:, 2 * h + j, :],
                                         k.ic[:, j, h * P:(h + 1) * P], start=j == 0, stop=j == 1)
                last.then_inc(state_mm, 1)
            pe.wait_ge(state_sb, 2)
            for d in range(2):
                for s in range(LEV + 1):
                    if s == 0:
                        pe.wait_ge(kk_ready, d + 1)
                        q, key = k.hq, kk
                    else:
                        m = 10 * d + s - 1
                        pe.wait_ge(ready, n_ready(d, s))
                        q, key = qd[:, m % 2], kd[:, m % 2]
                    for half in range(2):
                        done = n_mm(d, s, half) - 2 if s else 18 * d
                        if done > 0:
                            pe.wait_ge(level_cp, done)
                        for h in (2 * half, 2 * half + 1):
                            for i in range(TILES):
                                last = pe.matmul(ps[:, h, i * P:(i + 1) * P], key[:, h, i * P:(i + 1) * P],
                                                 q[:, h, i * P:(i + 1) * P], start=True, stop=True)
                        last.then_inc(level_mm, 1)
                pe.wait_ge(ready, n_ready(d, 8))
                pe.wait_ge(level_cp, n_mm(d, 7, 0))
                m = 10 * d + 7
                q, key = qd[:, m % 2], kd[:, m % 2]
                for h in range(HG):
                    for i in range(2):
                        a, b = 2 * i + d, 2 * i + 1 - d
                        at = (2 * h + i) % 4 * P
                        last = pe.matmul(ps[:, h // 2, at:at + P], key[:, h, a * P:(a + 1) * P],
                                         q[:, h, b * P:(b + 1) * P], start=True, stop=True)
                last.then_inc(level_mm, 1)
                pe.wait_ge(ready, n_ready(d, 9))
                pe.wait_ge(level_cp, n_mm(d, 8))
                m += 1
                q, key = qd[:, m % 2], kd[:, m % 2]
                for h in range(HG):
                    for i in range(2):
                        a, b = 2 * d + i, 2 * (1 - d)
                        last = pe.matmul(ps[:, h, 2 * i * P:2 * (i + 1) * P], key[:, h, a * P:(a + 1) * P],
                                         q[:, h, b * P:(b + 2) * P], start=True, stop=True)
                last.then_inc(level_mm, 1)
                pe.wait_ge(ready, n_ready(d, 10))
                pe.wait_ge(level_cp, n_mm(d, 9))
                m += 1
                q = qd[:, m % 2]
                for h in range(HG):
                    def values(tile):
                        return k.ix[:, tile, h * P:(h + 1) * P]

                    pe.matmul(ps[:, 4 + h, :], state[:, d, h, :], q[:, h, :], start=d == 0, stop=False)
                    for i in range(TILES):
                        pe.matmul(ps[:, 4 + h, i * P:(i + 1) * P], values(i), A[:, TILES * h + i, :],
                                  start=False, stop=False)
                    for i in range(2):
                        a, b = 2 * i + d, 2 * i + 1 - d
                        pe.matmul(ps[:, 4 + h, b * P:(b + 1) * P], values(a), aoff[:, h, i, :],
                                  start=False, stop=False)
                    for i in range(2):
                        a, b = 2 * d + i, 2 * (1 - d)
                        last = pe.matmul(ps[:, 4 + h, b * P:(b + 2) * P], values(a),
                                         aoff[:, h, 2 + 2 * i:4 + 2 * i, :].rearrange("p i t -> p (i t)"),
                                         start=False, stop=d == 1 and i == 1)
                    last.then_inc(av, 1)
            for h in range(HG):
                pe.wait_ge(squares, h + 1)
                pe.matmul(ps[:, h, :], k.ones[:], square[:, h, :], start=True, stop=True).then_inc(norm_mm, 1)



class Norm:

    def __init__(self, k, src, dst, root, bank, tiles, gain, shift=None):
        self.k, self.src, self.dst, self.root, self.bank, self.tiles = k, src, dst, root, bank, tiles
        self.gain, self.shift = gain, shift
        (self.squared, self.summed, self.mean, self.rooted, self.inverse, self.scaled, self.done) = k.norm_sems
        self.n, self.t0 = k.norms + 1, k.norm_tiles
        k.norms, k.norm_tiles = k.norms + 1, k.norm_tiles + tiles

    def act_square(self, act):
        for t in range(self.tiles):
            act.activation(self.dst[:, t, :], self.src[:, t, :], ACT.Square).then_inc(self.squared, 1)

    def pe_sum(self, pe):
        for t in range(self.tiles):
            pe.wait_ge(self.squared, self.t0 + t + 1)
            last = pe.matmul(self.k.ps[:, self.bank, :], self.k.ones[:], self.dst[:, t, :], start=t == 0,
                             stop=t == self.tiles - 1)
        last.then_inc(self.summed, 1)

    def act_root(self, act):
        act.wait_ge(self.mean, self.n)
        act.activation(self.root, self.root, ACT.Sqrt).then_inc(self.rooted, 1)

    def dve_scale(self, dve):
        dve.wait_ge(self.summed, self.n)
        dve.tensor_scalar(self.root, self.k.ps[:, self.bank, :], 1.0 / (P * self.tiles), EPS, ALU.mult, ALU.add)\
           .then_inc(self.mean, 1)
        dve.wait_ge(self.rooted, self.n)
        dve.reciprocal(self.root, self.root).then_inc(self.inverse, 1)
        dve.wait_ge(self.inverse, self.n)
        for t in range(self.tiles):
            dve.tensor_tensor(self.dst[:, t, :], self.src[:, t, :], self.root, ALU.mult).then_inc(self.scaled, 1)

    def act_affine(self, act):
        for t in range(self.tiles):
            act.wait_ge(self.scaled, self.t0 + t + 1)
            extra = {} if self.shift is None else {"bias": self.shift[:, t:t + 1]}
            act.activation(self.dst[:, t, :], self.dst[:, t, :], ACT.Copy if self.shift is None else ACT.Identity,
                           scale=self.gain[:, t:t + 1], **extra).then_inc(self.done, 1)

    def wait(self, eng, tiles=None):
        eng.wait_ge(self.done, self.t0 + (self.tiles if tiles is None else tiles))



def phase_route(k):
    nc, ps = k.nc, k.ps
    TT = T // P
    HH = 2 * PH
    with ExitStack() as ctx:
        def sb(name, shape, dt=F32):
            return ctx.enter_context(nc.sbuf_tensor(name, shape, dt))

        qp = sb("peer_q", [P, HH, T])
        keys = sb("peer_keysT", [P, HH, NKEYS])
        s_sb = sb("peer_s", [P, 2, HH, NKEYS])
        s_cut = sb("peer_s_cut", [P, HH, NKEYS])
        val = sb("peer_val", [P, HH, TOPK])
        ind = sb("peer_ind", [P, HH, TOPK], U32)
        indf = sb("peer_indf", [P, HH, TOPK])
        cand = sb("peer_cand", [P, PH, TOPK * TOPK])
        cand_cut = s_cut[:].rearrange("p (h two) n -> p h (two n)", two=2)
        top = sb("peer_top", [P, PH, TOPK])
        pos = sb("peer_pos", [P, PH * TOPK], U32)
        half = sb("peer_half", [P, 2, PH * TOPK], U32)
        pick = sb("peer_pick", [P, 2, PH * TOPK, TOPK])
        sel = sb("peer_sel", [P, 3, PH * TOPK])
        small = sb("peer_small", [P, 2, PH])
        io16 = sb("io16", [P, TOPK], I32)
        rt = sb("c_root", [P, T])
        a2 = sb("c_gain", [P, 8])
        cdve = k.sem("c_dve_chain")
        out_mm, out_sb, a2_ready = k.sem("out_mm"), k.sem("out_sb"), k.sem("c_gain_ready")
        q_mm, q_sb, keys_in = k.sem("peer_q_mm"), k.sem("peer_q_sb"), k.sem("peer_keys_loaded")
        s_mm, s_ready, s_used = k.sem("peer_s_mm"), k.sem("peer_s_ready"), k.sem("peer_s_used")
        io_ready, shifted, exped = k.sem("io_ready"), k.sem("top_shifted"), k.sem("top_exp")
        split, picked, selected = k.sem("pos_split"), k.sem("picked"), k.sem("selected")
        eqs, indexed, ind_cast = k.sem("pick_eq"), k.sem("peer_indexed"), k.sem("peer_ind_cast")
        turned, stored = k.sem("sel_turned"), k.sem("sel_stored")
        norm = Norm(k, k.xT, k.mixT, rt[:], 7, KT, a2, k.mod[:, 24:32])
        k.used[k.at["out0"]], k.used[k.at["out1"]] = (out_mm, 4), (out_mm, 8)
        for i in range(4):
            k.used[k.at[f"wq{i}"]] = (q_mm, 4 * i + 4)
        block = ctx.enter_context(nc.Block())

        @block.sync
        def _(sp):
            sp.dma_start(keys[:], k.dram["keysT"]).then_inc(keys_in, 16)
            load_chunks(k, sp, k.at["wq3"])

        @block.gpsimd
        def _(pool):
            pool.iota(io16[:], pattern=[[1, TOPK]], base=0, channel_multiplier=0).then_inc(io_ready, 1)
            pool.iota(k.io_int[:], pattern=[[1, P]], base=0, channel_multiplier=0).then_inc(io_ready, 1)
            pool.wait_ge(io_ready, 2)
            pool.tensor_copy(k.iota[:], k.io_int[:]).then_inc(io_ready, 1)
            for tt in range(TT):
                pool.wait_ge(indexed, tt + 1)
                pool.tensor_copy(indf[:], ind[:]).then_inc(ind_cast, 1)
                pool.wait_ge(ind_cast, tt + 1)
                for i in range(2):
                    pool.wait_ge(eqs, 2 * tt + i + 1)
                    p4 = pick[:, i].rearrange("p (h c) a -> p h c a", h=PH)
                    pool.tensor_tensor(p4, p4, indf[:, i::2, :].unsqueeze(2).to_broadcast([P, PH, TOPK, TOPK]),
                                       ALU.mult).then_inc(picked, 1)

        @block.vector
        def _(dve):
            link = chain(dve, cdve)
            dve.scalar_tensor_tensor(a2[:], k.mod[:, 32:40], 1.0, col(k, "norm2"), ALU.add, ALU.mult)\
               .then_inc(a2_ready, 1)
            for n in range(KT):
                dve.wait_ge(out_mm, n + 1)
                dve.scalar_tensor_tensor(k.xT[:, n, :], ps[:, n % 4, :], k.mod[:, 16 + n:17 + n], k.xT[:, n, :],
                                         ALU.mult, ALU.add).then_inc(out_sb, 1)
            dve.wait_ge(out_sb, KT)
            norm.dve_scale(dve)
            dve.wait_ge(io_ready, 3)
            for tt in range(TT):
                s = s_sb[:, tt % 2]
                dve.wait_ge(s_ready, 4 * tt + 4)
                if tt:
                    dve.wait_ge(ind_cast, tt)
                for h in range(HH):
                    last = dve.max(val[:, h, 0:8], s[:, h, :])
                link(last)
                for h in range(HH):
                    dve.max_index(ind[:, h, 0:8], val[:, h, 0:8], s[:, h, :])
                    last = dve.match_replace(s_cut[:, h, :], val[:, h, 0:8], s[:, h, :], LOWEST)
                last.then_inc(s_used, 1)
                dve.wait_ge(s_used, tt + 1)
                for h in range(HH):
                    last = dve.max(val[:, h, 8:16], s_cut[:, h, :])
                link(last)
                for h in range(HH):
                    last = dve.max_index(ind[:, h, 8:16], val[:, h, 8:16], s_cut[:, h, :])
                last.then_inc(indexed, 1)
                c4 = cand[:].rearrange("p h (a b) -> p h a b", a=TOPK)
                link(dve.tensor_tensor(c4, val[:, 0::2, :].unsqueeze(3).to_broadcast([P, PH, TOPK, TOPK]),
                                       val[:, 1::2, :].unsqueeze(2).to_broadcast([P, PH, TOPK, TOPK]), ALU.add))
                for h in range(PH):
                    last = dve.max(top[:, h, 0:8], cand[:, h, :])
                link(last)
                p3 = pos[:].rearrange("p (h c) -> p h c", h=PH)
                for h in range(PH):
                    dve.max_index(p3[:, h, 0:8], top[:, h, 0:8], cand[:, h, :])
                    last = dve.match_replace(cand_cut[:, h, :], top[:, h, 0:8], cand[:, h, :], LOWEST)
                link(last)
                for h in range(PH):
                    last = dve.max(top[:, h, 8:16], cand_cut[:, h, :])
                link(last)
                for h in range(PH):
                    last = dve.max_index(p3[:, h, 8:16], top[:, h, 8:16], cand_cut[:, h, :])
                link(last)
                dve.tensor_scalar(half[:, 0, :], pos[:], 4, None, ALU.logical_shift_right).then_inc(split, 1)
                dve.tensor_scalar(half[:, 1, :], pos[:], TOPK - 1, None, ALU.bitwise_and).then_inc(split, 1)
                dve.wait_ge(split, 2 * tt + 2)
                for i in range(2):
                    dve.tensor_tensor(pick[:, i], half[:, i, :].unsqueeze(2).to_broadcast([P, PH * TOPK, TOPK]),
                                      io16[:].unsqueeze(1).to_broadcast([P, PH * TOPK, TOPK]),
                                      ALU.is_equal).then_inc(eqs, 1)
                if tt:
                    dve.wait_ge(turned, tt)
                g = sel[:, 2, :].rearrange("p (h c) -> p h c", h=PH)
                dve.tensor_tensor(g, top[:], top[:, :, 0:1].to_broadcast([P, PH, TOPK]), ALU.subtract)\
                   .then_inc(shifted, 1)
                dve.wait_ge(exped, tt + 1)
                link(dve.tensor_reduce(small[:, 0, :], g, AX.X, ALU.add))
                link(dve.reciprocal(small[:, 1, :], small[:, 0, :]))
                dve.tensor_tensor(g, g, small[:, 1, :].unsqueeze(2).to_broadcast([P, PH, TOPK]), ALU.mult)\
                   .then_inc(selected, 1)
                for i in range(2):
                    dve.wait_ge(picked, 2 * tt + i + 1)
                    dve.tensor_reduce(sel[:, i, :], pick[:, i], AX.X, ALU.add).then_inc(selected, 1)

        def finish(act, tt):
            act.wait_ge(turned, tt + 1)
            act.activation(k.selT[:, :, tt * P:(tt + 1) * P], ps[:, 4 + tt % 2, 0:3 * P].rearrange("p (i t) -> p i t", t=P),
                           ACT.Copy).then_inc(stored, 1)

        @block.scalar
        def _(act):
            act.wait_ge(out_sb, KT)
            norm.act_square(act)
            norm.act_root(act)
            act.wait_ge(a2_ready, 1)
            norm.act_affine(act)
            for n in range(HH):
                act.wait_ge(q_mm, n + 1)
                act.activation(qp[:, n, :], ps[:, n % 4, :], ACT.Copy).then_inc(q_sb, 1)
            for tt in range(TT):
                if tt >= 2:
                    act.wait_ge(s_used, tt - 1)
                for b in range(4):
                    act.wait_ge(s_mm, 4 * tt + b + 1)
                    act.activation(s_sb[:, tt % 2, 4 * b:4 * b + 4, :], ps[:, b, :].rearrange("p (h n) -> p h n", n=NKEYS),
                                   ACT.Copy).then_inc(s_ready, 1)
                if tt:
                    finish(act, tt - 1)
                act.wait_ge(shifted, tt + 1)
                act.activation(sel[:, 2, :], sel[:, 2, :], ACT.Exp).then_inc(exped, 1)
            finish(act, TT - 1)

        @block.tensor
        def _(pe):
            for n in range(KT):
                if n % 4 == 0:
                    chunk_landed(k, pe, f"out{n // 4}")
                if n >= 4:
                    pe.wait_ge(out_sb, n - 3)
                w = chunk_view(k, f"out{n // 4}")
                for t in range(KT):
                    last = pe.matmul(ps[:, n % 4, :], w[:, t, n % 4 * P:(n % 4 + 1) * P], k.mixT[:, t, :],
                                     start=t == 0, stop=t == KT - 1)
                last.then_inc(out_mm, 1)
            norm.pe_sum(pe)
            norm.wait(pe)
            for n in range(HH):
                if n % 4 == 0:
                    chunk_landed(k, pe, f"wq{n // 4}")
                if n >= 4:
                    pe.wait_ge(q_sb, n - 3)
                w = chunk_view(k, f"wq{n // 4}")
                for t in range(KT):
                    last = pe.matmul(ps[:, n % 4, :], w[:, t, n % 4 * P:(n % 4 + 1) * P], k.mixT[:, t, :],
                                     start=t == 0, stop=t == KT - 1)
                last.then_inc(q_mm, 1)
            pe.wait_ge(keys_in, 16)
            pe.wait_ge(q_sb, HH)

            def turn(tt):
                pe.wait_ge(selected, 3 * tt + 3)
                if tt >= 2:
                    pe.wait_ge(stored, tt - 1)
                for i in range(3):
                    last = pe.transpose(ps[:, 4 + tt % 2, i * P:(i + 1) * P], sel[:, i, :], k.ident[:])
                last.then_inc(turned, 1)

            for tt in range(TT):
                for b in range(4):
                    if tt:
                        pe.wait_ge(s_ready, 4 * tt - 3 + b)
                    for i in range(4):
                        h = 4 * b + i
                        last = pe.matmul(ps[:, b, i * P:(i + 1) * P], qp[:, h, tt * P:(tt + 1) * P], keys[:, h, :],
                                         start=True, stop=True)
                    last.then_inc(s_mm, 1)
                if tt:
                    turn(tt - 1)
            turn(TT - 1)



def phase_spread(k):
    nc, ps = k.nc, k.ps
    G = 16
    TB = 64
    with ExitStack() as ctx:
        def sb(name, shape, dt=F32):
            return ctx.enter_context(nc.sbuf_tensor(name, shape, dt))

        one2 = sb("one2", [P, G, P])
        one1 = sb("one1", [P, G, P])
        gs = [sb(f"gates_sb{i}", [P, NKEYS, TB]) for i in range(2)]
        built, mixed, evac = k.sem("onehots"), k.sem("gates_mm"), k.sem("gates_sb")
        wrote = [k.sem(f"gates_written{i}") for i in range(2)]
        gates = k.gates.rearrange("a b t -> b a t")
        block = ctx.enter_context(nc.Block())
        NI = TB // G

        def turns(eng, body):
            with eng.Fori(0, T // (2 * TB)) as o:
                for half in range(2):
                    with eng.Fori(0, NI) as i:
                        body(o, half, i, o * (2 * NI) + i + half * NI)

        @block.vector
        def _(dve):
            def body(o, half, i, n):
                for j in range(G):
                    if j % 4 == 0:
                        dve.wait_ge(mixed, n * 4 + (j // 4 + 1))
                    t = n * G + j
                    dve.tensor_scalar(one2[:, j, :], k.iota[:], k.selT[:, 1, bass.ds(t, 1)], None, ALU.is_equal)
                    last = dve.tensor_scalar(one1[:, j, :], k.iota[:], k.selT[:, 0, bass.ds(t, 1)],
                                             k.selT[:, 2, bass.ds(t, 1)], ALU.is_equal, ALU.mult)
                    if j % 4 == 3:
                        last.then_inc(built, 1)

            dve.sem_inc(mixed, 4)
            turns(dve, body)

        @block.tensor
        def _(pe):
            def body(o, half, i, n):
                for j in range(G):
                    if j % 4 == 0:
                        pe.wait_ge(built, n * 4 + (j // 4 + 1))
                        pe.wait_ge(evac, n * 4 + (j // 4 + 1))
                    last = pe.matmul(ps[:, j // 4, (j % 4) * P:(j % 4 + 1) * P], one2[:, j, :], one1[:, j, :],
                                     start=True, stop=True)
                    if j % 4 == 3:
                        last.then_inc(mixed, 1)

            turns(pe, body)

        @block.scalar
        def _(act):
            def body(o, half, i, n):
                for b in range(4):
                    act.wait_ge(mixed, n * 4 + (b + 5))
                    if b == 0:
                        act.wait_ge(wrote[half], 16 * (o + 1))
                    act.activation(gs[half][:].rearrange("p a t -> p t a")[:, bass.ds(i * G + 4 * b, 4), :],
                                   ps[:, b, :].rearrange("p (t a) -> p t a", a=NKEYS), ACT.Copy).then_inc(evac, 1)

            act.sem_inc(evac, 4)
            turns(act, body)

        @block.sync
        def _(sp):
            for half in range(2):
                sp.sem_inc(wrote[half], 16)
            with sp.Fori(0, T // (2 * TB)) as o:
                for half in range(2):
                    sp.wait_ge(evac, o * (8 * NI) + (4 * NI * (half + 1) + 4))
                    sp.dma_start(gates[:, :, bass.ds(o * (2 * TB) + half * TB, TB)], gs[half][:])\
                      .then_inc(wrote[half], 16)
            for half in range(2):
                sp.wait_ge(wrote[half], 16 * (T // (2 * TB) + 1))



def phase_experts(k):
    nc, ps = k.nc, k.ps
    GE = 4
    NG = NKEYS // GE
    with ExitStack() as ctx:
        def sb(name, shape, dt=F32):
            return ctx.enter_context(nc.sbuf_tensor(name, shape, dt))

        vr = sb("v_ring", [P, 2, GE, D])
        gr = sb("gates_ring", [P, 2, GE, T])
        gel = sb("gelu", [P, 2, T])
        w = sb("weighted", [P, 2, GE, T])
        acc = sb("peer_acc", [P, KT, T])
        rt = sb("e_root", [P, T])
        ur = k.ring
        u_in = [k.sem(f"u_loaded{i}") for i in range(2)]
        v_in = [k.sem(f"v_loaded{i}") for i in range(2)]
        g_in = [k.sem(f"g_loaded{i}") for i in range(2)]
        u_mm, gelud, weighted = k.sem("u_mm"), k.sem("gelud"), k.sem("weighted_ready")
        v_mm, added, zeroed, resid = k.sem("v_mm"), k.sem("acc_added"), k.sem("acc_zeroed"), k.sem("e_resid")
        uT = k.dram["uT"]
        v = k.dram["peer_v"].rearrange("(g j p) d -> g p j d", p=P, j=GE)
        gates = k.gates.rearrange("(g j) p t -> g p j t", j=GE)
        norm = Norm(k, k.xT, acc, rt[:], 7, KT, col(k, "norm_f"))
        block = ctx.enter_context(nc.Block())

        def one(ap, g):
            return ap[bass.ds(g, 1)] if not isinstance(g, int) else ap[g:g + 1]

        @block.sync
        def _(sp):
            def load(g, i, b):
                if not (isinstance(i, int) and i == 0):
                    sp.wait_ge(u_mm, i * (2 * GE) + GE * (b - 1))
                sp.dma_start(ur[:, b, :], one(uT, g).rearrange("o p n -> (o p) n")).then_inc(u_in[b], 16)
                if not (isinstance(i, int) and i == 0):
                    sp.wait_ge(weighted, i * (2 * GE) + GE * (b - 1))
                sp.dma_start(gr[:, b], one(gates, g).rearrange("o p j t -> (o p) j t")).then_inc(g_in[b], 16)
                if not (isinstance(i, int) and i == 0):
                    sp.wait_ge(v_mm, i * (2 * KT) + KT * (b - 1))
                sp.dma_start(vr[:, b], one(v, g).rearrange("o p j d -> (o p) j d")).then_inc(v_in[b], 16)

            for b in range(2):
                load(b, 0, b)
            with sp.Fori(1, NG // 2) as i:
                for b in range(2):
                    load(i * 2 + b, i, b)

        @block.tensor
        def _(pe):
            def up(i, b):
                pe.wait_ge(u_in[b], i * 16 + 16)
                for j in range(GE):
                    first = isinstance(i, int) and i == 0 and b == 0
                    if not first:
                        pe.wait_ge(gelud, i * (2 * GE) + (GE * (b - 1) + j + 1))
                    for t in range(KT):
                        last = pe.matmul(ps[:, j, :], ur[:, b, t * CHUNK + j * P:t * CHUNK + (j + 1) * P],
                                         k.mixT[:, t, :], start=t == 0, stop=t == KT - 1)
                    last.then_inc(u_mm, 1)

            def down(i, b, first=False):
                pe.wait_ge(v_in[b], i * 16 + 16)
                pe.wait_ge(weighted, i * (2 * GE) + GE * (b + 1))
                for n in range(KT):
                    if not (first and n < 4):
                        pe.wait_ge(added, i * (2 * KT) + (KT * b + n - 3))
                    for j in range(GE):
                        last = pe.matmul(ps[:, 4 + n % 4, :], vr[:, b, j, n * P:(n + 1) * P], w[:, b, j, :],
                                         start=j == 0, stop=j == GE - 1)
                    last.then_inc(v_mm, 1)

            up(0, 0)
            up(0, 1)
            down(0, 0, first=True)
            with pe.Fori(1, NG // 2) as i:
                up(i, 0)
                down(i - 1, 1)
                up(i, 1)
                down(i, 0)
            down(NG // 2 - 1, 1)
            norm.pe_sum(pe)

        @block.scalar
        def _(act):
            def gelus(i, b):
                for j in range(GE):
                    act.wait_ge(u_mm, i * (2 * GE) + (GE * b + j + 1))
                    if not (isinstance(i, int) and i == 0 and b == 0 and j < 2):
                        act.wait_ge(weighted, i * (2 * GE) + (GE * b + j - 1))
                    act.activation(gel[:, j % 2, :], ps[:, j, :], ACT.Gelu).then_inc(gelud, 1)

            for b in range(2):
                gelus(0, b)
            with act.Fori(1, NG // 2) as i:
                for b in range(2):
                    gelus(i, b)
            act.wait_ge(resid, KT)
            norm.act_square(act)
            norm.act_root(act)
            norm.act_affine(act)

        @block.vector
        def _(dve):
            def weigh(i, b):
                dve.wait_ge(g_in[b], i * 16 + 16)
                if not (isinstance(i, int) and i == 0):
                    dve.wait_ge(v_mm, i * (2 * KT) + KT * (b - 1))
                for j in range(GE):
                    dve.wait_ge(gelud, i * (2 * GE) + (GE * b + j + 1))
                    dve.tensor_tensor(w[:, b, j, :], gel[:, j % 2, :], gr[:, b, j, :], ALU.mult).then_inc(weighted, 1)

            def add(i, b):
                for n in range(KT):
                    dve.wait_ge(v_mm, i * (2 * KT) + (KT * b + n + 1))
                    dve.tensor_tensor(acc[:, n, :], acc[:, n, :], ps[:, 4 + n % 4, :], ALU.add).then_inc(added, 1)

            dve.memset(acc[:], 0.0).then_inc(zeroed, 1)
            dve.wait_ge(zeroed, 1)
            weigh(0, 0)
            weigh(0, 1)
            add(0, 0)
            with dve.Fori(1, NG // 2) as i:
                weigh(i, 0)
                add(i - 1, 1)
                weigh(i, 1)
                add(i, 0)
            add(NG // 2 - 1, 1)
            dve.wait_ge(added, NG * KT)
            for n in range(KT):
                dve.scalar_tensor_tensor(k.xT[:, n, :], acc[:, n, :], k.mod[:, 40 + n:41 + n], k.xT[:, n, :],
                                         ALU.mult, ALU.add).then_inc(resid, 1)
            dve.wait_ge(resid, KT)
            norm.dve_scale(dve)
            for n in range(KT):
                norm.wait(dve, n + 1)
                dve.tensor_copy(k.xT[:, n, :], acc[:, n, :])



class Jobs:
    NB = 4

    def __init__(self, k, name):
        self.k, self.list = k, []
        self.filled, self.by_act, self.by_dve = (k.sem(f"{name}_{x}") for x in ("filled", "by_act", "by_dve"))

    def add(self, chunk, mm, out, act=None, dve=None, after_act=False, after_dve=0, before=None):
        self.list.append(Product(chunk=chunk, mm=mm, out=out, act=act, dve=dve, after_act=after_act,
                                         after_dve=after_dve, before=before))
        self.k.used[self.k.at[chunk]] = (self.filled, len(self.list))

    def counts(self, n):
        return sum(x.act is not None for x in self.list[:n]), sum(x.dve is not None for x in self.list[:n])

    def run_pe(self, pe, first=0, last=None):
        now = None
        for j in range(first, len(self.list) if last is None else last):
            job = self.list[j]
            if job.chunk != now:
                now = job.chunk
                chunk_landed(self.k, pe, now)
            if job.before:
                job.before(pe)
            if j >= self.NB:
                a, d = self.counts(j - self.NB + 1)
                if a:
                    pe.wait_ge(self.by_act, a)
                if d:
                    pe.wait_ge(self.by_dve, d)
            out = job.out(self.k.ps[:, j % self.NB, :])
            for i, (lhs, rhs) in enumerate(job.mm):
                ins = pe.matmul(out, lhs, rhs, start=i == 0, stop=i == len(job.mm) - 1)
            ins.then_inc(self.filled, 1)

    def run_act(self, act, first=0, last=None):
        for j in range(first, len(self.list) if last is None else last):
            if self.list[j].act:
                act.wait_ge(self.filled, j + 1)
                if self.list[j].after_dve:
                    act.wait_ge(self.by_dve, self.list[j].after_dve)
                self.list[j].act(act, self.k.ps[:, j % self.NB, :]).then_inc(self.by_act, 1)

    def run_dve(self, dve, first=0, last=None):
        for j in range(first, len(self.list) if last is None else last):
            job = self.list[j]
            if job.dve:
                dve.wait_ge(self.filled, j + 1)
                if job.after_act:
                    dve.wait_ge(self.by_act, self.counts(j + 1)[0])
                job.dve(dve, self.k.ps[:, j % self.NB, :]).then_inc(self.by_dve, 1)


def copy_to(dest, scale=1.0):
    return lambda act, bank: act.activation(dest, bank[0:dest.shape[0], :], ACT.Copy, scale=scale)


NOPE, ROPE, VD = 64, 32, 64
QKD = NOPE + ROPE


def phase_project2(k):
    nc, ps = k.nc, k.ps
    hT = k.mixT
    with ExitStack() as ctx:
        def sb(name, shape, dt=F32):
            return ctx.enter_context(nc.sbuf_tensor(name, shape, dt))

        cq, cqn = sb("cq", [P, 3, T]), sb("cqn", [P, 3, T])
        ckv, ckvn = sb("ckv", [P, 2, T]), sb("ckvn", [P, 2, T])
        rt, rtq, rtkv = sb("f_root", [P, T]), sb("f_root_q", [P, T]), sb("f_root_kv", [P, T])
        sig = sb("f_sig", [P, 2, T])
        rope_x, rope_s = sb("rope_x", [P, 2, T]), sb("rope_s", [P, 2, T])
        k_pe = sb("k_pe", [P, T])
        a3 = sb("f_gain", [P, 8])
        k.rope_cols = sb("rope_cols", [P, 2])
        k.sinT, k.cosT = sb("sinT", [P, T]), sb("cosT", [P, T])
        pos_i, turns = rope_x[:, 0, :].bitcast(I32), rope_s[:, 0, :]
        rope_in, angles, sines = k.sem("rope_loaded"), k.sem("rope_angles"), k.sem("rope_sines")
        fdve = k.sem("f_dve_chain")
        gain, rope_b = k.sem("f_gain_ready"), k.sem("rope_sin")
        norm = Norm(k, k.xT, hT, rt[:], 7, KT, a3, k.ada[:, 0:8])
        norm_q = Norm(k, cq, cqn, rtq[:], 6, 3, col(k, "q_norm_gain_2"))
        norm_kv = Norm(k, ckv, ckvn, rtkv[:], 5, 2, col(k, "kv_norm_gain_2"))
        jobs = Jobs(k, "proj2")
        R = slice(NOPE, QKD)
        whole = lambda bank: bank
        n_rope, n_silu = [0], [0]

        def feature(chunk, a, m, out=whole, src=hT, **kw):
            w = chunk_view(k, chunk)
            jobs.add(chunk, [(w[:, t, a:a + m], src[:, t, :]) for t in range(w.shape[1])],
                     lambda bank: out(bank)[0:m] if out is whole else out(bank), **kw)

        def token(chunk, tile, dest, src=hT, cols=None, **kw):
            w = chunk_view(k, chunk)
            cols = cols or (lambda x: x)
            jobs.add(chunk, [(src[:, t, tile * P:(tile + 1) * P], cols(w[:, t, :])) for t in range(w.shape[1])],
                     whole, act=copy_to(dest), **kw)

        def silu(chunk, a, dest):
            n_silu[0] += 1
            slot = n_silu[0] % 2
            feature(chunk, a, P, after_act=True, after_dve=jobs.counts(len(jobs.list) - 1)[1] if n_silu[0] > 2 else 0,
                    act=lambda act, bank: act.activation(sig[:, slot, :], bank, ACT.Sigmoid),
                    dve=lambda dve, bank: dve.tensor_tensor(dest, bank, sig[:, slot, :], ALU.mult))

        def rope(chunk, a, dest, act=None, swap=None, src=hT, width=ROPE, done=None):
            n_rope[0] += 1
            n, slot = n_rope[0], n_rope[0] % 2

            def first(dve, bank):
                return dve.tensor_tensor(rope_x[R, slot, :], bank[R], k.cosT[R], ALU.mult)

            def second(dve, bank):
                dve.tensor_tensor(rope_s[R, slot, :], bank[R], k.sinT[R], ALU.mult).then_inc(rope_b, 1)
                dve.wait_ge(rope_b, n)
                return dve.tensor_tensor(dest, rope_x[R, slot, :], rope_s[R, slot, :], ALU.add)

            if width == ROPE:
                feature(chunk, a, ROPE, out=lambda bank: bank[R], src=src, dve=first)
            else:
                feature(chunk, a, width, src=src, act=act, dve=first)
            feature(chunk, swap, ROPE, out=lambda bank: bank[R], src=src, dve=second)

        for i in range(3):
            feature("cq", i * P, P, act=copy_to(cq[:, i, :]))
        cq_done = len(jobs.list)
        for i in range(2):
            feature("kvr", i * P, P, act=copy_to(ckv[:, i, :]))
        ckv_done = len(jobs.list)
        rope("kvr", 256, k_pe[R], swap=256 + ROPE)
        kpe_job = len(jobs.list)
        for i in range(4):
            feature("sq", i * P, P, act=copy_to(k.sq[:, i, :], DH ** -0.5))
        for i in range(4):
            feature("sk", i * P, P, act=copy_to(k.sk[:, i, :]))
        for i in range(4):
            token("sv", i, k.sv[:, i, :])
        for i in range(4):
            silu("sz", i * P, k.sz[:, i, :])
        for i in range(4):
            silu("mz", i * P, k.mz[:, i, :])
        late = len(jobs.list)
        for h in range(NH):
            rope("uq", h * QKD, k.mq[R, h, :], act=copy_to(k.mq[0:NOPE, h, :]), swap=NH * QKD + h * ROPE,
                 src=cqn, width=QKD)
        for h in range(NH):
            feature("ukv", h * (NOPE + VD), NOPE, src=ckvn, act=copy_to(k.mk[0:NOPE, h, :]))
        for i in range(4):
            token("ukv", i, k.mv[:, i, :], src=ckvn,
                  cols=lambda w: w.rearrange("p (h x) -> p h x", h=NH)[:, :, NOPE:NOPE + VD])
        block = ctx.enter_context(nc.Block())

        def rope_angles(dve, link):
            R = slice(NOPE, QKD)
            a, b, c = turns[R], k.sinT[R], k.cosT[R]
            dve.wait_ge(rope_in, 32)
            link(dve.tensor_copy(b, pos_i[R]))
            link(dve.tensor_scalar(b, b, k.rope_cols[R, 0:1], None, ALU.mult))
            link(dve.tensor_scalar(a, b, 1.0 / (2 * np.pi), None, ALU.mult))
            link(dve.tensor_scalar(a, a, 12582912.0, 12582912.0, ALU.add, ALU.subtract))
            for part in TWO_PI:
                link(dve.scalar_tensor_tensor(b, a, -part, b, ALU.mult, ALU.add))
            link(dve.tensor_scalar(c, b, np.pi / 2, None, ALU.add))
            link(dve.tensor_scalar(a, c, PI_DOWN, -2 * np.pi, ALU.is_gt, ALU.mult))
            link(dve.tensor_tensor(c, c, a, ALU.add))
            dve.tensor_scalar(b, b, PI_DOWN, -PI_DOWN, ALU.min, ALU.max).then_inc(angles, 1)
            dve.tensor_scalar(c, c, PI_DOWN, -PI_DOWN, ALU.min, ALU.max).then_inc(angles, 1)
            dve.wait_ge(sines, 2)
            link(dve.tensor_scalar(b, b, k.rope_cols[R, 1:2], None, ALU.mult))

        @block.sync
        def _(sp):
            R = slice(NOPE, QKD)
            sp.dma_start(pos_i[R], k.dram["positions"].to_broadcast([ROPE, T])).then_inc(rope_in, 16)
            sp.dma_start(k.rope_cols[R], k.dram["rope_cols"]).then_inc(rope_in, 16)
            load_chunks(k, sp, k.at["ukv"] + SLOTS)

        @block.gpsimd
        def _(pool):
            pool.wait_ge(jobs.by_dve, jobs.counts(kpe_job)[1])
            pool.tensor_copy(k.mk[R], k_pe[R].unsqueeze(1).to_broadcast([ROPE, NH, T]))

        @block.vector
        def _(dve):
            dve.scalar_tensor_tensor(a3[:], k.ada[:, 8:16], 1.0, col(k, "norm_gain_2"), ALU.add, ALU.mult)\
               .then_inc(gain, 1)
            rope_angles(dve, chain(dve, fdve))
            norm.dve_scale(dve)
            jobs.run_dve(dve, 0, kpe_job)
            norm_q.dve_scale(dve)
            norm_kv.dve_scale(dve)
            jobs.run_dve(dve, kpe_job)

        @block.scalar
        def _(act):
            norm.act_square(act)
            R = slice(NOPE, QKD)
            act.wait_ge(angles, 2)
            act.activation(k.sinT[R], k.sinT[R], ACT.Sin).then_inc(sines, 1)
            act.activation(k.cosT[R], k.cosT[R], ACT.Sin).then_inc(sines, 1)
            norm.act_root(act)
            act.wait_ge(gain, 1)
            norm.act_affine(act)
            jobs.run_act(act, 0, ckv_done)
            act.wait_ge(jobs.by_act, ckv_done)
            norm_q.act_square(act)
            norm_kv.act_square(act)
            norm_q.act_root(act)
            norm_kv.act_root(act)
            norm_q.act_affine(act)
            norm_kv.act_affine(act)
            jobs.run_act(act, ckv_done)

        @block.tensor
        def _(pe):
            norm.pe_sum(pe)
            norm.wait(pe)
            jobs.run_pe(pe, 0, kpe_job)
            norm_q.pe_sum(pe)
            norm_kv.pe_sum(pe)
            jobs.run_pe(pe, kpe_job, late)
            norm_q.wait(pe)
            norm_kv.wait(pe)
            jobs.run_pe(pe, late)


def phase_attend2(k):
    nc, ps = k.nc, k.ps
    TT = T // P
    items = [(kind, h, i) for kind in ("stick", "soft") for h in range(NH) for i in range(TT)]
    N = len(items)
    NHD = 2 * NH
    with ExitStack() as ctx:
        def sb(name, shape, dt=F32):
            return ctx.enter_context(nc.sbuf_tensor(name, shape, dt))

        w = sb("at_w", [P, 3, T])
        rest = sb("at_rest", [P, 3, T])
        prod = sb("at_prod", [P, 3, T])
        pT = sb("at_wT", [P, 2, TT, T])
        nmax, sums = sb("at_nmax", [P, N]), sb("at_sums", [P, N, 2])
        cmask = sb("causal_mask", [P, 2, P])
        made = k.sem("causal_masks")
        scored, masked, acted = k.sem("at_scored"), k.sem("at_masked"), k.sem("at_acted")
        cdve, ready = k.sem("at_dve_chain"), k.sem("at_ready")
        turned, turned_sb, summed, stored = (k.sem("at_turned"), k.sem("at_turned_sb"), k.sem("at_summed"),
                                             k.sem("at_stored"))
        block = ctx.enter_context(nc.Block())

        def width(n):
            return (items[n][2] + 1) * P

        @block.gpsimd
        def _(pool):
            for j, base in enumerate((0, 1)):
                pool.affine_select(out=cmask[:, j, :], in_=k.zeros[:, 0:P], compare_op=ALU.is_gt, fill=NEG,
                                   base=base, pattern=[[-1, P]], channel_multiplier=1).then_inc(made, 1)

        @block.tensor
        def _(pe):
            def scores(n):
                kind, h, i = items[n]
                if n >= 4:
                    pe.wait_ge(acted, n - 3)
                if kind == "stick":
                    a, hp = DH * (h % 2), h // 2
                    q, key = k.sq[a:a + DH, hp], k.sk[a:a + DH, hp]
                else:
                    q, key = k.mq[0:QKD, h], k.mk[0:QKD, h]
                pe.matmul(ps[:, n % 4, 0:width(n)], q[:, i * P:(i + 1) * P], key[:, 0:width(n)], start=True,
                          stop=True).then_inc(scored, 1)

            def turn(n):
                kind, h, i = items[n]
                pe.wait_ge(ready, n + 1)
                if n >= 2:
                    pe.wait_ge(turned_sb, n - 1)
                for j in range(i + 1):
                    last = pe.transpose(ps[:, 4 + n % 2, j * P:(j + 1) * P], w[:, n % 3, j * P:(j + 1) * P], k.ident[:])
                last.then_inc(turned, 1)

            def values(m):
                h, v = m % NH, (k.sv if m < NH else k.mv)
                pe.wait_ge(turned_sb, TT * (m + 1))
                if m % 2 == 0 and m >= 4:
                    pe.wait_ge(stored, m // 2 - 1)
                a = DH * (h % 2)
                for j in range(TT):
                    last = pe.matmul(ps[a:a + DH, 6 + m // 2 % 2, j * P:T], v[:, j, h * DH:(h + 1) * DH],
                                     pT[:, m % 2, j, j * P:T], start=j == 0, stop=j == TT - 1)
                last.then_inc(summed, 1)

            for n in range(N + 4):
                if n < N:
                    scores(n)
                if 0 <= n - 2 < N:
                    turn(n - 2)
                if n - 3 >= 0 and (n - 3) % TT == TT - 1:
                    values((n - 3) // TT)

        def store(dve, pair):
            dve.wait_ge(summed, 2 * pair + 2)
            z = (k.sz if pair < NH // 2 else k.mz)[:, pair % (NH // 2), :]
            dve.tensor_tensor(z, z, ps[:, 6 + pair % 2, :], ALU.mult).then_inc(stored, 1)

        @block.vector
        def _(dve):
            link = chain(dve, cdve)
            dve.wait_ge(made, 2)
            for n in range(N + 1):
                if n < N:
                    kind, h, i = items[n]
                    W = width(n)
                    dve.wait_ge(scored, n + 1)
                    diag = ps[:, n % 4, W - P:W]
                    if kind == "stick":
                        dve.tensor_tensor(diag, diag, cmask[:, 0, :], ALU.add).then_inc(masked, 1)
                    else:
                        link(dve.tensor_tensor(diag, diag, cmask[:, 1, :], ALU.add))
                        link(dve.tensor_reduce(nmax[:, n:n + 1], ps[:, n % 4, 0:W], AX.X, ALU.max, negate=True))
                        dve.tensor_scalar(nmax[:, n:n + 1], nmax[:, n:n + 1], QKD ** -0.5, None, ALU.mult)\
                           .then_inc(masked, 1)
                if n >= 1:
                    m = n - 1
                    kind, h, i = items[m]
                    W, s = width(m), m % 3
                    if kind == "stick":
                        link(dve.memset(prod[:, s, W - 1:W], 1.0))
                        dve.wait_ge(acted, m + 1)
                        link(dve.tensor_tensor_scan(out=prod[:, s, W - 2::-1], data0=rest[:, s, W - 1:0:-1],
                                                    data1=k.zeros[:, 0:W - 1], initial=1.0, op0=ALU.mult,
                                                    op1=ALU.add))
                        dve.tensor_tensor(w[:, s, 0:W], w[:, s, 0:W], prod[:, s, 0:W], ALU.mult).then_inc(ready, 1)
                    else:
                        dve.wait_ge(acted, m + 1)
                        link(dve.reciprocal(sums[:, m, 1:2], sums[:, m, 0:1]))
                        dve.tensor_scalar(w[:, s, 0:W], w[:, s, 0:W], sums[:, m, 1:2], None, ALU.mult)\
                           .then_inc(ready, 1)
                if n >= 2 * TT + 3 and (n - 3) % (2 * TT) == 0:
                    store(dve, (n - 3) // (2 * TT) - 1)
            store(dve, NH - 1)

        @block.scalar
        def _(act):
            for n in range(N + 2):
                if n < N:
                    kind, h, i = items[n]
                    W, s = width(n), n % 3
                    act.wait_ge(masked, n + 1)
                    if n >= 3:
                        act.wait_ge(turned, n - 2)
                    if kind == "stick":
                        act.activation(w[:, s, 0:W], ps[:, n % 4, 0:W], ACT.Sigmoid)
                        act.activation(rest[:, s, 0:W], ps[:, n % 4, 0:W], ACT.Sigmoid, scale=-1.0).then_inc(acted, 1)
                    else:
                        act.activation(w[:, s, 0:W], ps[:, n % 4, 0:W], ACT.Exp, scale=QKD ** -0.5,
                                       bias=nmax[:, n:n + 1], accum_out=sums[:, n, 0:1]).then_inc(acted, 1)
                if 0 <= n - 2 < N:
                    m = n - 2
                    kind, h, i = items[m]
                    head = m // TT
                    act.wait_ge(turned, m + 1)
                    if head >= 2:
                        act.wait_ge(summed, head - 1)
                    act.activation(pT[:, head % 2, 0:i + 1, i * P:(i + 1) * P],
                                   ps[:, 4 + m % 2, 0:(i + 1) * P].rearrange("p (j t) -> p j t", t=P),
                                   ACT.Copy).then_inc(turned_sb, 1)


def phase_merge2(k):
    nc, ps = k.nc, k.ps
    hT = k.mixT
    with ExitStack() as ctx:
        def sb(name, shape, dt=F32):
            return ctx.enter_context(nc.sbuf_tensor(name, shape, dt))

        sg, merged = sb("gates2", [P, KT, T]), sb("merged", [P, KT, T])
        rt = sb("h_root", [P, T])
        weighed, stored = k.sem("b_weighed"), k.sem("out_stored")
        norm = Norm(k, k.xT, k.mixT, rt[:], 7, KT, col(k, "final_norm_gain_2"))
        jobs = Jobs(k, "merge")

        def feature(chunk, a, src, **kw):
            w = chunk_view(k, chunk)
            jobs.add(chunk, [(w[:, t, a:a + P], src[:, t, :]) for t in range(w.shape[1])], lambda bank: bank, **kw)

        def gate_of(n, branch):
            c, a = divmod(n, 4)
            before_act = (lambda act: act.wait_ge(jobs.by_dve, n + 1)) if branch else None

            def run(act, bank):
                if before_act:
                    before_act(act)
                return act.activation(sg[:, n, :], bank, ACT.Sigmoid)

            feature(f"g{'ab'[branch]}{c}", a * P, hT, act=run)

        def first(n):
            feature("bra", n * P, k.sz, after_act=True,
                    dve=lambda dve, bank: dve.tensor_tensor(merged[:, n, :], bank, sg[:, n, :], ALU.mult))

        def second(n):
            def run(dve, bank):
                dve.tensor_tensor(sg[:, n, :], bank, sg[:, n, :], ALU.mult).then_inc(weighed, 1)
                dve.wait_ge(weighed, n + 1)
                return dve.tensor_tensor(merged[:, n, :], merged[:, n, :], sg[:, n, :], ALU.add)

            feature("brb", n * P, k.mz, after_act=True, dve=run)

        for branch, rest in enumerate((first, second)):
            for n in range(KT):
                gate_of(n, branch)
            for n in range(KT):
                rest(n)
        n_merge = len(jobs.list)
        for n in range(KT):
            feature(f"wo{n // 4}", n % 4 * P, merged,
                    before=(lambda pe: pe.wait_ge(jobs.by_dve, 2 * KT)) if n == 0 else None,
                    dve=lambda dve, bank, n=n: dve.scalar_tensor_tensor(
                        k.xT[:, n, :], bank, k.ada[:, 16 + n:17 + n], k.xT[:, n, :], ALU.mult, ALU.add))
        block = ctx.enter_context(nc.Block())

        @block.sync
        def _(sp):
            load_chunks(k, sp, k.at["wo1"])
            o = k.out.rearrange("(k p) t -> p k t", p=P)
            for n in range(0, KT, 2):
                norm.wait(sp, n + 2)
                sp.dma_start(o[:, n:n + 2, :], k.mixT[:, n:n + 2, :]).then_inc(stored, 16)
            sp.wait_ge(stored, 16 * (KT // 2))

        @block.vector
        def _(dve):
            jobs.run_dve(dve)
            dve.wait_ge(jobs.by_dve, 3 * KT)
            norm.dve_scale(dve)

        @block.scalar
        def _(act):
            jobs.run_act(act)
            act.wait_ge(jobs.by_dve, 3 * KT)
            norm.act_square(act)
            norm.act_root(act)
            norm.act_affine(act)

        @block.tensor
        def _(pe):
            jobs.run_pe(pe)
            norm.pe_sum(pe)


def second_block(k, sb):
    with ExitStack() as outs:
        k.sz, k.mz = sb("sz", [P, 4, T], where=outs), sb("mz", [P, 4, T], where=outs)
        with ExitStack() as qkv:
            k.sq, k.sk, k.sv = (sb(n, [P, 4, T], where=qkv) for n in ("sq", "sk", "sv"))
            k.mq, k.mk = (sb(n, [P, NH, T], where=qkv) for n in ("mq", "mk"))
            k.mv = sb("mv", [P, 4, T], where=qkv)
            phase_project2(k)
            phase_attend2(k)
        phase_merge2(k)


def build(nc, dram, out):
    with ExitStack() as ctx:
        k = Kernel(nc=nc, dram=dram, out=out)

        def sem(name, n=None):
            if n is None:
                return ctx.enter_context(nc.semaphore(name))
            return [ctx.enter_context(nc.semaphore(f"{name}{i}")) for i in range(n)]

        def sb(name, shape, dt=F32, where=ctx):
            return where.enter_context(nc.sbuf_tensor(name, shape, dt))

        k.sem = sem
        k.norm_sems = [sem(f"norm_{x}") for x in ("squared", "summed", "mean", "rooted", "inverse", "scaled", "done")]
        k.norms, k.norm_tiles = 0, 0
        k.ps = ctx.enter_context(nc.psum_tensor("ps", [P, 8, 512], F32))
        k.xT = sb("xT", [P, KT, T])
        k.mixT = sb("mixT", [P, KT, T])
        k.ring = sb("ring", [P, SLOTS, KT * CHUNK])
        k.cols = sb("cols", [P, NCOL])
        k.ones = sb("ones", [P, P])
        k.zeros = sb("zeros", [P, T])

        k.ident = sb("ident", [P, P])
        k.mod = sb("mod", [P, 48])
        k.ada = sb("ada", [P, 24])
        k.ring_full = sem("ring_full", SLOTS)
        plan_stream(k)
        with ExitStack() as hg:
            k.hq = sb("hq", [P, HG, T], where=hg)
            k.fx = [sb(f"fx{d}", [P, HG, T], where=hg) for d in range(2)]
            k.fc = [sb(f"fc{d}", [P, HG, C], where=hg) for d in range(2)]
            k.hgate = sb("hgate", [P, HG, T], where=hg)
            k.ix = sb("ix", [P, 4, 512], where=hg)
            k.ic = sb("ic", [P, 2, 512], where=hg)
            with ExitStack() as na:
                k.qT = sb("qT", [P, 4, T], where=na)
                k.kT = sb("kT", [P, 4, T + C], where=na)
                k.vw = sb("vw", [P, 8, 512], where=na)
                k.vc = sb("vc", [P, 2, 512], where=na)
                phase_project(k)
                phase_neighbourhood(k)
            phase_hgrn(k)
        k.gates = nc.dram_tensor("gates", [NKEYS, NKEYS, T], F32, kind="Internal").ap()
        with ExitStack() as peer:
            k.selT = sb("selT", [P, 3, T], where=peer)
            k.io_int = sb("io_int", [P, P], I32, where=peer)
            k.iota = sb("iota", [P, P], where=peer)
            phase_route(k)
            phase_spread(k)
        phase_experts(k)
        second_block(k, sb)


def lay_out(inputs):
    f = {n: np.asarray(a) for n, a in inputs.items()}

    def columns(v):
        return np.ascontiguousarray(v.reshape(-1, P).T)

    a = {"xT": f["x"][0].T, "ctxT": f["ctx"][0].T}
    a["cols"] = np.concatenate([columns(f[name]) for name, _ in _COLS], axis=1)
    for name in ("w_mod", "w_in", "w_out", "peer_wq"):
        a[name] = f[name][0]
    padded = np.pad(f["na_rpb"][0].transpose(1, 0, 2), ((0, 0), (0, 0), (QB, QB)))
    a["rpb_shifted"] = np.stack([padded[:, :, QB - 1 - q:QB - 1 - q + KB + QB] for q in range(QB)])
    q, key = np.arange(P)[:, None] % QB, np.arange(KB)[None, :]
    a["win_mask"] = np.stack([np.where((key >= first) & (key < first + KB // 2), 0.0, NEG).astype(np.float32)
                              for first in (np.maximum(q - 8, 0), q, np.minimum(q + 8, 16))], axis=1)
    t, s = np.arange(P)[None, :], np.arange(P)[:, None]
    pred = np.stack([(t >> lv) == (s >> lv) + 1 for lv in range(7)]) \
        & np.stack([(t >> lv + 1) == (s >> lv + 1) for lv in range(7)])
    a["pred"] = np.stack([pred, pred.transpose(0, 2, 1)]).transpose(2, 0, 1, 3).astype(np.float32)
    a["keysT"] = f["peer_keys"][0].transpose(3, 0, 1, 2).reshape(P, 2 * PH, NKEYS)
    a["uT"] = f["peer_u"][0].reshape(-1, CHUNK, KT, P).transpose(0, 3, 2, 1).reshape(-1, P, KT * CHUNK)
    a["peer_v"] = f["peer_v"][0]
    for name in ("w_ada_2", "w_in_2", "w_ukv_2", "w_branch_a_2", "w_branch_b_2", "w_out_2"):
        a[name] = f[name][0]
    def swapped(w):
        h = w.reshape(w.shape[0], -1, 2, ROPE // 2)
        return h[:, :, ::-1].reshape(w.shape)

    kv = f["w_in_2"][0][:, 2432:2720]
    a["w_kvr_2"] = np.concatenate([kv, swapped(kv[:, 256:])], axis=1)
    uq = f["w_uq_2"][0]
    rot = uq.reshape(-1, NH, QKD)[:, :, NOPE:].reshape(uq.shape[0], NH * ROPE)
    a["w_uq_2"] = np.concatenate([uq, swapped(rot)], axis=1)
    a["positions"] = f["positions_2"]
    i = np.arange(ROPE)
    a["rope_cols"] = np.stack([10000.0 ** (-(2 * (i % (ROPE // 2))) / ROPE), np.where(i < ROPE // 2, -1.0, 1.0)],
                              axis=1).astype(np.float32)
    return {n: np.ascontiguousarray(v) for n, v in a.items()}


def kernel(**inputs):
    import concourse.bacc as bacc
    from concourse.bass_utils import run_bass_kernel_spmd

    nc = bacc.Bacc("TRN2", target_bir_lowering=False, num_devices=1)
    arrays = {f"in_{name}": a for name, a in lay_out(inputs).items()}
    dram = {name[3:]: nc.dram_tensor(name, a.shape, mybir.dt.from_np(a.dtype), kind="ExternalInput").ap()
            for name, a in arrays.items()}
    out = nc.dram_tensor("out_T", (D, T), F32, kind="ExternalOutput").ap()
    build(nc, dram, out)
    result = run_bass_kernel_spmd(nc, [arrays], core_ids=[0])
    return np.ascontiguousarray(result.results[0]["out_T"].T).reshape(1, T, D)
```

```python
from contextlib import ExitStack

import numpy as np
import concourse.bass as bass
from concourse import mybir

F32 = mybir.dt.float32
F32R = mybir.dt.float32r
U32 = mybir.dt.uint32
I32 = mybir.dt.int32
ALU = mybir.AluOpType
ACT = mybir.ActivationFunctionType
AX = mybir.AxisListType

P = 128
D = 1024
T = 512
C = 256
KT = D // P
NH, DH = 8, 64
ROWS, GW = 8, 64
NCB, QB, KB = 4, 16, 32
HG = 4
EPS = 1e-6
NEG = -1e30
LOWEST = -3e38
NKEYS, TOPK, PH = 128, 16, 8
CHUNK = 512
SLOTS = 2
EXPERT_TILES = 2
TOKEN_BLOCK = 64

TWO_PI = (6.28125, 0.0019350051879882812, 3.0199159819602908e-07)
PI_DOWN = float(np.nextafter(np.float32(np.pi), np.float32(0)))

_COLS = [("c", 8), ("c_ctx", 8), ("c_2", 8), ("b_mod", 48), ("norm1", 8), ("norm2", 8), ("norm_f", 8),
         ("b_ada_2", 24), ("norm_gain_2", 8), ("q_norm_gain_2", 3), ("kv_norm_gain_2", 2),
         ("final_norm_gain_2", 8), ("hg_norm", 4), ("hg_lb", 16)]
COL = {}
_n = 0
for _name, _count in _COLS:
    COL[_name] = (_n, _count)
    _n += _count
NCOL = _n


def col(k, name, a=0, b=None):
    start, count = COL[name]
    return k.cols[:, start + a:start + (count if b is None else b)]


class Kernel:
    def __init__(self, nc, dram, out):
        self.nc, self.dram, self.out = nc, dram, out


class Product:
    def __init__(self, chunk, mm, kind=None, dest=None, N=None, out=None, act=None, dve=None, after_act=False,
                 after_dve=0, before=None):
        self.chunk, self.mm, self.kind, self.dest, self.N, self.out = chunk, mm, kind, dest, N, out
        self.act, self.dve, self.after_act, self.after_dve, self.before = act, dve, after_act, after_dve, before


def chain(eng, sem, start=0):
    state = [start]

    def link(ins):
        state[0] += 1
        ins.then_inc(sem, 1)
        eng.wait_ge(sem, state[0])
        return state[0]

    link.state = state
    return link



def plan_stream(k):
    d = k.dram

    def cols_of(w, a, n):
        return w.rearrange("(k p) n -> p k n", p=P)[:, :, a:a + n]

    s = []
    for i in range(4):
        s.append((f"mod{i}", cols_of(d["w_mod"], i * CHUNK, CHUNK)))
    for i in range(8):
        s.append((f"in{i}", cols_of(d["w_in"], i * CHUNK, CHUNK)))
    for i in range(4, 10):
        s.append((f"mod{i}", cols_of(d["w_mod"], i * CHUNK, CHUNK)))
    for i in range(2):
        s.append((f"out{i}", cols_of(d["w_out"], i * CHUNK, CHUNK)))
    for i in range(4):
        s.append((f"wq{i}", cols_of(d["peer_wq"], i * CHUNK, CHUNK)))
    for i in range(10, 12):
        s.append((f"mod{i}", cols_of(d["w_mod"], i * CHUNK, CHUNK)))
    for i in range(6):
        s.append((f"ada{i}", cols_of(d["w_ada_2"], i * CHUNK, CHUNK)))
    for name, a, n in (("cq", 2048, 384), ("kvr", None, 320), ("sq", 0, 512), ("sk", 512, 512), ("sv", 1024, 512),
                       ("sz", 1536, 512), ("mz", 2720, 512)):
        s.append((name, cols_of(d["w_in_2"], a, n) if a is not None else cols_of(d["w_kvr_2"], 0, n)))
    s.append(("uq", cols_of(d["w_uq_2"], 0, 1024)))
    s.append(("ukv", cols_of(d["w_ukv_2"], 0, 1024)))
    for x, a in (("a", 3232), ("b", 4256)):
        for i in range(2):
            s.append((f"g{x}{i}", cols_of(d["w_in_2"], a + i * CHUNK, CHUNK)))
        s.append((f"br{x}", cols_of(d[f"w_branch_{x}_2"], 0, D)))
    for i in range(2):
        s.append((f"wo{i}", cols_of(d["w_out_2"], i * CHUNK, CHUNK)))
    k.stream = s
    k.at = {name: i for i, (name, _) in enumerate(s)}
    k.used = {}
    k.issued = 0


def chunk_view(k, name):
    i = k.at[name]
    _, kt, n = k.stream[i][1].shape
    return k.ring[:, i % SLOTS, 0:kt * n].rearrange("p (k n) -> p k n", k=kt)


def chunk_landed(k, eng, name):
    i = k.at[name]
    eng.wait_ge(k.ring_full[i % SLOTS], 16 * (i // SLOTS + 1))


def load_chunks(k, eng, last):
    while k.issued <= min(last, len(k.stream) - 1):
        i = k.issued
        if i >= SLOTS:
            sem, value = k.used[i - SLOTS]
            eng.wait_ge(sem, value)
        eng.dma_start(chunk_view(k, k.stream[i][0]), k.stream[i][1]).then_inc(k.ring_full[i % SLOTS], 16)
        k.issued += 1



def modulation(k, pe, name, rhs, at, width, tiles=range(4)):
    if 0 in tiles:
        chunk_landed(k, pe, name)
    w = chunk_view(k, name)
    for n in tiles:
        for t in range(KT):
            last = pe.matmul(k.ps[:, 7, at + width * n:at + width * (n + 1)], w[:, t, n * P:(n + 1) * P],
                             rhs[:, t, :], start=t == 0, stop=t == KT - 1)
    if 3 in tiles:
        last.then_inc(k.mod_done, 1)


def phase_project(k):
    nc, ps = k.nc, k.ps
    with ExitStack() as ctx:
        def sb(name, shape, dt=F32):
            return ctx.enter_context(nc.sbuf_tensor(name, shape, dt))

        ctxT = sb("ctxT", [P, KT, C])
        hcT = sb("hcT", [P, KT, C])
        vnat = sb("vnat", [P, 4, 512])
        rx = sb("rx", [P, T])
        rc = sb("rc", [P, C])
        sig = sb("sig", [P, 2, 512])
        sc = k.sc
        sgc = sb("sgc", [P, 24])
        m1 = sb("m1", [P, 16, 2])
        a1 = sb("a1", [P, 8, 2])
        lbt = sb("lbt", [P, 4, 8])
        hT = k.mixT
        load_x, load_c, load_cols = k.sem("load_x", 2), k.sem("load_ctx"), k.sem("load_cols")
        consts, ones_ready = k.sem("consts_ready"), k.sem("ones_ready")
        squared = k.sem("squared")
        summed = k.sem("a_summed")
        silu_c = k.sem("silu_c")
        sg_c = k.sem("sigmoid_c")
        mod_done = k.mod_done = k.sem("mod_done")
        root_in, root_out = k.sem("a_root_in"), k.sem("a_root_out")
        scaled, modulated, affine = k.sem("h_scaled"), k.sem("h_modulated"), k.sem("mod_affine")
        proj, evac, gated = k.sem("proj_done"), k.sem("proj_evac"), k.sem("proj_gated")
        lbs, lb_exp = k.sem("lb_in"), k.sem("lb_exp")
        moved = k.sem("v_moved")
        dve_chain = k.sem("a_dve_chain")

        jobs = []

        def feature_job(chunk, n, tokens, kind, dest):
            w = chunk_view(k, chunk)
            src, N = (hT, T) if tokens == "x" else (hcT, C)
            jobs.append(Product(chunk=chunk, kind=kind, dest=dest, N=N, mm=[
                (w[:, t, n * P:(n + 1) * P], src[:, t, :]) for t in range(KT)]))

        def token_job(chunk, tile, tokens, dest):
            w = chunk_view(k, chunk)
            src = hT if tokens == "x" else hcT
            jobs.append(Product(chunk=chunk, kind="copy", dest=dest, N=512, mm=[
                (src[:, t, tile * P:(tile + 1) * P], w[:, t, :]) for t in range(KT)]))

        for n in range(4):
            feature_job("in0", n, "x", "query", k.qT[:, n, :])
        for n in range(4):
            feature_job("in1", n, "x", "copy", k.kT[:, n, 0:T])
            feature_job("in1", n, "ctx", "copy", k.kT[:, n, T:T + C])
        for t in range(4):
            token_job("in2", t, "x", vnat[:, t, :])
        v_last = len(jobs)
        for t in range(2):
            token_job("in2", t, "ctx", k.vc[:, t, :])
        for n in range(4):
            feature_job("in3", n, "x", "silu", k.hq[:, n, :])
        for d in range(2):
            for n in range(4):
                feature_job(f"in{4 + d}", n, "x", "sigmoid", k.fx[d][:, n, :])
                feature_job(f"in{4 + d}", n, "ctx", "sigmoid", k.fc[d][:, n, :])
        f_last = len(jobs)
        for t in range(4):
            token_job("in6", t, "x", k.ix[:, t, :])
        for t in range(2):
            token_job("in6", t, "ctx", k.ic[:, t, :])
        for n in range(4):
            feature_job("in7", n, "x", "silu", k.hgate[:, n, :])
        NB = 5
        silu_before = [sum(x.kind == "silu" for x in jobs[:j + 1]) for j in range(len(jobs))]
        for j, job in enumerate(jobs):
            k.used[k.at[job.chunk]] = (proj, j + 1)
        n_mod = 0
        mods = [f"mod{i}" for i in range(4)] + [f"mod{i}" for i in range(4, 12)] + [f"ada{i}" for i in range(6)]
        for name in mods:
            n_mod += 1
            k.used[k.at[name]] = (mod_done, n_mod)

        block = ctx.enter_context(nc.Block())

        @block.sync
        def _(sp):
            sp.dma_start(k.cols[:], k.dram["cols"]).then_inc(load_cols, 16)
            xv = k.dram["xT"].rearrange("(k p) t -> p k t", p=P)
            for h in range(2):
                sp.dma_start(k.xT[:, 4 * h:4 * h + 4, :], xv[:, 4 * h:4 * h + 4, :]).then_inc(load_x[h], 16)
            sp.dma_start(ctxT[:], k.dram["ctxT"].rearrange("(k p) t -> p k t", p=P)).then_inc(load_c, 16)
            load_chunks(k, sp, k.at["in2"] + 1)
            sp.wait_ge(evac, v_last)
            for c in range(NCB):
                k0 = min(max(QB * c - KB // 4, 0), GW - KB)
                for r in range(ROWS):
                    sp.dma_start(k.vw[KB * (r % 4):KB * (r % 4) + KB, 2 * c + r // 4, :],
                                 vnat[GW * (r % 2) + k0:GW * (r % 2) + k0 + KB, r // 2, :]).then_inc(moved, 16)
            load_chunks(k, sp, k.at["in7"] + SLOTS)
            sp.wait_ge(moved, 16 * NCB * ROWS)

        @block.gpsimd
        def _(pool):
            pool.memset(k.ones[:], 1.0).then_inc(ones_ready, 1)
            pool.memset(k.zeros[:], 0.0).then_inc(consts, 1)
            pool.wait_ge(consts, 1)
            pool.affine_select(out=k.ident[:], in_=k.zeros[:, 0:P], compare_op=ALU.not_equal, fill=1.0, base=0,
                               pattern=[[-1, P]], channel_multiplier=1).then_inc(consts, 1)

        @block.vector
        def _(dve):
            link = chain(dve, dve_chain)
            dve.wait_ge(load_cols, 16)
            lb0, lb1 = col(k, "hg_lb", 0, 8), col(k, "hg_lb", 8, 16)
            link(dve.tensor_tensor(lbt[:, 2, :], lb0, lb1, ALU.max))
            dve.tensor_tensor(lbt[:, 0, :], lb0, lbt[:, 2, :], ALU.subtract).then_inc(lbs, 1)
            dve.tensor_tensor(lbt[:, 1, :], lb1, lbt[:, 2, :], ALU.subtract).then_inc(lbs, 1)
            dve.wait_ge(sg_c, 1)
            dve.tensor_tensor(sc[:, :, 0], col(k, "c"), sgc[:, 0:8], ALU.mult).then_inc(silu_c, 1)
            dve.tensor_tensor(sc[:, :, 1], col(k, "c_ctx"), sgc[:, 8:16], ALU.mult).then_inc(silu_c, 1)
            for h in range(2):
                dve.wait_ge(load_x[h], 16)
                dve.tensor_tensor(hT[:, 4 * h:4 * h + 4, :], k.xT[:, 4 * h:4 * h + 4, :],
                                  k.xT[:, 4 * h:4 * h + 4, :], ALU.mult).then_inc(squared, 1)
            dve.wait_ge(load_c, 16)
            dve.tensor_tensor(hcT[:], ctxT[:], ctxT[:], ALU.mult).then_inc(squared, 1)
            dve.wait_ge(summed, 1)
            dve.tensor_scalar(rx[:], ps[:, 5, :], 1.0 / D, EPS, ALU.mult, ALU.add).then_inc(root_in, 1)
            dve.wait_ge(summed, 2)
            dve.tensor_scalar(rc[:], ps[:, 6, 0:C], 1.0 / D, EPS, ALU.mult, ALU.add).then_inc(root_in, 1)
            dve.wait_ge(lb_exp, 1)
            link(dve.tensor_tensor(lbt[:, 2, :], lbt[:, 0, :], lbt[:, 1, :], ALU.add))
            link(dve.reciprocal(lbt[:, 3, :], lbt[:, 2, :]))
            link(dve.tensor_tensor(lbt[:, 0, :], lbt[:, 0, :], lbt[:, 3, :], ALU.mult))
            link(dve.tensor_scalar(lbt[:, 1, :], lbt[:, 0, :], -1.0, 1.0, ALU.mult, ALU.add))
            dve.wait_ge(root_out, 1)
            link(dve.reciprocal(rx[:], rx[:]))
            dve.wait_ge(root_out, 2)
            link(dve.reciprocal(rc[:], rc[:]))
            dve.wait_ge(mod_done, 4)
            b16 = col(k, "b_mod", 0, 16).unsqueeze(2).to_broadcast([P, 16, 2])
            link(dve.tensor_tensor(m1[:], ps[:, 7, 0:32].rearrange("p (j s) -> p j s", s=2), b16, ALU.add))
            g8 = col(k, "norm1").unsqueeze(2).to_broadcast([P, 8, 2])
            dve.scalar_tensor_tensor(a1[:], m1[:, 8:16, :], 1.0, g8, ALU.add, ALU.mult).then_inc(affine, 1)
            for t in range(KT):
                dve.tensor_tensor(hT[:, t, :], k.xT[:, t, :], rx[:], ALU.mult).then_inc(scaled, 1)
                dve.tensor_tensor(hcT[:, t, :], ctxT[:, t, :], rc[:], ALU.mult).then_inc(scaled, 1)
            n = 0
            for j, job in enumerate(jobs):
                if job.kind == "silu":
                    n += 1
                    dve.wait_ge(evac, j + 1)
                    dve.tensor_tensor(job.dest, ps[:, j % NB, 0:job.N], sig[:, n % 2, :], ALU.mult).then_inc(gated, 1)
                if j == f_last - 1:
                    dve.wait_ge(evac, f_last)
                    for d in range(2):
                        for h in range(HG):
                            i = 4 * d + h
                            for f in (k.fx[d], k.fc[d]):
                                dve.tensor_scalar(f[:, h, :], f[:, h, :], lbt[:, 1, i:i + 1], lbt[:, 0, i:i + 1],
                                                  ALU.mult, ALU.add)

        @block.scalar
        def _(act):
            act.wait_ge(load_cols, 16)
            act.activation(sgc[:, 0:16], k.cols[:, 0:16], ACT.Sigmoid).then_inc(sg_c, 1)
            act.wait_ge(lbs, 2)
            act.activation(lbt[:, 0:2, :], lbt[:, 0:2, :], ACT.Exp).then_inc(lb_exp, 1)
            act.wait_ge(root_in, 1)
            act.activation(rx[:], rx[:], ACT.Sqrt).then_inc(root_out, 1)
            act.wait_ge(root_in, 2)
            act.activation(rc[:], rc[:], ACT.Sqrt).then_inc(root_out, 1)
            act.wait_ge(affine, 1)
            for t in range(KT):
                for s, h in ((0, hT), (1, hcT)):
                    act.wait_ge(scaled, 2 * t + s + 1)
                    act.activation(h[:, t, :], h[:, t, :], ACT.Identity, scale=a1[:, t, s:s + 1],
                                   bias=m1[:, t, s:s + 1]).then_inc(modulated, 1)
            n = 0
            for j, job in enumerate(jobs):
                act.wait_ge(proj, j + 1)
                src = ps[:, j % NB, 0:job.N]
                if job.kind == "query":
                    act.activation(job.dest.rearrange("p (c r l) -> p r c l", c=NCB, r=ROWS),
                                   src.rearrange("p (r c l) -> p r c l", r=ROWS, c=NCB), ACT.Copy,
                                   scale=DH ** -0.5).then_inc(evac, 1)
                elif job.kind == "silu":
                    n += 1
                    if n > 2:
                        act.wait_ge(gated, n - 2)
                    act.activation(sig[:, n % 2, :], src, ACT.Sigmoid).then_inc(evac, 1)
                else:
                    act.activation(job.dest, src, ACT.Sigmoid if job.kind == "sigmoid" else ACT.Copy).then_inc(evac, 1)

        @block.tensor
        def _(pe):
            pe.wait_ge(ones_ready, 1)
            for t in range(KT):
                if t % 4 == 0:
                    pe.wait_ge(squared, t // 4 + 1)
                last = pe.matmul(ps[:, 5, :], k.ones[:], hT[:, t, :], start=t == 0, stop=t == KT - 1)
            last.then_inc(summed, 1)
            pe.wait_ge(squared, 3)
            for t in range(KT):
                last = pe.matmul(ps[:, 6, 0:C], k.ones[:], hcT[:, t, :], start=t == 0, stop=t == KT - 1)
            last.then_inc(summed, 1)
            pe.wait_ge(silu_c, 2)

            for i in range(4):
                modulation(k, pe, f"mod{i}", sc, 8 * i, 2)
            pe.wait_ge(modulated, 2 * KT)
            now = None
            for j, job in enumerate(jobs):
                if job.chunk != now:
                    now = job.chunk
                    chunk_landed(k, pe, now)
                if j >= NB:
                    pe.wait_ge(evac, j - NB + 1)
                    if jobs[j - NB].kind == "silu":
                        pe.wait_ge(gated, silu_before[j - NB])
                for i, (a, b) in enumerate(job.mm):
                    last = pe.matmul(ps[:, j % NB, 0:job.N], a, b, start=i == 0, stop=i == KT - 1)
                last.then_inc(proj, 1)



def phase_neighbourhood(k):
    nc, ps = k.nc, k.ps
    WIN = ROWS * KB
    items = [(2 * hp + s, c) for hp in range(4) for c in range(NCB) for s in range(2)]
    N = len(items)
    variant = [0, 1, 1, 2]
    with ExitStack() as ctx:
        def sb(name, shape, dt=F32):
            return ctx.enter_context(nc.sbuf_tensor(name, shape, dt))

        toep = sb("toep", [P, ROWS, NH, KB + QB])
        bias = sb("bias", [P, 3, ROWS, NH, KB])
        mask = sb("win_mask", [P, 3, KB])
        s_sb = sb("s_sb", [P, 3, 512])
        pT = sb("pT", [P, 2, 512])
        mx = sb("na_max", [P, N, 4])
        sums = sb("na_sums", [P, N, 2])
        loaded, table = k.sem("rpb_loaded"), k.sem("bias_table")
        scored, maxed, nmax = k.sem("na_scored"), k.sem("na_maxed"), k.sem("na_nmax")
        exped, recip, normed = k.sem("na_exp"), k.sem("na_recip"), k.sem("na_normed")
        turned, turned_sb, summed, stored = (k.sem("na_turned"), k.sem("na_turned_sb"), k.sem("na_pv"),
                                             k.sem("na_stored"))
        block = ctx.enter_context(nc.Block())

        @block.sync
        def _(sp):
            for r in range(ROWS):
                sp.dma_start(toep[QB * r:QB * r + QB], k.dram["rpb_shifted"][:, ROWS - 1 - r:2 * ROWS - 1 - r])\
                  .then_inc(loaded, 16)
            sp.dma_start(mask[:], k.dram["win_mask"]).then_inc(loaded, 16)
            load_chunks(k, sp, k.at["mod9"] + SLOTS)

        @block.gpsimd
        def _(pool):
            pool.wait_ge(loaded, 16 * (ROWS + 1))
            for v, off in enumerate((16, 8, 0)):
                pool.tensor_tensor(bias[:, v].rearrange("p a h m -> p (a h) m"),
                                   toep[:, :, :, off:off + KB].rearrange("p a h m -> p (a h) m"),
                                   mask[:, v, :].unsqueeze(1).to_broadcast([P, ROWS * NH, KB]),
                                   ALU.add).then_inc(table, 1)

        @block.tensor
        def _(pe):
            def scores(i):
                h, c = items[i]
                a, hp = DH * (h % 2), h // 2
                if i >= 2:
                    pe.wait_ge(maxed, 2 * (i - 1))
                q = k.qT[a:a + DH, hp, c * P:(c + 1) * P]
                k0 = min(max(QB * c - KB // 4, 0), GW - KB)
                win = k.kT[a:a + DH, hp, 0:T].rearrange("p (r x) -> p r x", r=ROWS)[:, :, k0:k0 + KB]
                pe.matmul(ps[:, i % 2, 0:WIN], q, win, start=True, stop=True)
                pe.matmul(ps[:, i % 2, WIN:512], q, k.kT[a:a + DH, hp, T:T + C], start=True, stop=True)\
                  .then_inc(scored, 1)

            def turn(i):
                pe.wait_ge(normed, i + 1)
                if i >= 2:
                    pe.wait_ge(turned_sb, i - 1)
                for j in range(4):
                    last = pe.transpose(ps[:, 2 + i % 2, j * P:(j + 1) * P], s_sb[:, i % 3, j * P:(j + 1) * P],
                                        k.ident[:])
                last.then_inc(turned, 1)

            def values(i):
                h, c = items[i]
                pair = i // 2
                pe.wait_ge(turned_sb, i + 1)
                if i % 2 == 0 and pair >= 2:
                    pe.wait_ge(stored, pair - 1)
                a = DH * (h % 2)
                for j in range(4):
                    v = (k.vw[:, 2 * c + j, :] if j < 2 else k.vc[:, j - 2, :])[:, h * DH:(h + 1) * DH]
                    last = pe.matmul(ps[a:a + DH, 4 + pair % 2, 0:P], v, pT[:, i % 2, j * P:(j + 1) * P],
                                     start=j == 0, stop=j == 3)
                last.then_inc(summed, 1)

            mods = [(f"mod{i}", k.sc, 8 * i, 2, (n,)) for i in range(4, 10) for n in range(4)]
            done = 0
            for n in range(N + 3):
                if n < N:
                    scores(n)
                if 0 <= n - 2 < N:
                    turn(n - 2)
                if 0 <= n - 3 < N:
                    values(n - 3)
                while done < n * len(mods) // (N + 2):
                    modulation(k, pe, *mods[done])
                    done += 1

        @block.vector
        def _(dve):
            dve.wait_ge(table, 3)
            for n in range(N + 1):
                if n < N:
                    h, c = items[n]
                    dve.wait_ge(scored, n + 1)
                    if n >= 3:
                        dve.wait_ge(turned, n - 2)
                    dve.tensor_tensor_reduce(
                        s_sb[:, n % 3, 0:WIN].rearrange("p (r x) -> p r x", r=ROWS),
                        ps[:, n % 2, 0:WIN].rearrange("p (r x) -> p r x", r=ROWS), bias[:, variant[c], :, h, :],
                        1.0, LOWEST, ALU.add, ALU.max, mx[:, n, 0:1]).then_inc(maxed, 1)
                    dve.tensor_tensor_reduce(s_sb[:, n % 3, WIN:512], ps[:, n % 2, WIN:512], k.zeros[:, 0:C], 1.0, LOWEST,
                                             ALU.add, ALU.max, mx[:, n, 1:2]).then_inc(maxed, 1)
                    dve.wait_ge(maxed, 2 * n + 2)
                    dve.tensor_reduce(mx[:, n, 2:3], mx[:, n, 0:2], AX.X, ALU.max, negate=True).then_inc(nmax, 1)
                if n >= 1:
                    i = n - 1
                    dve.wait_ge(exped, i + 1)
                    dve.reciprocal(sums[:, i, 1:2], sums[:, i, 0:1]).then_inc(recip, 1)
                    dve.wait_ge(recip, i + 1)
                    dve.tensor_scalar(s_sb[:, i % 3, :], s_sb[:, i % 3, :], sums[:, i, 1:2], None, ALU.mult)\
                       .then_inc(normed, 1)
            dve.wait_ge(k.mod_done, 10)
            dve.tensor_tensor(k.mod[:, 0:40], ps[:, 7, 0:80].rearrange("p (j s) -> p j s", s=2)[:, :, 0],
                              col(k, "b_mod", 0, 40), ALU.add)

        @block.scalar
        def _(act):
            for n in range(N + 4):
                if n < N:
                    act.wait_ge(nmax, n + 1)
                    act.activation(s_sb[:, n % 3, :], s_sb[:, n % 3, :], ACT.Exp, bias=mx[:, n, 2:3],
                                   accum_out=sums[:, n, 0:1]).then_inc(exped, 1)
                if 0 <= n - 2 < N:
                    i = n - 2
                    act.wait_ge(turned, i + 1)
                    if i >= 2:
                        act.wait_ge(summed, i - 1)
                    act.activation(pT[:, i % 2, :], ps[:, 2 + i % 2, :], ACT.Copy).then_inc(turned_sb, 1)
                if 0 <= n - 4 < N and (n - 4) % 2:
                    pair = (n - 4) // 2
                    hp, c = divmod(pair, NCB)
                    act.wait_ge(summed, 2 * pair + 2)
                    act.activation(k.mixT[:, hp, :].rearrange("p (r c l) -> p c r l", r=ROWS, c=NCB)[:, c],
                                   ps[:, 4 + pair % 2, 0:P].rearrange("p (r l) -> p r l", r=ROWS),
                                   ACT.Copy).then_inc(stored, 1)



def phase_hgrn(k):
    nc, ps = k.nc, k.ps
    TILES = T // P
    LEV = 7
    with ExitStack() as ctx:
        def sb(name, shape, dt=F32):
            return ctx.enter_context(nc.sbuf_tensor(name, shape, dt))

        kk = sb("kk", [P, HG, T])
        suf = sb("suf", [P, HG, T])
        qd = sb("qd", [P, 2, HG, T])
        kd = sb("kd", [P, 2, HG, T])
        A = sb("A_diag", [P, HG * TILES, P])
        aoff = sb("A_off", [P, HG, 6, P])
        state = sb("ctx_state", [P, 2, HG, P])
        pred = sb("pred", [P, 2, LEV, P], mybir.dt.uint8)
        kc, sufc = kd[:, 0, 0:2, :].rearrange("p a t -> p (a t)").rearrange("p (h t) -> p h t", h=HG), \
            kd[:, 0, 2:4, :].rearrange("p a t -> p (a t)").rearrange("p (h t) -> p h t", h=HG)
        kcT = kd[:, 1, 0:2, :].rearrange("p a t -> p (a t)").rearrange("p (n d) -> p n d", d=P)
        square, root = qd[:, 0], qd[:, 1]
        pred_f = qd[:, 1].rearrange("p h t -> p (h t)")[:, 0:2 * LEV * P]
        cdve = k.sem("hg_dve_chain")
        keys_c, turned_c, turned_c_sb = k.sem("ctx_keys"), k.sem("ctx_turned"), k.sem("ctx_turned_sb")
        state_mm, state_sb, preds = k.sem("ctx_state_mm"), k.sem("ctx_state_sb"), k.sem("pred_loaded")
        kk_ready, ready, updated = k.sem("kk_ready"), k.sem("level_ready"), k.sem("level_updated")
        level_mm, level_cp, av = k.sem("level_mm"), k.sem("level_copied"), k.sem("av_done")
        suf_one = k.sem("suf_one")
        squares, norm_mm, rooted, rin, o_norm = (k.sem("hg_squares"), k.sem("hg_norm_mm"), k.sem("hg_rooted"),
                                                 k.sem("hg_root_in"), k.sem("hg_o_norm"))

        def n_ready(d, s):
            return 19 * d + min(2 * s, 19)

        def n_mm(d, s, half=1):
            return 18 * d + (2 * s + half + 1 if s <= LEV else s + 9)

        def n_upd(d, s):
            return 17 * d + min(2 * s, 17)

        def halves(x, s, d):
            v = x.rearrange("p h t -> p (h t)").rearrange("p (n two m) -> p n two m", two=2, m=1 << (s - 1))
            return v[:, :, d, :], v[:, :, 1 - d, :]

        def totals(pre, s, d):
            m = 1 << (s - 1)
            a, b = halves(pre, s, d)
            at = 0 if d else m - 1
            return [x[:, :, at:at + 1].to_broadcast([P, HG * T // (2 * m), m]) for x in (a, b)]

        block = ctx.enter_context(nc.Block())

        @block.sync
        def _(sp):
            sp.dma_start(pred_f, k.dram["pred"].rearrange("p d s t -> p (d s t)")).then_inc(preds, 16)

        @block.gpsimd
        def _(pool):
            for d in range(2):
                if d:
                    pool.wait_ge(ready, n_ready(0, 9))
                    pool.wait_ge(updated, n_upd(0, 9))
                else:
                    pool.wait_ge(state_mm, 2)
                pool.memset(suf[:], 1.0).then_inc(suf_one, 1)
                for s in range(1, 11):
                    m = 10 * d + s - 1
                    if s == 1:
                        pool.wait_ge(kk_ready, d + 1)
                        pool.wait_ge(suf_one, d + 1)
                    else:
                        pool.wait_ge(updated, n_upd(d, s - 1))
                    if m >= 2:
                        if s == 1:
                            pool.wait_ge(level_mm, n_mm(0, 9))
                        elif s == 2:
                            pool.wait_ge(level_mm, n_mm(d - 1, 9))
                            if d:
                                pool.wait_ge(av, HG * d)
                        else:
                            pool.wait_ge(level_mm, n_mm(d, s - 2))
                    q, key = qd[:, m % 2], kd[:, m % 2]
                    pre = k.fx[d]
                    if s == 10:
                        pool.tensor_tensor(q[:], k.hq[:], pre[:], ALU.mult).then_inc(ready, 1)
                        continue
                    if m < 2:
                        pool.tensor_tensor(key[:], kk[:], suf[:], ALU.mult).then_inc(ready, 1)
                        pool.tensor_tensor(q[:], k.hq[:], pre[:], ALU.mult).then_inc(ready, 1)
                        continue
                    pool.tensor_tensor(halves(key, s, d)[0], halves(kk, s, d)[0], halves(suf, s, d)[0],
                                       ALU.mult).then_inc(ready, 1)
                    pool.tensor_tensor(halves(q, s, d)[1], halves(k.hq, s, d)[1], halves(pre, s, d)[1],
                                       ALU.mult).then_inc(ready, 1)

        @block.vector
        def _(dve):
            link = chain(dve, cdve)
            for d in range(2):
                if d:
                    dve.wait_ge(turned_c, 1)
                f = k.fc[d]
                link(dve.memset(sufc[:], 1.0))
                link(dve.tensor_scalar(kc[:], f[:], -1.0, 1.0, ALU.mult, ALU.add))
                for h in range(HG):
                    if d == 0:
                        o, g = sufc[:, h, C - 2::-1], f[:, h, C - 1:0:-1]
                    else:
                        o, g = sufc[:, h, 1:C], f[:, h, 0:C - 1]
                    last = dve.tensor_tensor_scan(out=o, data0=g, data1=k.zeros[:, 0:C - 1], initial=1.0,
                                                  op0=ALU.mult, op1=ALU.add)
                link(last)
                dve.tensor_tensor(kc[:], kc[:], sufc[:], ALU.mult).then_inc(keys_c, 1)
            dve.wait_ge(preds, 16)
            link(dve.tensor_copy(pred[:].rearrange("p d s t -> p (d s t)"), pred_f))
            for d in range(2):
                if d:
                    dve.wait_ge(ready, n_ready(0, 9))
                dve.tensor_scalar(kk[:], k.fx[d][:], -1.0, 1.0, ALU.mult, ALU.add).then_inc(kk_ready, 1)
                for s in range(10):
                    if s >= 1:
                        dve.wait_ge(ready, n_ready(d, s))
                        pre = k.fx[d]
                        tot_s, tot_q = totals(pre, s, d)
                        if s < 9:
                            side = halves(suf, s, d)[0]
                            dve.tensor_tensor(side, side, tot_q, ALU.mult).then_inc(updated, 1)
                        dve.wait_ge(updated, n_upd(d, s) - 1)
                        side = halves(pre, s, d)[1]
                        dve.tensor_tensor(side, side, tot_s, ALU.mult).then_inc(updated, 1)
                        dve.wait_ge(updated, n_upd(d, s))
                    if s <= LEV:
                        for half in range(2):
                            dve.wait_ge(level_mm, n_mm(d, s, half))
                            src = ps[:, 2 * half:2 * half + 2, :].rearrange("p b (i t) -> p (b i) t", t=P)
                            dst = A[:, 8 * half:8 * half + 8, :]
                            if s == 0:
                                if d and half == 0:
                                    dve.wait_ge(av, HG)
                                ins = dve.tensor_tensor(dst, src, k.ident[:].unsqueeze(1).to_broadcast([P, 8, P]),
                                                        ALU.mult)
                            else:
                                dve.wait_ge(level_cp, n_mm(d, s - 1, half))
                                ins = dve.copy_predicated(
                                    dst, pred[:, d, s - 1, :].unsqueeze(1).to_broadcast([P, 8, P]), src)
                            ins.then_inc(level_cp, 1)
                    else:
                        dve.wait_ge(level_mm, n_mm(d, s))
                        if s == 8:
                            dve.tensor_copy(aoff[:, :, 0:2, :], ps[:, 0:2, :].rearrange("p b (h i t) -> p (b h) i t", i=2, t=P))\
                               .then_inc(level_cp, 1)
                        else:
                            dve.tensor_copy(aoff[:, :, 2:6, :], ps[:, 0:4, :].rearrange("p h (i t) -> p h i t", t=P))\
                               .then_inc(level_cp, 1)
            for h in range(HG):
                dve.wait_ge(norm_mm, h + 1)
                dve.tensor_scalar(root[:, h, :], ps[:, h, :], 1.0 / P, EPS, ALU.mult, ALU.add).then_inc(rin, 1)
            for h in range(HG):
                dve.wait_ge(rooted, h + 1)
                link(dve.reciprocal(root[:, h, :], root[:, h, :]))
                link(dve.scalar_tensor_tensor(root[:, h, :], ps[:, 4 + h, :], col(k, "hg_norm", h, h + 1),
                                              root[:, h, :], ALU.mult, ALU.mult))
                dve.tensor_tensor(k.mixT[:, 4 + h, :], root[:, h, :], k.hgate[:, h, :], ALU.mult)

        @block.scalar
        def _(act):
            for d in range(2):
                act.wait_ge(turned_c, d + 1)
                if d:
                    act.wait_ge(state_mm, 1)
                act.activation(kcT[:], ps[:, 0:2, :].rearrange("p b (i t) -> p (b i) t", t=P), ACT.Copy)\
                   .then_inc(turned_c_sb, 1)
                act.wait_ge(state_mm, d + 1)
                act.activation(state[:, d], ps[:, 2, :].rearrange("p (h t) -> p h t", t=P), ACT.Copy)\
                   .then_inc(state_sb, 1)
            act.wait_ge(av, 2 * HG)
            for h in range(HG):
                act.activation(square[:, h, :], ps[:, 4 + h, :], ACT.Square).then_inc(squares, 1)
            for h in range(HG):
                act.wait_ge(rin, h + 1)
                act.activation(root[:, h, :], root[:, h, :], ACT.Sqrt).then_inc(rooted, 1)

        @block.tensor
        def _(pe):
            for d in range(2):
                pe.wait_ge(keys_c, d + 1)
                if d:
                    pe.wait_ge(turned_c_sb, 1)
                for i in range(2 * HG):
                    h, j = divmod(i, 2)
                    last = pe.transpose(ps[:, i // 4, (i % 4) * P:(i % 4 + 1) * P], kc[:, h, j * P:(j + 1) * P],
                                        k.ident[:])
                last.then_inc(turned_c, 1)
                pe.wait_ge(turned_c_sb, d + 1)
                if d:
                    pe.wait_ge(state_sb, 1)
                for h in range(HG):
                    for j in range(2):
                        last = pe.matmul(ps[:, 2, h * P:(h + 1) * P], kcT[:, 2 * h + j, :],
                                         k.ic[:, j, h * P:(h + 1) * P], start=j == 0, stop=j == 1)
                last.then_inc(state_mm, 1)
            pe.wait_ge(state_sb, 2)
            for d in range(2):
                for s in range(LEV + 1):
                    if s == 0:
                        pe.wait_ge(kk_ready, d + 1)
                        q, key = k.hq, kk
                    else:
                        m = 10 * d + s - 1
                        pe.wait_ge(ready, n_ready(d, s))
                        q, key = qd[:, m % 2], kd[:, m % 2]
                    for half in range(2):
                        done = n_mm(d, s, half) - 2 if s else 18 * d
                        if done > 0:
                            pe.wait_ge(level_cp, done)
                        for h in (2 * half, 2 * half + 1):
                            for i in range(TILES):
                                last = pe.matmul(ps[:, h, i * P:(i + 1) * P], key[:, h, i * P:(i + 1) * P],
                                                 q[:, h, i * P:(i + 1) * P], start=True, stop=True)
                        last.then_inc(level_mm, 1)
                pe.wait_ge(ready, n_ready(d, 8))
                pe.wait_ge(level_cp, n_mm(d, 7, 0))
                m = 10 * d + 7
                q, key = qd[:, m % 2], kd[:, m % 2]
                for h in range(HG):
                    for i in range(2):
                        a, b = 2 * i + d, 2 * i + 1 - d
                        at = (2 * h + i) % 4 * P
                        last = pe.matmul(ps[:, h // 2, at:at + P], key[:, h, a * P:(a + 1) * P],
                                         q[:, h, b * P:(b + 1) * P], start=True, stop=True)
                last.then_inc(level_mm, 1)
                pe.wait_ge(ready, n_ready(d, 9))
                pe.wait_ge(level_cp, n_mm(d, 8))
                m += 1
                q, key = qd[:, m % 2], kd[:, m % 2]
                for h in range(HG):
                    for i in range(2):
                        a, b = 2 * d + i, 2 * (1 - d)
                        last = pe.matmul(ps[:, h, 2 * i * P:2 * (i + 1) * P], key[:, h, a * P:(a + 1) * P],
                                         q[:, h, b * P:(b + 2) * P], start=True, stop=True)
                last.then_inc(level_mm, 1)
                pe.wait_ge(ready, n_ready(d, 10))
                pe.wait_ge(level_cp, n_mm(d, 9))
                m += 1
                q = qd[:, m % 2]
                for h in range(HG):
                    def values(tile):
                        return k.ix[:, tile, h * P:(h + 1) * P]

                    pe.matmul(ps[:, 4 + h, :], state[:, d, h, :], q[:, h, :], start=d == 0, stop=False)
                    for i in range(TILES):
                        pe.matmul(ps[:, 4 + h, i * P:(i + 1) * P], values(i), A[:, TILES * h + i, :],
                                  start=False, stop=False)
                    for i in range(2):
                        a, b = 2 * i + d, 2 * i + 1 - d
                        pe.matmul(ps[:, 4 + h, b * P:(b + 1) * P], values(a), aoff[:, h, i, :],
                                  start=False, stop=False)
                    for i in range(2):
                        a, b = 2 * d + i, 2 * (1 - d)
                        last = pe.matmul(ps[:, 4 + h, b * P:(b + 2) * P], values(a),
                                         aoff[:, h, 2 + 2 * i:4 + 2 * i, :].rearrange("p i t -> p (i t)"),
                                         start=False, stop=d == 1 and i == 1)
                    last.then_inc(av, 1)
            for h in range(HG):
                pe.wait_ge(squares, h + 1)
                pe.matmul(ps[:, h, :], k.ones[:], square[:, h, :], start=True, stop=True).then_inc(norm_mm, 1)



class Norm:

    def __init__(self, k, src, dst, root, bank, tiles, gain, shift=None):
        self.k, self.src, self.dst, self.root, self.bank, self.tiles = k, src, dst, root, bank, tiles
        self.gain, self.shift = gain, shift
        (self.squared, self.summed, self.mean, self.rooted, self.inverse, self.scaled, self.done) = k.norm_sems
        self.n, self.t0 = k.norms + 1, k.norm_tiles
        k.norms, k.norm_tiles = k.norms + 1, k.norm_tiles + tiles

    def act_square(self, act):
        for t in range(self.tiles):
            act.activation(self.dst[:, t, :], self.src[:, t, :], ACT.Square).then_inc(self.squared, 1)

    def pe_sum(self, pe):
        for t in range(self.tiles):
            pe.wait_ge(self.squared, self.t0 + t + 1)
            last = pe.matmul(self.k.ps[:, self.bank, :], self.k.ones[:], self.dst[:, t, :], start=t == 0,
                             stop=t == self.tiles - 1)
        last.then_inc(self.summed, 1)

    def act_root(self, act):
        act.wait_ge(self.mean, self.n)
        act.activation(self.root, self.root, ACT.Sqrt).then_inc(self.rooted, 1)

    def dve_scale(self, dve):
        dve.wait_ge(self.summed, self.n)
        dve.tensor_scalar(self.root, self.k.ps[:, self.bank, :], 1.0 / (P * self.tiles), EPS, ALU.mult, ALU.add)\
           .then_inc(self.mean, 1)
        dve.wait_ge(self.rooted, self.n)
        dve.reciprocal(self.root, self.root).then_inc(self.inverse, 1)
        dve.wait_ge(self.inverse, self.n)
        for t in range(self.tiles):
            dve.tensor_tensor(self.dst[:, t, :], self.src[:, t, :], self.root, ALU.mult).then_inc(self.scaled, 1)

    def act_affine(self, act):
        for t in range(self.tiles):
            act.wait_ge(self.scaled, self.t0 + t + 1)
            extra = {} if self.shift is None else {"bias": self.shift[:, t:t + 1]}
            act.activation(self.dst[:, t, :], self.dst[:, t, :], ACT.Copy if self.shift is None else ACT.Identity,
                           scale=self.gain[:, t:t + 1], **extra).then_inc(self.done, 1)

    def wait(self, eng, tiles=None):
        eng.wait_ge(self.done, self.t0 + (self.tiles if tiles is None else tiles))



def phase_route(k):
    nc, ps = k.nc, k.ps
    TT = T // P
    HH = 2 * PH
    UH = 4
    UP = UH // 2
    UNITS = TT * HH // UH
    with ExitStack() as ctx:
        def sb(name, shape, dt=F32):
            return ctx.enter_context(nc.sbuf_tensor(name, shape, dt))

        qp = sb("peer_q", [P, HH, T])
        keys = sb("peer_keysT", [P, HH, NKEYS])
        s_sb = sb("peer_s", [P, 4, UH, NKEYS])
        s_cut = sb("peer_s_cut", [P, UH, NKEYS])
        val = sb("peer_val", [P, UH, TOPK])
        ind = sb("peer_ind", [P, 2, UH, TOPK], U32)
        indf = sb("peer_indf", [P, UH, TOPK])
        cand = sb("peer_cand", [P, UP, TOPK * TOPK])
        cand_cut = s_cut[:].rearrange("p (h two) n -> p h (two n)", two=2)
        top = sb("peer_top", [P, TT, PH, TOPK])
        pos = sb("peer_pos", [P, UP * TOPK], U32)
        half = sb("peer_half", [P, 2, UP * TOPK], U32)
        pick = sb("peer_pick", [P, 2, 2, UP * TOPK, TOPK])
        sel = sb("peer_sel", [P, TT, 3, PH * TOPK])
        small = sb("peer_small", [P, 2, TT, PH])
        io16 = sb("io16", [P, TOPK], I32)
        rt = sb("c_root", [P, T])
        a2 = sb("c_gain", [P, 8])
        cdve = k.sem("c_dve_chain")
        out_mm, out_sb, a2_ready = k.sem("out_mm"), k.sem("out_sb"), k.sem("c_gain_ready")
        q_mm, q_sb, keys_in = k.sem("peer_q_mm"), k.sem("peer_q_sb"), k.sem("peer_keys_loaded")
        s_mm, s_ready, s_used = k.sem("peer_s_mm"), k.sem("peer_s_ready"), k.sem("peer_s_used")
        io_ready, shifted, exped = k.sem("io_ready"), k.sem("top_shifted"), k.sem("top_exp")
        split, picked, selected = k.sem("pos_split"), k.sem("picked"), k.sem("selected")
        eqs, indexed, ind_cast = k.sem("pick_eq"), k.sem("peer_indexed"), k.sem("peer_ind_cast")
        turned = k.sem("sel_turned")
        norm = Norm(k, k.xT, k.mixT, rt[:], 7, KT, a2, k.mod[:, 24:32])
        k.used[k.at["out0"]], k.used[k.at["out1"]] = (out_mm, 4), (out_mm, 8)
        for i in range(4):
            k.used[k.at[f"wq{i}"]] = (q_mm, 4 * i + 4)
        block = ctx.enter_context(nc.Block())

        def in_order(queries, scores):
            for n in range(HH + 1):
                if n < HH:
                    queries(n)
                if n and n % UH == 0:
                    for tt in range(TT):
                        scores(TT * (n // UH - 1) + tt)

        @block.sync
        def _(sp):
            sp.dma_start(keys[:], k.dram["keysT"]).then_inc(keys_in, 16)
            load_chunks(k, sp, k.at["ada5"])

        @block.gpsimd
        def _(pool):
            pool.iota(io16[:], pattern=[[1, TOPK]], base=0, channel_multiplier=0).then_inc(io_ready, 1)
            pool.iota(k.io_int[:], pattern=[[1, P]], base=0, channel_multiplier=0).then_inc(io_ready, 1)
            pool.wait_ge(io_ready, 2)
            pool.tensor_copy(k.iota[:], k.io_int[:]).then_inc(io_ready, 1)
            for u in range(UNITS):
                pool.wait_ge(indexed, u + 1)
                if u:
                    pool.wait_ge(picked, 2 * u)
                pool.tensor_copy(indf[:], ind[:, u % 2]).then_inc(ind_cast, 1)
                pool.wait_ge(ind_cast, u + 1)
                for i in range(2):
                    pool.wait_ge(eqs, 2 * u + i + 1)
                    p4 = pick[:, u % 2, i].rearrange("p (h c) a -> p h c a", h=UP)
                    pool.tensor_tensor(p4, p4, indf[:, i::2, :].unsqueeze(2).to_broadcast([P, UP, TOPK, TOPK]),
                                       ALU.mult).then_inc(picked, 1)

        @block.vector
        def _(dve):
            link = chain(dve, cdve)
            dve.scalar_tensor_tensor(a2[:], k.mod[:, 32:40], 1.0, col(k, "norm2"), ALU.add, ALU.mult)\
               .then_inc(a2_ready, 1)
            for n in range(KT):
                dve.wait_ge(out_mm, n + 1)
                dve.scalar_tensor_tensor(k.xT[:, n, :], ps[:, n % 4, :], k.mod[:, 16 + n:17 + n], k.xT[:, n, :],
                                         ALU.mult, ALU.add).then_inc(out_sb, 1)
            dve.wait_ge(out_sb, KT)
            norm.dve_scale(dve)
            dve.wait_ge(io_ready, 3)

            def gather(u):
                c, tt = divmod(u, TT)
                dve.wait_ge(picked, 2 * u + 2)
                for i in range(2):
                    dve.tensor_reduce(sel[:, tt, i, c * UP * TOPK:(c + 1) * UP * TOPK], pick[:, u % 2, i], AX.X, ALU.add)

            for u in range(UNITS):
                c, tt = divmod(u, TT)
                s = s_sb[:, u % 4]
                dve.wait_ge(s_ready, u + 1)
                for h in range(UH):
                    last = dve.max(val[:, h, 0:8], s[:, h, :])
                link(last)
                if u >= 2:
                    dve.wait_ge(ind_cast, u - 1)
                for h in range(UH):
                    dve.max_index(ind[:, u % 2, h, 0:8], val[:, h, 0:8], s[:, h, :])
                    last = dve.match_replace(s_cut[:, h, :], val[:, h, 0:8], s[:, h, :], LOWEST)
                last.then_inc(s_used, 1)
                dve.wait_ge(s_used, u + 1)
                for h in range(UH):
                    last = dve.max(val[:, h, 8:16], s_cut[:, h, :])
                link(last)
                for h in range(UH):
                    last = dve.max_index(ind[:, u % 2, h, 8:16], val[:, h, 8:16], s_cut[:, h, :])
                last.then_inc(indexed, 1)
                c4 = cand[:].rearrange("p h (a b) -> p h a b", a=TOPK)
                link(dve.tensor_tensor(c4, val[:, 0::2, :].unsqueeze(3).to_broadcast([P, UP, TOPK, TOPK]),
                                       val[:, 1::2, :].unsqueeze(2).to_broadcast([P, UP, TOPK, TOPK]), ALU.add))
                best = top[:, tt, c * UP:(c + 1) * UP, :]
                for h in range(UP):
                    last = dve.max(best[:, h, 0:8], cand[:, h, :])
                link(last)
                p3 = pos[:].rearrange("p (h c) -> p h c", h=UP)
                for h in range(UP):
                    dve.max_index(p3[:, h, 0:8], best[:, h, 0:8], cand[:, h, :])
                    last = dve.match_replace(cand_cut[:, h, :], best[:, h, 0:8], cand[:, h, :], LOWEST)
                link(last)
                for h in range(UP):
                    last = dve.max(best[:, h, 8:16], cand_cut[:, h, :])
                link(last)
                for h in range(UP):
                    last = dve.max_index(p3[:, h, 8:16], best[:, h, 8:16], cand_cut[:, h, :])
                link(last)
                dve.tensor_scalar(half[:, 0, :], pos[:], 4, None, ALU.logical_shift_right).then_inc(split, 1)
                dve.tensor_scalar(half[:, 1, :], pos[:], TOPK - 1, None, ALU.bitwise_and).then_inc(split, 1)
                dve.wait_ge(split, 2 * u + 2)
                for i in range(2):
                    dve.tensor_tensor(pick[:, u % 2, i], half[:, i, :].unsqueeze(2).to_broadcast([P, UP * TOPK, TOPK]),
                                      io16[:].unsqueeze(1).to_broadcast([P, UP * TOPK, TOPK]),
                                      ALU.is_equal).then_inc(eqs, 1)
                if u:
                    gather(u - 1)
            g = sel[:, :, 2, :].rearrange("p t (h c) -> p t h c", h=PH)
            dve.tensor_tensor(g, top[:], top[:, :, :, 0:1].to_broadcast([P, TT, PH, TOPK]), ALU.subtract)\
               .then_inc(shifted, 1)
            gather(UNITS - 1)
            dve.wait_ge(exped, 1)
            link(dve.tensor_reduce(small[:, 0], g, AX.X, ALU.add))
            link(dve.reciprocal(small[:, 1], small[:, 0]))
            dve.tensor_tensor(g, g, small[:, 1].unsqueeze(3).to_broadcast([P, TT, PH, TOPK]), ALU.mult)\
               .then_inc(selected, 1)
            dve.wait_ge(k.mod_done, 12 + 6)
            dve.tensor_tensor(k.mod[:, 40:48], ps[:, 7, 80:96].rearrange("p (j s) -> p j s", s=2)[:, :, 0],
                              col(k, "b_mod", 40, 48), ALU.add)
            dve.tensor_tensor(k.ada[:], ps[:, 7, 96:120], col(k, "b_ada_2"), ALU.add)

        @block.scalar
        def _(act):
            act.wait_ge(out_sb, KT)
            norm.act_square(act)
            norm.act_root(act)
            act.wait_ge(a2_ready, 1)
            norm.act_affine(act)

            def queries(n):
                act.wait_ge(q_mm, n + 1)
                act.activation(qp[:, n, :], ps[:, n % 4, :], ACT.Copy).then_inc(q_sb, 1)

            def scores(u):
                act.wait_ge(s_mm, u + 1)
                if u >= 4:
                    act.wait_ge(s_used, u - 3)
                act.activation(s_sb[:, u % 4], ps[:, 4 + u % 3, :].rearrange("p (h n) -> p h n", n=NKEYS),
                               ACT.Copy).then_inc(s_ready, 1)

            in_order(queries, scores)
            act.wait_ge(shifted, 1)
            g = sel[:, :, 2, :]
            act.activation(g, g, ACT.Exp).then_inc(exped, 1)
            for tt in range(TT):
                act.wait_ge(turned, tt + 1)
                act.activation(k.selT[:, :, tt * P:(tt + 1) * P], ps[:, tt, 0:3 * P].rearrange("p (i t) -> p i t", t=P),
                               ACT.Copy)

        @block.tensor
        def _(pe):
            for n in range(KT):
                if n % 4 == 0:
                    chunk_landed(k, pe, f"out{n // 4}")
                if n >= 4:
                    pe.wait_ge(out_sb, n - 3)
                w = chunk_view(k, f"out{n // 4}")
                for t in range(KT):
                    last = pe.matmul(ps[:, n % 4, :], w[:, t, n % 4 * P:(n % 4 + 1) * P], k.mixT[:, t, :],
                                     start=t == 0, stop=t == KT - 1)
                last.then_inc(out_mm, 1)
            norm.pe_sum(pe)
            norm.wait(pe)
            pe.wait_ge(keys_in, 16)

            def queries(n):
                if n % 4 == 0:
                    chunk_landed(k, pe, f"wq{n // 4}")
                if n >= 4:
                    pe.wait_ge(q_sb, n - 3)
                w = chunk_view(k, f"wq{n // 4}")
                for t in range(KT):
                    last = pe.matmul(ps[:, n % 4, :], w[:, t, n % 4 * P:(n % 4 + 1) * P], k.mixT[:, t, :],
                                     start=t == 0, stop=t == KT - 1)
                last.then_inc(q_mm, 1)

            def scores(u):
                c, tt = divmod(u, TT)
                pe.wait_ge(q_sb, UH * c + UH)
                if u >= 3:
                    pe.wait_ge(s_ready, u - 2)
                for i in range(UH):
                    h = UH * c + i
                    last = pe.matmul(ps[:, 4 + u % 3, i * P:(i + 1) * P], qp[:, h, tt * P:(tt + 1) * P], keys[:, h, :],
                                     start=True, stop=True)
                last.then_inc(s_mm, 1)

            in_order(queries, scores)
            for i in range(10, 12):
                modulation(k, pe, f"mod{i}", k.sc, 8 * i, 2)
            for i in range(6):
                modulation(k, pe, f"ada{i}", col(k, "c_2").unsqueeze(2), 96 + 4 * i, 1)
            pe.wait_ge(selected, 1)
            for tt in range(TT):
                for i in range(3):
                    last = pe.transpose(ps[:, tt, i * P:(i + 1) * P], sel[:, tt, i, :], k.ident[:])
                last.then_inc(turned, 1)


def raw_experts(k):
    return (k.ring[:, 0, :].rearrange("p (b x) -> p b x", b=2),
            k.ring[:, 1, :].rearrange("p (b j d) -> p b j d", b=2, j=EXPERT_TILES))



def phase_spread(k):
    nc, ps = k.nc, k.ps
    G = 32
    B = 8
    Q = G // 4
    TB = TOKEN_BLOCK
    with ExitStack() as ctx:
        def sb(name, shape, dt=F32):
            return ctx.enter_context(nc.sbuf_tensor(name, shape, dt))

        one2 = sb("one2", [P, G, P])
        one1 = sb("one1", [P, G, P])
        gs = [sb(f"gates_sb{i}", [P, NKEYS, TB]) for i in range(2)]
        equal, built, mixed, evac = k.sem("onehot_equal"), k.sem("onehots"), k.sem("gates_mm"), k.sem("gates_sb")
        wrote = [k.sem(f"gates_written{i}") for i in range(2)]
        k.u_in = [k.sem(f"u_loaded{i}") for i in range(2)]
        k.v_in = [k.sem(f"v_loaded{i}") for i in range(2)]
        u_raw, v_raw = raw_experts(k)
        block = ctx.enter_context(nc.Block())
        NI = TB // G

        def turns(eng, body):
            with eng.Fori(0, T // (2 * TB)) as o:
                for half in range(2):
                    with eng.Fori(0, NI) as i:
                        body(o, half, i, o * (2 * NI) + i + half * NI)

        @block.vector
        def _(dve):
            def body(o, half, i, n):
                for q in range(G // B):
                    dve.wait_ge(mixed, n * Q + (q + 1) * (B // 4))
                    for one, which in ((one2, 1), (one1, 0)):
                        last = dve.tensor_tensor(one[:, q * B:(q + 1) * B, :],
                                                 k.iota[:].unsqueeze(1).to_broadcast([P, B, P]),
                                                 k.selT[:, which, bass.ds(n * G + q * B, B)].unsqueeze(2)
                                                 .to_broadcast([P, B, P]), ALU.is_equal)
                    last.then_inc(equal, 1)

            dve.sem_inc(mixed, Q)
            turns(dve, body)

        @block.gpsimd
        def _(pool):
            def body(o, half, i, n):
                for q in range(G // B):
                    pool.wait_ge(equal, n * (G // B) + (q + 1))
                    pool.tensor_tensor(one1[:, q * B:(q + 1) * B, :], one1[:, q * B:(q + 1) * B, :],
                                       k.selT[:, 2, bass.ds(n * G + q * B, B)].unsqueeze(2)
                                       .to_broadcast([P, B, P]), ALU.mult).then_inc(built, 1)

            turns(pool, body)

        @block.tensor
        def _(pe):
            def body(o, half, i, n):
                for j in range(G):
                    if j % B == 0:
                        pe.wait_ge(built, n * (G // B) + (j // B + 1))
                    if j % 4 == 0:
                        pe.wait_ge(evac, n * Q + (j // 4 + 1))
                    last = pe.matmul(ps[:, j // 4, (j % 4) * P:(j % 4 + 1) * P], one2[:, j, :], one1[:, j, :],
                                     start=True, stop=True)
                    if j % 4 == 3:
                        last.then_inc(mixed, 1)

            turns(pe, body)

        @block.scalar
        def _(act):
            def body(o, half, i, n):
                for b in range(Q):
                    act.wait_ge(mixed, n * Q + (b + Q + 1))
                    if b == 0:
                        act.wait_ge(wrote[half], 16 * (o + 1))
                    act.activation(gs[half][:].rearrange("p a t -> p t a")[:, bass.ds(i * G + 4 * b, 4), :],
                                   ps[:, b, :].rearrange("p (t a) -> p t a", a=NKEYS), ACT.Copy).then_inc(evac, 1)

            act.sem_inc(evac, Q)
            turns(act, body)

        @block.sync
        def _(sp):
            v = k.dram["peer_v"].rearrange("(g j p) d -> g p j d", p=P, j=EXPERT_TILES)
            for b, (u_slot, v_slot) in enumerate(((u_raw[:, 0], v_raw[:, 0]), (u_raw[:, 1], v_raw[:, 1]))):
                sp.dma_start(u_slot, k.dram["uT"][b]).then_inc(k.u_in[b], 16)
                sp.dma_start(v_slot, v[b]).then_inc(k.v_in[b], 16)
            for half in range(2):
                sp.sem_inc(wrote[half], 16)
            with sp.Fori(0, T // (2 * TB)) as o:
                for half in range(2):
                    sp.wait_ge(evac, o * (2 * Q * NI) + (Q * NI * (half + 1) + Q))
                    sp.dma_start(k.gates[:, bass.ds(o * 2 + half, 1)], gs[half][:].unsqueeze(1))\
                      .then_inc(wrote[half], 16)
            for half in range(2):
                sp.wait_ge(wrote[half], 16 * (T // (2 * TB) + 1))



def split_high(act, high, x):
    return act.activation(high, x, ACT.Copy)


def split_low(eng, low, x, high):
    return eng.tensor_tensor(low, x, high.bitcast(F32), ALU.subtract)


def matmul_split(pe, out, weights, moving, start, stop):
    (wh, wl), (mh, ml) = weights, moving
    pe.matmul(out, wh, mh, start=start, stop=False)
    pe.matmul(out, wh, ml, start=False, stop=False)
    return pe.matmul(out, wl, mh, start=False, stop=stop)


def phase_experts(k):
    nc, ps = k.nc, k.ps
    GE = EXPERT_TILES
    NG = NKEYS // GE
    with ExitStack() as ctx:
        def sb(name, shape, dt=F32):
            return ctx.enter_context(nc.sbuf_tensor(name, shape, dt))

        u_raw, v_raw = raw_experts(k)
        u_high, u_low = [sb(f"u_{x}", [P, 2, KT * GE * P], F32R) for x in ("high", "low")]
        v_high, v_low = [sb(f"v_{x}", [P, 2, GE, D], F32R) for x in ("high", "low")]
        gr = sb("gates_ring", [P, 2, T // TOKEN_BLOCK, GE, TOKEN_BLOCK])
        gel = sb("gelu", [P, 2, T])
        w = sb("weighted", [P, 2, GE, T])
        w_high, w_low = [sb(f"w_{x}", [P, 2, GE, T], F32R) for x in ("high", "low")]
        h_high, h_low = [sb(f"h_{x}", [P, KT, T], F32R) for x in ("high", "low")]
        acc = k.mixT
        rt = sb("e_root", [P, T])
        u_in, v_in = k.u_in, k.v_in
        g_in = [k.sem(f"g_loaded{i}") for i in range(2)]
        u_mm, gelud, weighted = k.sem("u_mm"), k.sem("gelud"), k.sem("weighted_ready")
        v_mm, added, zeroed, resid = k.sem("v_mm"), k.sem("acc_added"), k.sem("acc_zeroed"), k.sem("e_resid")
        h_hi, h_split, u_hi, u_split = k.sem("h_highs"), k.sem("h_split"), k.sem("u_highs"), k.sem("u_split")
        v_hi, v_split, w_hi, w_split = k.sem("v_highs"), k.sem("v_split"), k.sem("w_highs"), k.sem("w_split")
        uT = k.dram["uT"]
        v = k.dram["peer_v"].rearrange("(g j p) d -> g p j d", p=P, j=GE)
        gates = k.gates.rearrange("p n (g j) t -> g p n (j t)", j=GE)
        norm = Norm(k, k.xT, acc, rt[:], 7, KT, col(k, "norm_f"))
        block = ctx.enter_context(nc.Block())

        def one(ap, g):
            return ap[bass.ds(g, 1)] if not isinstance(g, int) else ap[g:g + 1]

        def at_start(i):
            return isinstance(i, int) and i == 0

        @block.sync
        def _(sp):
            def load(g, i, b):
                if not at_start(i):
                    sp.wait_ge(u_split, i * 2 + (b - 1))
                    sp.dma_start(u_raw[:, b], one(uT, g).rearrange("o p n -> (o p) n")).then_inc(u_in[b], 16)
                if not at_start(i):
                    sp.wait_ge(weighted, i * (2 * GE) + GE * (b - 1))
                sp.dma_start(gr[:, b].rearrange("p n j t -> p n (j t)"), one(gates, g).rearrange("o p n x -> (o p) n x"))\
                  .then_inc(g_in[b], 16)
                if not at_start(i):
                    sp.wait_ge(v_split, i * 2 + (b - 1))
                    sp.dma_start(v_raw[:, b], one(v, g).rearrange("o p j d -> (o p) j d")).then_inc(v_in[b], 16)

            for b in range(2):
                load(b, 0, b)
            with sp.Fori(1, NG // 2) as i:
                for b in range(2):
                    load(i * 2 + b, i, b)

        @block.tensor
        def _(pe):
            def up(i, b):
                pe.wait_ge(u_split, i * 2 + (b + 1))
                for j in range(GE):
                    if not at_start(i):
                        pe.wait_ge(gelud, i * (2 * GE) + (GE * (b - 1) + j + 1))
                    for t in range(KT):
                        at = slice(t * GE * P + j * P, t * GE * P + (j + 1) * P)
                        last = matmul_split(pe, ps[:, GE * b + j, :], (u_high[:, b, at], u_low[:, b, at]),
                                            (h_high[:, t, :], h_low[:, t, :]), t == 0, t == KT - 1)
                    last.then_inc(u_mm, 1)

            def down(i, b, first=False):
                pe.wait_ge(v_split, i * 2 + (b + 1))
                pe.wait_ge(w_split, i * 2 + (b + 1))
                for n in range(KT):
                    if not (first and n < 4):
                        pe.wait_ge(added, i * (2 * KT) + (KT * b + n - 3))
                    for j in range(GE):
                        at = slice(n * P, (n + 1) * P)
                        last = matmul_split(pe, ps[:, 4 + n % 4, :], (v_high[:, b, j, at], v_low[:, b, j, at]),
                                            (w_high[:, b, j, :], w_low[:, b, j, :]), j == 0, j == GE - 1)
                    last.then_inc(v_mm, 1)

            pe.wait_ge(h_split, KT)
            up(0, 0)
            up(0, 1)
            down(0, 0, first=True)
            with pe.Fori(1, NG // 2) as i:
                up(i, 0)
                down(i - 1, 1)
                up(i, 1)
                down(i, 0)
            down(NG // 2 - 1, 1)
            norm.pe_sum(pe)

        @block.scalar
        def _(act):
            def high_u(i, b):
                act.wait_ge(u_in[b], i * 16 + 16)
                if not at_start(i):
                    act.wait_ge(u_mm, i * (2 * GE) + GE * (b - 1))
                split_high(act, u_high[:, b], u_raw[:, b]).then_inc(u_hi, 1)

            def high_v(i, b):
                act.wait_ge(v_in[b], i * 16 + 16)
                if not at_start(i):
                    act.wait_ge(v_mm, i * (2 * KT) + KT * (b - 1))
                split_high(act, v_high[:, b], v_raw[:, b]).then_inc(v_hi, 1)

            def gelus(i, b):
                for j in range(GE):
                    act.wait_ge(u_mm, i * (2 * GE) + (GE * b + j + 1))
                    if not (at_start(i) and b == 0):
                        act.wait_ge(weighted, i * (2 * GE) + (GE * (b - 1) + j + 1))
                    act.activation(gel[:, j % 2, :], ps[:, GE * b + j, :], ACT.Gelu).then_inc(gelud, 1)

            def high_w(i, b):
                act.wait_ge(weighted, i * (2 * GE) + GE * (b + 1))
                if not at_start(i):
                    act.wait_ge(v_mm, i * (2 * KT) + KT * (b - 1))
                split_high(act, w_high[:, b], w[:, b]).then_inc(w_hi, 1)

            def step(i, b):
                gelus(i, b)
                high_v(i, b)
                high_w(i, b)

            for t in range(KT):
                split_high(act, h_high[:, t, :], k.mixT[:, t, :]).then_inc(h_hi, 1)
            high_u(0, 0)
            high_u(0, 1)
            high_v(0, 0)
            gelus(0, 0)
            high_w(0, 0)
            high_u(1, 0)
            high_v(0, 1)
            gelus(0, 1)
            high_w(0, 1)
            with act.Fori(1, NG // 2 - 1) as i:
                high_u(i, 1)
                step(i, 0)
                high_u(i + 1, 0)
                step(i, 1)
            high_u(NG // 2 - 1, 1)
            step(NG // 2 - 1, 0)
            step(NG // 2 - 1, 1)
            act.wait_ge(resid, KT)
            norm.act_square(act)
            norm.act_root(act)
            norm.act_affine(act)

        @block.gpsimd
        def _(pool):
            def low_u(i, b):
                pool.wait_ge(u_hi, i * 2 + (b + 1))
                split_low(pool, u_low[:, b], u_raw[:, b], u_high[:, b]).then_inc(u_split, 1)

            def low_v(i, b):
                pool.wait_ge(v_hi, i * 2 + (b + 1))
                split_low(pool, v_low[:, b], v_raw[:, b], v_high[:, b]).then_inc(v_split, 1)

            low_u(0, 0)
            with pool.Fori(0, NG // 2 - 1) as i:
                low_u(i, 1)
                low_v(i, 0)
                low_u(i + 1, 0)
                low_v(i, 1)
            low_u(NG // 2 - 1, 1)
            low_v(NG // 2 - 1, 0)
            low_v(NG // 2 - 1, 1)

        @block.vector
        def _(dve):
            def weigh(i, b):
                dve.wait_ge(g_in[b], i * 16 + 16)
                if not at_start(i):
                    dve.wait_ge(w_hi, i * 2 + (b - 1))
                for j in range(GE):
                    dve.wait_ge(gelud, i * (2 * GE) + (GE * b + j + 1))
                    out, x = [y.rearrange("p (n t) -> p n t", t=TOKEN_BLOCK) for y in (w[:, b, j, :], gel[:, j % 2, :])]
                    dve.tensor_tensor(out, x, gr[:, b, :, j, :], ALU.mult).then_inc(weighted, 1)

            def add(i, b):
                for n in range(KT):
                    dve.wait_ge(v_mm, i * (2 * KT) + (KT * b + n + 1))
                    dve.tensor_tensor(acc[:, n, :], acc[:, n, :], ps[:, 4 + n % 4, :], ALU.add).then_inc(added, 1)

            def low_w(i, b):
                dve.wait_ge(w_hi, i * 2 + (b + 1))
                split_low(dve, w_low[:, b], w[:, b], w_high[:, b]).then_inc(w_split, 1)

            for t in range(KT):
                dve.wait_ge(h_hi, t + 1)
                split_low(dve, h_low[:, t, :], k.mixT[:, t, :], h_high[:, t, :]).then_inc(h_split, 1)
            dve.wait_ge(h_split, KT)
            dve.memset(acc[:], 0.0).then_inc(zeroed, 1)
            dve.wait_ge(zeroed, 1)
            weigh(0, 0)
            low_w(0, 0)
            weigh(0, 1)
            low_w(0, 1)
            add(0, 0)
            with dve.Fori(1, NG // 2) as i:
                weigh(i, 0)
                add(i - 1, 1)
                low_w(i, 0)
                weigh(i, 1)
                add(i, 0)
                low_w(i, 1)
            add(NG // 2 - 1, 1)
            dve.wait_ge(added, NG * KT)
            for n in range(KT):
                dve.scalar_tensor_tensor(k.xT[:, n, :], acc[:, n, :], k.mod[:, 40 + n:41 + n], k.xT[:, n, :],
                                         ALU.mult, ALU.add).then_inc(resid, 1)
            dve.wait_ge(resid, KT)
            norm.dve_scale(dve)
            for n in range(KT):
                norm.wait(dve, n + 1)
                dve.tensor_copy(k.xT[:, n, :], acc[:, n, :])



class Jobs:
    NB = 4

    def __init__(self, k, name):
        self.k, self.list = k, []
        self.filled, self.by_act, self.by_dve = (k.sem(f"{name}_{x}") for x in ("filled", "by_act", "by_dve"))

    def add(self, chunk, mm, out, act=None, dve=None, after_act=False, after_dve=0, before=None):
        self.list.append(Product(chunk=chunk, mm=mm, out=out, act=act, dve=dve, after_act=after_act,
                                         after_dve=after_dve, before=before))
        self.k.used[self.k.at[chunk]] = (self.filled, len(self.list))

    def counts(self, n):
        return sum(x.act is not None for x in self.list[:n]), sum(x.dve is not None for x in self.list[:n])

    def run_pe(self, pe, first=0, last=None):
        now = None
        for j in range(first, len(self.list) if last is None else last):
            job = self.list[j]
            if job.chunk != now:
                now = job.chunk
                chunk_landed(self.k, pe, now)
            if job.before:
                job.before(pe)
            if j >= self.NB:
                a, d = self.counts(j - self.NB + 1)
                if a:
                    pe.wait_ge(self.by_act, a)
                if d:
                    pe.wait_ge(self.by_dve, d)
            out = job.out(self.k.ps[:, j % self.NB, :])
            for i, (lhs, rhs) in enumerate(job.mm):
                ins = pe.matmul(out, lhs, rhs, start=i == 0, stop=i == len(job.mm) - 1)
            ins.then_inc(self.filled, 1)

    def run_act(self, act, first=0, last=None):
        for j in range(first, len(self.list) if last is None else last):
            if self.list[j].act:
                act.wait_ge(self.filled, j + 1)
                if self.list[j].after_dve:
                    act.wait_ge(self.by_dve, self.list[j].after_dve)
                self.list[j].act(act, self.k.ps[:, j % self.NB, :]).then_inc(self.by_act, 1)

    def run_dve(self, dve, first=0, last=None):
        for j in range(first, len(self.list) if last is None else last):
            job = self.list[j]
            if job.dve:
                dve.wait_ge(self.filled, j + 1)
                if job.after_act:
                    dve.wait_ge(self.by_act, self.counts(j + 1)[0])
                job.dve(dve, self.k.ps[:, j % self.NB, :]).then_inc(self.by_dve, 1)


def copy_to(dest, scale=1.0):
    return lambda act, bank: act.activation(dest, bank[0:dest.shape[0], :], ACT.Copy, scale=scale)


NOPE, ROPE, VD = 64, 32, 64
QKD = NOPE + ROPE


def phase_project2(k):
    nc, ps = k.nc, k.ps
    hT = k.mixT
    with ExitStack() as ctx:
        def sb(name, shape, dt=F32):
            return ctx.enter_context(nc.sbuf_tensor(name, shape, dt))

        cq, cqn = sb("cq", [P, 3, T]), sb("cqn", [P, 3, T])
        ckv, ckvn = sb("ckv", [P, 2, T]), sb("ckvn", [P, 2, T])
        rt, rtq, rtkv = sb("f_root", [P, T]), sb("f_root_q", [P, T]), sb("f_root_kv", [P, T])
        sig = sb("f_sig", [P, 2, T])
        rope_x, rope_s = sb("rope_x", [P, 2, T]), sb("rope_s", [P, 2, T])
        k_pe = sb("k_pe", [P, T])
        a3 = sb("f_gain", [P, 8])
        k.rope_cols = sb("rope_cols", [P, 2])
        k.sinT, k.cosT = sb("sinT", [P, T]), sb("cosT", [P, T])
        pos_i, turns = rope_x[:, 0, :].bitcast(I32), rope_s[:, 0, :]
        rope_in, angles, sines = k.sem("rope_loaded"), k.sem("rope_angles"), k.sem("rope_sines")
        fdve = k.sem("f_dve_chain")
        gain, rope_b = k.sem("f_gain_ready"), k.sem("rope_sin")
        norm = Norm(k, k.xT, hT, rt[:], 7, KT, a3, k.ada[:, 0:8])
        norm_q = Norm(k, cq, cqn, rtq[:], 6, 3, col(k, "q_norm_gain_2"))
        norm_kv = Norm(k, ckv, ckvn, rtkv[:], 5, 2, col(k, "kv_norm_gain_2"))
        jobs = Jobs(k, "proj2")
        R = slice(NOPE, QKD)
        whole = lambda bank: bank
        n_rope, n_silu = [0], [0]

        def feature(chunk, a, m, out=whole, src=hT, **kw):
            w = chunk_view(k, chunk)
            jobs.add(chunk, [(w[:, t, a:a + m], src[:, t, :]) for t in range(w.shape[1])],
                     lambda bank: out(bank)[0:m] if out is whole else out(bank), **kw)

        def token(chunk, tile, dest, src=hT, cols=None, **kw):
            w = chunk_view(k, chunk)
            cols = cols or (lambda x: x)
            jobs.add(chunk, [(src[:, t, tile * P:(tile + 1) * P], cols(w[:, t, :])) for t in range(w.shape[1])],
                     whole, act=copy_to(dest), **kw)

        def silu(chunk, a, dest):
            n_silu[0] += 1
            slot = n_silu[0] % 2
            feature(chunk, a, P, after_act=True, after_dve=jobs.counts(len(jobs.list) - 1)[1] if n_silu[0] > 2 else 0,
                    act=lambda act, bank: act.activation(sig[:, slot, :], bank, ACT.Sigmoid),
                    dve=lambda dve, bank: dve.tensor_tensor(dest, bank, sig[:, slot, :], ALU.mult))

        def rope(chunk, a, dest, act=None, swap=None, src=hT, width=ROPE, done=None):
            n_rope[0] += 1
            n, slot = n_rope[0], n_rope[0] % 2

            def first(dve, bank):
                return dve.tensor_tensor(rope_x[R, slot, :], bank[R], k.cosT[R], ALU.mult)

            def second(dve, bank):
                dve.tensor_tensor(rope_s[R, slot, :], bank[R], k.sinT[R], ALU.mult).then_inc(rope_b, 1)
                dve.wait_ge(rope_b, n)
                return dve.tensor_tensor(dest, rope_x[R, slot, :], rope_s[R, slot, :], ALU.add)

            if width == ROPE:
                feature(chunk, a, ROPE, out=lambda bank: bank[R], src=src, dve=first)
            else:
                feature(chunk, a, width, src=src, act=act, dve=first)
            feature(chunk, swap, ROPE, out=lambda bank: bank[R], src=src, dve=second)

        for i in range(3):
            feature("cq", i * P, P, act=copy_to(cq[:, i, :]))
        cq_done = len(jobs.list)
        for i in range(2):
            feature("kvr", i * P, P, act=copy_to(ckv[:, i, :]))
        ckv_done = len(jobs.list)
        rope("kvr", 256, k_pe[R], swap=256 + ROPE)
        kpe_job = len(jobs.list)
        for i in range(4):
            feature("sq", i * P, P, act=copy_to(k.sq[:, i, :], DH ** -0.5))
        for i in range(4):
            feature("sk", i * P, P, act=copy_to(k.sk[:, i, :]))
        for i in range(4):
            token("sv", i, k.sv[:, i, :])
        for i in range(4):
            silu("sz", i * P, k.sz[:, i, :])
        for i in range(4):
            silu("mz", i * P, k.mz[:, i, :])
        late = len(jobs.list)
        for h in range(NH):
            rope("uq", h * QKD, k.mq[R, h, :], act=copy_to(k.mq[0:NOPE, h, :]), swap=NH * QKD + h * ROPE,
                 src=cqn, width=QKD)
        for h in range(NH):
            feature("ukv", h * (NOPE + VD), NOPE, src=ckvn, act=copy_to(k.mk[0:NOPE, h, :]))
        for i in range(4):
            token("ukv", i, k.mv[:, i, :], src=ckvn,
                  cols=lambda w: w.rearrange("p (h x) -> p h x", h=NH)[:, :, NOPE:NOPE + VD])
        block = ctx.enter_context(nc.Block())

        def rope_angles(dve, link):
            R = slice(NOPE, QKD)
            a, b, c = turns[R], k.sinT[R], k.cosT[R]
            dve.wait_ge(rope_in, 32)
            link(dve.tensor_copy(b, pos_i[R]))
            link(dve.tensor_scalar(b, b, k.rope_cols[R, 0:1], None, ALU.mult))
            link(dve.tensor_scalar(a, b, 1.0 / (2 * np.pi), None, ALU.mult))
            link(dve.tensor_scalar(a, a, 12582912.0, 12582912.0, ALU.add, ALU.subtract))
            for part in TWO_PI:
                link(dve.scalar_tensor_tensor(b, a, -part, b, ALU.mult, ALU.add))
            link(dve.tensor_scalar(c, b, np.pi / 2, None, ALU.add))
            link(dve.tensor_scalar(a, c, PI_DOWN, -2 * np.pi, ALU.is_gt, ALU.mult))
            link(dve.tensor_tensor(c, c, a, ALU.add))
            dve.tensor_scalar(b, b, PI_DOWN, -PI_DOWN, ALU.min, ALU.max).then_inc(angles, 1)
            dve.tensor_scalar(c, c, PI_DOWN, -PI_DOWN, ALU.min, ALU.max).then_inc(angles, 1)
            dve.wait_ge(sines, 2)
            link(dve.tensor_scalar(b, b, k.rope_cols[R, 1:2], None, ALU.mult))

        @block.sync
        def _(sp):
            R = slice(NOPE, QKD)
            sp.dma_start(pos_i[R], k.dram["positions"].to_broadcast([ROPE, T])).then_inc(rope_in, 16)
            sp.dma_start(k.rope_cols[R], k.dram["rope_cols"]).then_inc(rope_in, 16)
            load_chunks(k, sp, k.at["ukv"] + SLOTS)

        @block.gpsimd
        def _(pool):
            pool.wait_ge(jobs.by_dve, jobs.counts(kpe_job)[1])
            pool.tensor_copy(k.mk[R], k_pe[R].unsqueeze(1).to_broadcast([ROPE, NH, T]))

        @block.vector
        def _(dve):
            dve.scalar_tensor_tensor(a3[:], k.ada[:, 8:16], 1.0, col(k, "norm_gain_2"), ALU.add, ALU.mult)\
               .then_inc(gain, 1)
            rope_angles(dve, chain(dve, fdve))
            norm.dve_scale(dve)
            jobs.run_dve(dve, 0, kpe_job)
            norm_q.dve_scale(dve)
            norm_kv.dve_scale(dve)
            jobs.run_dve(dve, kpe_job)

        @block.scalar
        def _(act):
            norm.act_square(act)
            R = slice(NOPE, QKD)
            act.wait_ge(angles, 2)
            act.activation(k.sinT[R], k.sinT[R], ACT.Sin).then_inc(sines, 1)
            act.activation(k.cosT[R], k.cosT[R], ACT.Sin).then_inc(sines, 1)
            norm.act_root(act)
            act.wait_ge(gain, 1)
            norm.act_affine(act)
            jobs.run_act(act, 0, ckv_done)
            act.wait_ge(jobs.by_act, ckv_done)
            norm_q.act_square(act)
            norm_kv.act_square(act)
            norm_q.act_root(act)
            norm_kv.act_root(act)
            norm_q.act_affine(act)
            norm_kv.act_affine(act)
            jobs.run_act(act, ckv_done)

        @block.tensor
        def _(pe):
            norm.pe_sum(pe)
            norm.wait(pe)
            jobs.run_pe(pe, 0, kpe_job)
            norm_q.pe_sum(pe)
            norm_kv.pe_sum(pe)
            jobs.run_pe(pe, kpe_job, late)
            norm_q.wait(pe)
            norm_kv.wait(pe)
            jobs.run_pe(pe, late)


def phase_attend2(k):
    nc, ps = k.nc, k.ps
    TT = T // P
    items = [(kind, h, i) for kind in ("stick", "soft") for h in range(NH) for i in range(TT)]
    N = len(items)
    NHD = 2 * NH
    with ExitStack() as ctx:
        def sb(name, shape, dt=F32):
            return ctx.enter_context(nc.sbuf_tensor(name, shape, dt))

        w = sb("at_w", [P, 3, T])
        rest = sb("at_rest", [P, 3, T])
        prod = sb("at_prod", [P, 3, T])
        pT = sb("at_wT", [P, 2, TT, T])
        nmax, sums = sb("at_nmax", [P, N]), sb("at_sums", [P, N, 2])
        cmask = sb("causal_mask", [P, 2, P])
        made = k.sem("causal_masks")
        scored, masked, acted = k.sem("at_scored"), k.sem("at_masked"), k.sem("at_acted")
        cdve, ready = k.sem("at_dve_chain"), k.sem("at_ready")
        turned, turned_sb, summed, stored = (k.sem("at_turned"), k.sem("at_turned_sb"), k.sem("at_summed"),
                                             k.sem("at_stored"))
        block = ctx.enter_context(nc.Block())

        def width(n):
            return (items[n][2] + 1) * P

        @block.gpsimd
        def _(pool):
            for j, base in enumerate((0, 1)):
                pool.affine_select(out=cmask[:, j, :], in_=k.zeros[:, 0:P], compare_op=ALU.is_gt, fill=NEG,
                                   base=base, pattern=[[-1, P]], channel_multiplier=1).then_inc(made, 1)

        @block.tensor
        def _(pe):
            def scores(n):
                kind, h, i = items[n]
                if n >= 4:
                    pe.wait_ge(acted, n - 3)
                if kind == "stick":
                    a, hp = DH * (h % 2), h // 2
                    q, key = k.sq[a:a + DH, hp], k.sk[a:a + DH, hp]
                else:
                    q, key = k.mq[0:QKD, h], k.mk[0:QKD, h]
                pe.matmul(ps[:, n % 4, 0:width(n)], q[:, i * P:(i + 1) * P], key[:, 0:width(n)], start=True,
                          stop=True).then_inc(scored, 1)

            def turn(n):
                kind, h, i = items[n]
                pe.wait_ge(ready, n + 1)
                if n >= 2:
                    pe.wait_ge(turned_sb, n - 1)
                for j in range(i + 1):
                    last = pe.transpose(ps[:, 4 + n % 2, j * P:(j + 1) * P], w[:, n % 3, j * P:(j + 1) * P], k.ident[:])
                last.then_inc(turned, 1)

            def values(m):
                h, v = m % NH, (k.sv if m < NH else k.mv)
                pe.wait_ge(turned_sb, TT * (m + 1))
                if m % 2 == 0 and m >= 4:
                    pe.wait_ge(stored, m // 2 - 1)
                a = DH * (h % 2)
                for j in range(TT):
                    last = pe.matmul(ps[a:a + DH, 6 + m // 2 % 2, j * P:T], v[:, j, h * DH:(h + 1) * DH],
                                     pT[:, m % 2, j, j * P:T], start=j == 0, stop=j == TT - 1)
                last.then_inc(summed, 1)

            for n in range(N + 4):
                if n < N:
                    scores(n)
                if 0 <= n - 2 < N:
                    turn(n - 2)
                if n - 3 >= 0 and (n - 3) % TT == TT - 1:
                    values((n - 3) // TT)

        def store(dve, pair):
            dve.wait_ge(summed, 2 * pair + 2)
            z = (k.sz if pair < NH // 2 else k.mz)[:, pair % (NH // 2), :]
            dve.tensor_tensor(z, z, ps[:, 6 + pair % 2, :], ALU.mult).then_inc(stored, 1)

        @block.vector
        def _(dve):
            link = chain(dve, cdve)
            dve.wait_ge(made, 2)
            for n in range(N + 1):
                if n < N:
                    kind, h, i = items[n]
                    W = width(n)
                    dve.wait_ge(scored, n + 1)
                    diag = ps[:, n % 4, W - P:W]
                    if kind == "stick":
                        dve.tensor_tensor(diag, diag, cmask[:, 0, :], ALU.add).then_inc(masked, 1)
                    else:
                        link(dve.tensor_tensor(diag, diag, cmask[:, 1, :], ALU.add))
                        link(dve.tensor_reduce(nmax[:, n:n + 1], ps[:, n % 4, 0:W], AX.X, ALU.max, negate=True))
                        dve.tensor_scalar(nmax[:, n:n + 1], nmax[:, n:n + 1], QKD ** -0.5, None, ALU.mult)\
                           .then_inc(masked, 1)
                if n >= 1:
                    m = n - 1
                    kind, h, i = items[m]
                    W, s = width(m), m % 3
                    if kind == "stick":
                        link(dve.memset(prod[:, s, W - 1:W], 1.0))
                        dve.wait_ge(acted, m + 1)
                        link(dve.tensor_tensor_scan(out=prod[:, s, W - 2::-1], data0=rest[:, s, W - 1:0:-1],
                                                    data1=k.zeros[:, 0:W - 1], initial=1.0, op0=ALU.mult,
                                                    op1=ALU.add))
                        dve.tensor_tensor(w[:, s, 0:W], w[:, s, 0:W], prod[:, s, 0:W], ALU.mult).then_inc(ready, 1)
                    else:
                        dve.wait_ge(acted, m + 1)
                        link(dve.reciprocal(sums[:, m, 1:2], sums[:, m, 0:1]))
                        dve.tensor_scalar(w[:, s, 0:W], w[:, s, 0:W], sums[:, m, 1:2], None, ALU.mult)\
                           .then_inc(ready, 1)
                if n >= 2 * TT + 3 and (n - 3) % (2 * TT) == 0:
                    store(dve, (n - 3) // (2 * TT) - 1)
            store(dve, NH - 1)

        @block.scalar
        def _(act):
            for n in range(N + 2):
                if n < N:
                    kind, h, i = items[n]
                    W, s = width(n), n % 3
                    act.wait_ge(masked, n + 1)
                    if n >= 3:
                        act.wait_ge(turned, n - 2)
                    if kind == "stick":
                        act.activation(w[:, s, 0:W], ps[:, n % 4, 0:W], ACT.Sigmoid)
                        act.activation(rest[:, s, 0:W], ps[:, n % 4, 0:W], ACT.Sigmoid, scale=-1.0).then_inc(acted, 1)
                    else:
                        act.activation(w[:, s, 0:W], ps[:, n % 4, 0:W], ACT.Exp, scale=QKD ** -0.5,
                                       bias=nmax[:, n:n + 1], accum_out=sums[:, n, 0:1]).then_inc(acted, 1)
                if 0 <= n - 2 < N:
                    m = n - 2
                    kind, h, i = items[m]
                    head = m // TT
                    act.wait_ge(turned, m + 1)
                    if head >= 2:
                        act.wait_ge(summed, head - 1)
                    act.activation(pT[:, head % 2, 0:i + 1, i * P:(i + 1) * P],
                                   ps[:, 4 + m % 2, 0:(i + 1) * P].rearrange("p (j t) -> p j t", t=P),
                                   ACT.Copy).then_inc(turned_sb, 1)


def phase_merge2(k):
    nc, ps = k.nc, k.ps
    hT = k.mixT
    with ExitStack() as ctx:
        def sb(name, shape, dt=F32):
            return ctx.enter_context(nc.sbuf_tensor(name, shape, dt))

        sg, merged = sb("gates2", [P, KT, T]), sb("merged", [P, KT, T])
        rt = sb("h_root", [P, T])
        weighed, stored = k.sem("b_weighed"), k.sem("out_stored")
        norm = Norm(k, k.xT, k.mixT, rt[:], 7, KT, col(k, "final_norm_gain_2"))
        jobs = Jobs(k, "merge")

        def feature(chunk, a, src, **kw):
            w = chunk_view(k, chunk)
            jobs.add(chunk, [(w[:, t, a:a + P], src[:, t, :]) for t in range(w.shape[1])], lambda bank: bank, **kw)

        def gate_of(n, branch):
            c, a = divmod(n, 4)
            before_act = (lambda act: act.wait_ge(jobs.by_dve, n + 1)) if branch else None

            def run(act, bank):
                if before_act:
                    before_act(act)
                return act.activation(sg[:, n, :], bank, ACT.Sigmoid)

            feature(f"g{'ab'[branch]}{c}", a * P, hT, act=run)

        def first(n):
            feature("bra", n * P, k.sz, after_act=True,
                    dve=lambda dve, bank: dve.tensor_tensor(merged[:, n, :], bank, sg[:, n, :], ALU.mult))

        def second(n):
            def run(dve, bank):
                dve.tensor_tensor(sg[:, n, :], bank, sg[:, n, :], ALU.mult).then_inc(weighed, 1)
                dve.wait_ge(weighed, n + 1)
                return dve.tensor_tensor(merged[:, n, :], merged[:, n, :], sg[:, n, :], ALU.add)

            feature("brb", n * P, k.mz, after_act=True, dve=run)

        for branch, rest in enumerate((first, second)):
            for n in range(KT):
                gate_of(n, branch)
            for n in range(KT):
                rest(n)
        n_merge = len(jobs.list)
        for n in range(KT):
            feature(f"wo{n // 4}", n % 4 * P, merged,
                    before=(lambda pe: pe.wait_ge(jobs.by_dve, 2 * KT)) if n == 0 else None,
                    dve=lambda dve, bank, n=n: dve.scalar_tensor_tensor(
                        k.xT[:, n, :], bank, k.ada[:, 16 + n:17 + n], k.xT[:, n, :], ALU.mult, ALU.add))
        block = ctx.enter_context(nc.Block())

        @block.sync
        def _(sp):
            load_chunks(k, sp, k.at["wo1"])
            o = k.out.rearrange("(k p) t -> p k t", p=P)
            for n in range(0, KT, 2):
                norm.wait(sp, n + 2)
                sp.dma_start(o[:, n:n + 2, :], k.mixT[:, n:n + 2, :]).then_inc(stored, 16)
            sp.wait_ge(stored, 16 * (KT // 2))

        @block.vector
        def _(dve):
            jobs.run_dve(dve)
            dve.wait_ge(jobs.by_dve, 3 * KT)
            norm.dve_scale(dve)

        @block.scalar
        def _(act):
            jobs.run_act(act)
            act.wait_ge(jobs.by_dve, 3 * KT)
            norm.act_square(act)
            norm.act_root(act)
            norm.act_affine(act)

        @block.tensor
        def _(pe):
            jobs.run_pe(pe)
            norm.pe_sum(pe)


def second_block(k, sb):
    with ExitStack() as outs:
        k.sz, k.mz = sb("sz", [P, 4, T], where=outs), sb("mz", [P, 4, T], where=outs)
        with ExitStack() as qkv:
            k.sq, k.sk, k.sv = (sb(n, [P, 4, T], where=qkv) for n in ("sq", "sk", "sv"))
            k.mq, k.mk = (sb(n, [P, NH, T], where=qkv) for n in ("mq", "mk"))
            k.mv = sb("mv", [P, 4, T], where=qkv)
            phase_project2(k)
            phase_attend2(k)
        phase_merge2(k)


def build(nc, dram, out):
    with ExitStack() as ctx:
        k = Kernel(nc=nc, dram=dram, out=out)

        def sem(name, n=None):
            if n is None:
                return ctx.enter_context(nc.semaphore(name))
            return [ctx.enter_context(nc.semaphore(f"{name}{i}")) for i in range(n)]

        def sb(name, shape, dt=F32, where=ctx):
            return where.enter_context(nc.sbuf_tensor(name, shape, dt))

        k.sem = sem
        k.norm_sems = [sem(f"norm_{x}") for x in ("squared", "summed", "mean", "rooted", "inverse", "scaled", "done")]
        k.norms, k.norm_tiles = 0, 0
        k.ps = ctx.enter_context(nc.psum_tensor("ps", [P, 8, 512], F32))
        k.xT = sb("xT", [P, KT, T])
        k.mixT = sb("mixT", [P, KT, T])
        k.ring = sb("ring", [P, SLOTS, KT * CHUNK])
        k.cols = sb("cols", [P, NCOL])
        k.ones = sb("ones", [P, P])
        k.zeros = sb("zeros", [P, T])

        k.ident = sb("ident", [P, P])
        k.mod = sb("mod", [P, 48])
        k.sc = sb("silu_c", [P, KT, 2])
        k.ada = sb("ada", [P, 24])
        k.ring_full = sem("ring_full", SLOTS)
        plan_stream(k)
        with ExitStack() as hg:
            k.hq = sb("hq", [P, HG, T], where=hg)
            k.fx = [sb(f"fx{d}", [P, HG, T], where=hg) for d in range(2)]
            k.fc = [sb(f"fc{d}", [P, HG, C], where=hg) for d in range(2)]
            k.hgate = sb("hgate", [P, HG, T], where=hg)
            k.ix = sb("ix", [P, 4, 512], where=hg)
            k.ic = sb("ic", [P, 2, 512], where=hg)
            with ExitStack() as na:
                k.qT = sb("qT", [P, 4, T], where=na)
                k.kT = sb("kT", [P, 4, T + C], where=na)
                k.vw = sb("vw", [P, 8, 512], where=na)
                k.vc = sb("vc", [P, 2, 512], where=na)
                phase_project(k)
                phase_neighbourhood(k)
            phase_hgrn(k)
        k.gates = nc.dram_tensor("gates", [NKEYS, T // TOKEN_BLOCK, NKEYS, TOKEN_BLOCK], F32, kind="Internal").ap()
        with ExitStack() as peer:
            k.selT = sb("selT", [P, 3, T], where=peer)
            k.io_int = sb("io_int", [P, P], I32, where=peer)
            k.iota = sb("iota", [P, P], where=peer)
            phase_route(k)
            phase_spread(k)
        phase_experts(k)
        second_block(k, sb)


def lay_out(inputs):
    f = {n: np.asarray(a) for n, a in inputs.items()}

    def columns(v):
        return np.ascontiguousarray(v.reshape(-1, P).T)

    a = {"xT": f["x"][0].T, "ctxT": f["ctx"][0].T}
    a["cols"] = np.concatenate([columns(f[name]) for name, _ in _COLS], axis=1)
    for name in ("w_mod", "w_in", "w_out", "peer_wq"):
        a[name] = f[name][0]
    padded = np.pad(f["na_rpb"][0].transpose(1, 0, 2), ((0, 0), (0, 0), (QB, QB)))
    a["rpb_shifted"] = np.stack([padded[:, :, QB - 1 - q:QB - 1 - q + KB + QB] for q in range(QB)])
    q, key = np.arange(P)[:, None] % QB, np.arange(KB)[None, :]
    a["win_mask"] = np.stack([np.where((key >= first) & (key < first + KB // 2), 0.0, NEG).astype(np.float32)
                              for first in (np.maximum(q - 8, 0), q, np.minimum(q + 8, 16))], axis=1)
    t, s = np.arange(P)[None, :], np.arange(P)[:, None]
    pred = np.stack([(t >> lv) == (s >> lv) + 1 for lv in range(7)]) \
        & np.stack([(t >> lv + 1) == (s >> lv + 1) for lv in range(7)])
    a["pred"] = np.stack([pred, pred.transpose(0, 2, 1)]).transpose(2, 0, 1, 3).astype(np.float32)
    a["keysT"] = f["peer_keys"][0].transpose(3, 0, 1, 2).reshape(P, 2 * PH, NKEYS)
    group = EXPERT_TILES * P
    a["uT"] = f["peer_u"][0].reshape(-1, group, KT, P).transpose(0, 3, 2, 1).reshape(-1, P, KT * group)
    a["peer_v"] = f["peer_v"][0]
    for name in ("w_ada_2", "w_in_2", "w_ukv_2", "w_branch_a_2", "w_branch_b_2", "w_out_2"):
        a[name] = f[name][0]
    def swapped(w):
        h = w.reshape(w.shape[0], -1, 2, ROPE // 2)
        return h[:, :, ::-1].reshape(w.shape)

    kv = f["w_in_2"][0][:, 2432:2720]
    a["w_kvr_2"] = np.concatenate([kv, swapped(kv[:, 256:])], axis=1)
    uq = f["w_uq_2"][0]
    rot = uq.reshape(-1, NH, QKD)[:, :, NOPE:].reshape(uq.shape[0], NH * ROPE)
    a["w_uq_2"] = np.concatenate([uq, swapped(rot)], axis=1)
    a["positions"] = f["positions_2"]
    i = np.arange(ROPE)
    a["rope_cols"] = np.stack([10000.0 ** (-(2 * (i % (ROPE // 2))) / ROPE), np.where(i < ROPE // 2, -1.0, 1.0)],
                              axis=1).astype(np.float32)
    return {n: np.ascontiguousarray(v) for n, v in a.items()}


def kernel(**inputs):
    import concourse.bacc as bacc
    from concourse.bass_utils import run_bass_kernel_spmd

    nc = bacc.Bacc("TRN2", target_bir_lowering=False, num_devices=1)
    arrays = {f"in_{name}": a for name, a in lay_out(inputs).items()}
    dram = {name[3:]: nc.dram_tensor(name, a.shape, mybir.dt.from_np(a.dtype), kind="ExternalInput").ap()
            for name, a in arrays.items()}
    out = nc.dram_tensor("out_T", (D, T), F32, kind="ExternalOutput").ap()
    build(nc, dram, out)
    result = run_bass_kernel_spmd(nc, [arrays], core_ids=[0])
    return np.ascontiguousarray(result.results[0]["out_T"].T).reshape(1, T, D)
```
